# Optimizing a Trainium2 kernel written in Bass

```python
import math
import numpy as np
import jax
import jax.numpy as jnp
from jax import lax

D_MODEL = 1024
BATCH = 1
SEQ = 4096
DEPTH = 1
DEC_BATCH = 8
DEC_SEQ = 1
PAST_LEN = 1024
PAGE_SIZE = 128

HEAD_DIM = 64
N_FOX_HEADS = 6
W_FOX = N_FOX_HEADS * HEAD_DIM
SSM_GROUP = 16
N_SSM_GROUPS = 24
W_SSM = N_SSM_GROUPS * SSM_GROUP
SSM_STATE = 64
N_MEM_HEADS = 4
W_MEM = N_MEM_HEADS * HEAD_DIM
N_MEM = 256
W_MIX = W_FOX + W_SSM + W_MEM
IN_SIZES = (W_FOX, W_FOX, W_FOX, N_FOX_HEADS, W_FOX, W_SSM, W_SSM, W_MEM, W_MEM)
D_IN = sum(IN_SIZES)
Q_BLOCK = 128
RMS_EPS = 1e-6
POOL_NUM = 5
POOL_DEN = 4
DT_MIN = 1e-3
DT_MAX = 1e-1
FORGET_BIAS_INIT = 2.0

kernel_name = 'hymba_fox_s5_memory_decoder_step'

def rmsnorm(x, g):
    x32 = x.astype(jnp.float32)
    y = x32 * lax.rsqrt(jnp.mean(x32 * x32, axis=-1, keepdims=True) + RMS_EPS)
    return (y * g.astype(jnp.float32)).astype(x.dtype)

def split_heads(t, n_heads):
    return t.reshape(t.shape[:-1] + (n_heads, HEAD_DIM))

def in_projection(x, g_norm, w_in, b_f):
    xn = rmsnorm(x, g_norm)
    z = jnp.einsum('bld,de->ble', xn, w_in)
    cuts = np.cumsum(IN_SIZES)[:-1].tolist()
    q, k, v, f, gate_a, u, gate_s, q_m, gate_m = jnp.split(z, cuts, axis=-1)
    log_f = jax.nn.log_sigmoid((f + b_f).astype(jnp.float32))
    u = u.reshape(u.shape[:2] + (N_SSM_GROUPS, SSM_GROUP))
    return (split_heads(q, N_FOX_HEADS), split_heads(k, N_FOX_HEADS), split_heads(v, N_FOX_HEADS),
            log_f, gate_a, u, gate_s, split_heads(q_m, N_MEM_HEADS), gate_m)

def fox_attend(q, c_q, q_pos, k, v, c_k):
    s = jnp.einsum('bqhd,bkhd->bhqk', q, k).astype(jnp.float32) * (HEAD_DIM ** -0.5)
    s = s + jnp.swapaxes(c_q, 1, 2)[..., :, None] - jnp.swapaxes(c_k, 1, 2)[..., None, :]
    causal = jnp.arange(k.shape[1])[None, :] <= q_pos[:, None]
    s = jnp.where(causal, s, -jnp.inf)
    p = jax.nn.softmax(s, axis=-1)
    return jnp.einsum('bhqk,bkhd->bqhd', p.astype(v.dtype), v)

def fox_prompt(q, k, v, log_f):
    b, l, h, dh = q.shape
    n_blocks = l // Q_BLOCK
    c = jnp.cumsum(log_f, axis=1)
    q_blocks = jnp.moveaxis(q.reshape(b, n_blocks, Q_BLOCK, h, dh), 1, 0)
    c_blocks = jnp.moveaxis(c.reshape(b, n_blocks, Q_BLOCK, h), 1, 0)

    def one_block(args):
        i, q_i, c_i = args
        q_pos = i * Q_BLOCK + jnp.arange(Q_BLOCK)
        return fox_attend(q_i, c_i, q_pos, k, v, c)

    out = lax.map(one_block, (jnp.arange(n_blocks), q_blocks, c_blocks))
    return jnp.moveaxis(out, 0, 1).reshape(b, l, h, dh)

def fox_sample(q, k_new, v_new, log_f_new, k_past, v_past, log_f_past):
    past = k_past.shape[1]
    k = jnp.concatenate([k_past, k_new.astype(k_past.dtype)], axis=1)
    v = jnp.concatenate([v_past, v_new.astype(v_past.dtype)], axis=1)
    c = jnp.cumsum(jnp.concatenate([log_f_past.astype(jnp.float32), log_f_new], axis=1), axis=1)
    q_pos = past + jnp.arange(q.shape[1])
    return fox_attend(q, c[:, past:], q_pos, k, v, c)

def s5_scan(u, h0, lam_re, lam_im, log_dt, b_re, b_im, c_re, c_im, d_skip):
    f32 = jnp.float32
    lam = lax.complex(lam_re.astype(f32), lam_im.astype(f32))
    dt = jnp.exp(log_dt.astype(f32))[:, None]
    lam_bar = jnp.exp(lam * dt)
    b_bar = ((lam_bar - 1.0) / lam)[..., None] * lax.complex(b_re.astype(f32), b_im.astype(f32))
    c_mat = lax.complex(c_re.astype(f32), c_im.astype(f32))
    u32 = u.astype(f32)
    bu = jnp.einsum('gpc,blgc->blgp', b_bar, u32.astype(jnp.complex64))
    bu = bu.at[:, 0].add(lam_bar * h0)
    a = jnp.broadcast_to(lam_bar, bu.shape)

    def combine(e1, e2):
        a1, b1 = e1
        a2, b2 = e2
        return a1 * a2, a2 * b1 + b2

    _, h = lax.associative_scan(combine, (a, bu), axis=1)
    y = jnp.einsum('gcp,blgp->blgc', c_mat, h).real + d_skip.astype(f32) * u32
    return y, h[:, -1]

def memory_kv(mem, g_mem, w_mem_kv):
    m = rmsnorm(mem, g_mem)
    kv = jnp.einsum('bnd,de->bne', m, w_mem_kv)
    k, v = jnp.split(kv, 2, axis=-1)
    return split_heads(k, N_MEM_HEADS), split_heads(v, N_MEM_HEADS)

def memory_attend(q, k, v):
    s = jnp.einsum('bqhd,bnhd->bhqn', q, k.astype(q.dtype)).astype(jnp.float32) * (HEAD_DIM ** -0.5)
    p = jax.nn.softmax(s, axis=-1)
    return jnp.einsum('bhqn,bnhd->bqhd', p.astype(q.dtype), v.astype(q.dtype))

def out_projection(x, fox_out, gate_a, ssm_y, gate_s, w_glu, b_glu, mem_out, gate_m, w_out):
    b, l = x.shape[:2]
    dt = x.dtype
    a = fox_out.reshape(b, l, W_FOX).astype(dt) * jax.nn.silu(gate_a)
    s = jax.nn.gelu(ssm_y.reshape(b, l, W_SSM), approximate=False)
    s = s * jax.nn.sigmoid(jnp.einsum('blc,ce->ble', s, w_glu.astype(jnp.float32)) + b_glu.astype(jnp.float32))
    s = s.astype(dt) * jax.nn.silu(gate_s)
    m = mem_out.reshape(b, l, W_MEM).astype(dt) * jax.nn.silu(gate_m)
    mix = jnp.concatenate([a, s, m], axis=-1)
    return x + jnp.einsum('ble,ed->bld', mix, w_out)

def setup_inputs(seed: int = 0) -> dict:
    key = jax.random.key(seed)
    ks = jax.random.split(key, 28)
    f32 = jnp.float32
    n_pages = PAST_LEN // PAGE_SIZE
    n_pool = (DEC_BATCH * n_pages * POOL_NUM) // POOL_DEN

    def nrm(k, shape, scale=1.0):
        return jax.random.normal(k, shape, f32) * scale

    G, P = N_SSM_GROUPS, SSM_STATE
    x_prompt = nrm(ks[0], (BATCH, SEQ, D_MODEL))
    x_sample = nrm(ks[1], (DEC_BATCH, DEC_SEQ, D_MODEL))
    mem_prompt = nrm(ks[2], (BATCH, N_MEM, D_MODEL))
    cache_k = nrm(ks[3], (DEPTH, n_pool, PAGE_SIZE, N_FOX_HEADS, HEAD_DIM))
    cache_v = nrm(ks[4], (DEPTH, n_pool, PAGE_SIZE, N_FOX_HEADS, HEAD_DIM))
    cache_logf = jax.nn.log_sigmoid(nrm(ks[5], (DEPTH, n_pool, PAGE_SIZE, N_FOX_HEADS)) + FORGET_BIAS_INIT)
    state_ssm = nrm(ks[6], (DEPTH, DEC_BATCH, G, P, 2), 0.2)
    cache_mem_k = nrm(ks[7], (DEPTH, DEC_BATCH, N_MEM, N_MEM_HEADS, HEAD_DIM))
    cache_mem_v = nrm(ks[8], (DEPTH, DEC_BATCH, N_MEM, N_MEM_HEADS, HEAD_DIM))
    page_table = jax.random.permutation(ks[9], n_pool)[: DEC_BATCH * n_pages].reshape(
        DEC_BATCH, n_pages).astype(jnp.int32)
    g_norm = 1.0 + nrm(ks[10], (DEPTH, D_MODEL), 0.02)
    w_in = nrm(ks[11], (DEPTH, D_MODEL, D_IN), D_MODEL ** -0.5)
    b_f = FORGET_BIAS_INIT + nrm(ks[12], (DEPTH, N_FOX_HEADS), 0.5)
    lam_re = -0.5 + nrm(ks[13], (DEPTH, G, P), 0.01)
    lam_im = math.pi * jnp.arange(P, dtype=f32) + nrm(ks[14], (DEPTH, G, P), 0.01)
    log_dt = jax.random.uniform(ks[15], (DEPTH, G), f32, math.log(DT_MIN), math.log(DT_MAX))
    b_re = nrm(ks[16], (DEPTH, G, P, SSM_GROUP), (2 * SSM_GROUP) ** -0.5)
    b_im = nrm(ks[17], (DEPTH, G, P, SSM_GROUP), (2 * SSM_GROUP) ** -0.5)
    c_re = nrm(ks[18], (DEPTH, G, SSM_GROUP, P), SSM_STATE ** -0.5)
    c_im = nrm(ks[19], (DEPTH, G, SSM_GROUP, P), SSM_STATE ** -0.5)
    d_skip = nrm(ks[20], (DEPTH, G, SSM_GROUP))
    w_glu = nrm(ks[21], (DEPTH, W_SSM, W_SSM), W_SSM ** -0.5)
    b_glu = nrm(ks[22], (DEPTH, W_SSM), 0.02)
    g_mem = 1.0 + nrm(ks[23], (DEPTH, D_MODEL), 0.02)
    w_mem_kv = nrm(ks[24], (DEPTH, D_MODEL, 2 * W_MEM), D_MODEL ** -0.5)
    w_out = nrm(ks[25], (DEPTH, W_MIX, D_MODEL), W_MIX ** -0.5)
    g_final = 1.0 + nrm(ks[26], (D_MODEL,), 0.02)
    return {'x_prompt': x_prompt, 'x_sample': x_sample, 'mem_prompt': mem_prompt,
            'cache_k': cache_k, 'cache_v': cache_v, 'cache_logf': cache_logf, 'state_ssm': state_ssm,
            'cache_mem_k': cache_mem_k, 'cache_mem_v': cache_mem_v, 'page_table': page_table,
            'g_norm': g_norm, 'w_in': w_in, 'b_f': b_f, 'lam_re': lam_re, 'lam_im': lam_im,
            'log_dt': log_dt, 'b_re': b_re, 'b_im': b_im, 'c_re': c_re, 'c_im': c_im,
            'd_skip': d_skip, 'w_glu': w_glu, 'b_glu': b_glu, 'g_mem': g_mem,
            'w_mem_kv': w_mem_kv, 'w_out': w_out, 'g_final': g_final}

def reference(x_prompt, x_sample, mem_prompt, cache_k, cache_v, cache_logf, state_ssm,
              cache_mem_k, cache_mem_v, page_table, g_norm, w_in, b_f, lam_re, lam_im,
              log_dt, b_re, b_im, c_re, c_im, d_skip, w_glu, b_glu, g_mem, w_mem_kv,
              w_out, g_final):
    f32 = jnp.float32
    dec_b = x_sample.shape[0]
    past_len = page_table.shape[1] * cache_k.shape[2]
    xp, xs = x_prompt, x_sample
    kp, vp, lfp, hp, mkp, mvp = [], [], [], [], [], []
    ks_, vs_, lfs, hs = [], [], [], []
    for l in range(DEPTH):
        ssm_params = (lam_re[l], lam_im[l], log_dt[l], b_re[l], b_im[l], c_re[l], c_im[l], d_skip[l])

        q, k, v, log_f, ga, u, gs, qm, gm = in_projection(xp, g_norm[l], w_in[l], b_f[l])
        fox_o = fox_prompt(q, k, v, log_f)
        h0 = jnp.zeros((xp.shape[0], N_SSM_GROUPS, SSM_STATE), jnp.complex64)
        ssm_y, h_last = s5_scan(u, h0, *ssm_params)
        mk, mv = memory_kv(mem_prompt, g_mem[l], w_mem_kv[l])
        mem_o = memory_attend(qm, mk, mv)
        xp = out_projection(xp, fox_o, ga, ssm_y, gs, w_glu[l], b_glu[l], mem_o, gm, w_out[l])
        kp.append(k)
        vp.append(v)
        lfp.append(log_f)
        hp.append(jnp.stack([h_last.real, h_last.imag], axis=-1).astype(f32))
        mkp.append(mk)
        mvp.append(mv)

        q, k, v, log_f, ga, u, gs, qm, gm = in_projection(xs, g_norm[l], w_in[l], b_f[l])
        k_past = cache_k[l, page_table].reshape(dec_b, past_len, N_FOX_HEADS, HEAD_DIM)
        v_past = cache_v[l, page_table].reshape(dec_b, past_len, N_FOX_HEADS, HEAD_DIM)
        lf_past = cache_logf[l, page_table].reshape(dec_b, past_len, N_FOX_HEADS)
        fox_o = fox_sample(q, k, v, log_f, k_past, v_past, lf_past)
        h0 = lax.complex(state_ssm[l, ..., 0].astype(f32), state_ssm[l, ..., 1].astype(f32))
        ssm_y, h_last = s5_scan(u, h0, *ssm_params)
        mem_o = memory_attend(qm, cache_mem_k[l], cache_mem_v[l])
        xs = out_projection(xs, fox_o, ga, ssm_y, gs, w_glu[l], b_glu[l], mem_o, gm, w_out[l])
        ks_.append(k)
        vs_.append(v)
        lfs.append(log_f)
        hs.append(jnp.stack([h_last.real, h_last.imag], axis=-1).astype(f32))

    y_prompt = rmsnorm(xp, g_final)
    y_sample = rmsnorm(xs, g_final)
    return (y_prompt, y_sample,
            jnp.stack(kp), jnp.stack(vp), jnp.stack(lfp), jnp.stack(hp), jnp.stack(mkp), jnp.stack(mvp),
            jnp.stack(ks_), jnp.stack(vs_), jnp.stack(lfs), jnp.stack(hs))


_drawn_inputs = setup_inputs


def setup_inputs(seed=0):
    import zlib

    import numpy as np

    out = dict(_drawn_inputs(seed))
    spreads = {}
    factors = {'g_norm': 2.841, 'lam_re': 3.94, 'b_glu': 8.0, 'g_mem': 2.904, 'g_final': 2.79}
    for name, (base, spread) in spreads.items():
        noise = np.random.default_rng([zlib.crc32(name.encode()), seed]).standard_normal(out[name].shape)
        drawn = base * np.exp(spread * noise) if base else spread * noise
        out[name] = jnp.asarray(drawn.astype(out[name].dtype))
    for name, factor in factors.items():
        out[name] = (out[name] * factor).astype(out[name].dtype)
    return out
```

```python
from contextlib import ExitStack

import concourse.bass as bass
from concourse import mybir

F32 = mybir.dt.float32
F32R = mybir.dt.float32r
BF16 = mybir.dt.bfloat16
I32 = mybir.dt.int32
I64 = mybir.dt.int64
ALU = mybir.AluOpType
ACT = mybir.ActivationFunctionType
AX = mybir.AxisListType

P = 128
D = 1024
T = 4096
HD = 64
NF, WF = 6, 384
G, GC, NS, WS = 24, 16, 64, 384
NM, WM, NMEM = 4, 256, 256
KD = D // P
EPS = 1e-6
CQ, CK, CV, CF = 0, WF, 2 * WF, 3 * WF
CGA = CF + NF
CU = CGA + WF
CGS = CU + WS
CQM = CGS + WS
CGM = CQM + WM
DIN = CGM + WM
NEG = -1e30


def at(per, i, n):
    return per * (i + 1) + n


class Core:
    pass


def setup_constants(nc, c):
    with ExitStack() as s:
        filled = s.enter_context(nc.semaphore("const_filled"))
        made = s.enter_context(nc.semaphore("const_made"))
        block = s.enter_context(nc.Block())

        @block.gpsimd
        def _(pool):
            fills = [(c.ident, 0.0), (c.identb, 0.0), (c.upper, 1.0), (c.lower_strict, 1.0),
                     (c.mask_kq, 0.0), (c.mask_qk, 0.0), (c.ones, 1.0), (c.minus_half, -0.5)]
            for t, v in fills:
                pool.memset(t[:], v).then_inc(filled, 1)
            pool.wait_ge(filled, len(fills))
            for t in (c.ident, c.identb):
                pool.affine_select(out=t[:], in_=t[:], pattern=[[-1, P]], compare_op=ALU.not_equal,
                                   fill=1.0, base=0, channel_multiplier=1).then_inc(made, 1)
            pool.affine_select(out=c.upper[:], in_=c.upper[:], pattern=[[1, P]], compare_op=ALU.is_ge,
                               fill=0.0, base=0, channel_multiplier=-1).then_inc(made, 1)
            pool.affine_select(out=c.lower_strict[:], in_=c.lower_strict[:], pattern=[[-1, P]],
                               compare_op=ALU.is_gt, fill=0.0, base=0, channel_multiplier=1).then_inc(made, 1)
            pool.affine_select(out=c.mask_kq[:], in_=c.mask_kq[:], pattern=[[1, P]], compare_op=ALU.is_ge,
                               fill=NEG, base=0, channel_multiplier=-1).then_inc(made, 1)
            pool.affine_select(out=c.mask_qk[:], in_=c.mask_qk[:], pattern=[[-1, P]], compare_op=ALU.is_ge,
                               fill=NEG, base=0, channel_multiplier=1).then_inc(made, 1)
            pool.wait_ge(made, 6)


def project_prompt(nc, c, x_prompt, w_in, g_norm, k_out, v_out):
    TB = 1024
    NTB = T // TB
    NT = TB // P
    SEGW = WF + NF
    SEGS = [("q", CQ, WF), ("k", CK, WF), ("v", CV, WF + NF), ("ga", CGA, WF), ("u", CU, WS),
            ("gs", CGS, WS), ("qm", CQM, WM), ("gm", CGM, WM)]
    outs = []
    for si, (name, c0, w) in enumerate(SEGS):
        if name in ("k", "v", "u"):
            outs += [(si, t, None) for t in range(NT)]
        else:
            outs += [(si, m, h) for m in range(w // P) for h in range(2)]
    NO = len(outs)
    seg_end = [max(n for n, o in enumerate(outs) if o[0] == si) + 1 for si in range(len(SEGS))]
    PB = 5
    assert NO % PB == 0
    NG = KD * 2
    dest = {"q": (c.q_t, 0, 0.125), "qm": (c.qm_t, 0, 0.125), "ga": (c.gate_t, 0, None),
            "gs": (c.gate_t, WF, None), "gm": (c.gate_t, WF + WS, None)}
    x_v = x_prompt.rearrange("o (b t p) d -> (o b) p t d", p=P, t=NT)
    w_v = w_in.rearrange("o (k p) n -> (o p) k n", p=P)
    k_v = k_out.rearrange("l o (b t p) h d -> (l o b) t p (h d)", p=P, t=NT)
    v_v = v_out.rearrange("l o (b t p) h d -> (l o b) t p (h d)", p=P, t=NT)

    with ExitStack() as s:
        def sb(name, shape, dt=F32):
            return s.enter_context(nc.sbuf_tensor(name, shape, dt))

        def sem(name):
            return s.enter_context(nc.semaphore(name))

        x = sb("x_tok", [P, NT, D])
        xhi, xlo = sb("xhi", [P, KD, TB], F32R), sb("xlo", [P, KD, TB], F32R)
        wraw = sb("wraw", [P, KD, SEGW])
        whi, wlo = sb("whi", [P, 2, KD, SEGW], F32R), sb("wlo", [P, 2, KD, SEGW], F32R)
        fstage = sb("fstage", [P, 2, TB])
        tstage = sb("tstage", [P, 4, WF])
        ustage = sb("ustage", [P, G, 8, GC])
        gn = sb("gn", [P, KD])
        junk = sb("sq_junk", [P, D], BF16)
        ss, rstd = sb("ss", [P, NT]), sb("rstd", [P, NT])
        rstd_in = sb("rstd_in", [P, NT])
        x_loaded, w_loaded, g_loaded = sem("x_loaded"), sem("w_loaded"), sem("g_loaded")
        sq_done, mean_done, rstd_done, xn_done = sem("sq_done"), sem("mean_done"), sem("rstd_done"), sem("xn_done")
        tr_done, hi_done, lo_done = sem("tr_done"), sem("hi_done"), sem("lo_done")
        whi_done, wlo_done, proj_done, evac_done = sem("whi_done"), sem("wlo_done"), sem("proj_done"), sem("evac_done")
        f_stored = [sem(f"f_stored{j}") for j in range(2)]
        t_stored = [sem(f"t_stored{j}") for j in range(4)]
        u_stored = sem("u_stored")
        block = s.enter_context(nc.Block())
        NSEG = len(SEGS)
        NFM = sum(1 for si, m, h in outs if h == 1)
        fper = [16 * len([f for f in range(NFM) if f % 2 == j]) for j in range(2)]

        @block.sync
        def _(sp):
            with nc.allow_non_contiguous_dma(reason="1024 gains"):
                sp.dma_start(gn[:], g_norm.rearrange("o (k p) -> p (o k)", p=P)).then_inc(g_loaded, 16)
            with sp.Fori(0, NTB) as i:
                sp.wait_ge(lo_done, at(NG, i, 0))
                sp.dma_start(x[:], x_v[i]).then_inc(x_loaded, 16)
                for si, (_, c0, w) in enumerate(SEGS):
                    sp.wait_ge(wlo_done, at(NSEG, i, si))
                    sp.dma_start(wraw[:, :, 0:w], w_v[:, :, c0:c0 + w]).then_inc(w_loaded, 16)

        @block.gpsimd
        def _(pool):
            with pool.Fori(0, NTB) as i:
                pool.wait_ge(mean_done, i + 1)
                pool.tensor_tensor(rstd[:], rstd_in[:], c.minus_half[:, 0:NT], ALU.pow).then_inc(rstd_done, 1)

        @block.vector
        def _(dve):
            dve.sem_inc(lo_done, NG)
            dve.sem_inc(wlo_done, NSEG)
            dve.wait_ge(g_loaded, 16)

            def split(i, si):
                w = SEGS[si][2]
                dve.wait_ge(w_loaded, 16 * (NSEG * i + si + 1))
                before = seg_end[si - 2] if si >= 2 else seg_end[si - 2] - NO
                dve.wait_ge(proj_done, at(NO, i, before))
                dve.tensor_copy(whi[:, si % 2, :, 0:w], wraw[:, :, 0:w]).then_inc(whi_done, 1)
                dve.wait_ge(whi_done, NSEG * i + si + 1)
                hi = whi[:, si % 2, :, 0:w]
                dve.tensor_tensor(wlo[:, si % 2, :, 0:w], wraw[:, :, 0:w], hi.bitcast(F32),
                                  ALU.subtract).then_inc(wlo_done, 1)

            with dve.Fori(0, NTB) as i:
                dve.wait_ge(x_loaded, 16 * (i + 1))
                for t in range(NT):
                    if t:
                        dve.wait_ge(sq_done, NT * i + t)
                    dve.tensor_tensor_reduce(junk[:], x[:, t, :], x[:, t, :], 1.0, 0.0, ALU.mult, ALU.add,
                                             ss[:, t:t + 1]).then_inc(sq_done, 1)
                dve.wait_ge(sq_done, NT * (i + 1))
                dve.tensor_scalar(rstd_in[:], ss[:], 1.0 / D, EPS, ALU.mult, ALU.add).then_inc(mean_done, 1)
                dve.wait_ge(rstd_done, i + 1)
                for t in range(NT):
                    dve.tensor_scalar(x[:, t, :], x[:, t, :], rstd[:, t:t + 1], None,
                                      ALU.mult).then_inc(xn_done, 1)
                split(i, 0)
                for g in range(NG):
                    k, h = g // 2, g % 2
                    dve.wait_ge(hi_done, NG * i + g + 1)
                    hi = xhi[:, k, 512 * h:512 * (h + 1)]
                    dve.scalar_tensor_tensor(xlo[:, k, 512 * h:512 * (h + 1)], c.bank[g % 2][:], gn[:, k:k + 1],
                                             hi.bitcast(F32), ALU.mult, ALU.subtract).then_inc(lo_done, 1)
                for si in range(1, NSEG):
                    split(i, si)

        @block.tensor
        def _(pe):
            pe.sem_inc(proj_done, NO)
            with pe.Fori(0, NTB) as i:
                pe.wait_ge(xn_done, NT * (i + 1))
                for g in range(NG):
                    k, h = g // 2, g % 2
                    pe.wait_ge(lo_done, at(NG, i, g - 1))
                    for t in range(4):
                        tr = pe.transpose(c.bank[g % 2][:, t * P:(t + 1) * P],
                                          x[:, 4 * h + t, k * P:(k + 1) * P], c.ident[:])
                    tr.then_inc(tr_done, 1)
                pe.wait_ge(lo_done, at(NG, i, NG))
                for n, (si, m, h) in enumerate(outs):
                    w = SEGS[si][2]
                    if n == 0 or outs[n - 1][0] != si:
                        pe.wait_ge(wlo_done, at(NSEG, i, si + 1))
                    pe.wait_ge(evac_done, at(NO, i, n - PB + 1))
                    bank = c.bank[2 + n % PB]
                    b = si % 2
                    for k in range(KD):
                        for xs, ws in ((xhi, whi), (xlo, whi), (xhi, wlo)):
                            if h is not None:
                                lhsT, rhs = ws[:, b, k, m * P:(m + 1) * P], xs[:, k, 512 * h:512 * (h + 1)]
                                dst = bank[:, :]
                            elif SEGS[si][0] == "u":
                                lhsT, rhs, dst = xs[:, k, m:TB:8], ws[:, b, k, 0:w], bank[:, 0:w]
                            else:
                                lhsT, rhs, dst = xs[:, k, m * P:(m + 1) * P], ws[:, b, k, 0:w], bank[:, 0:w]
                            last = pe.matmul(dst, lhsT, rhs, start=(k == 0 and ws is whi and xs is xhi),
                                             stop=(k == KD - 1 and ws is wlo))
                    last.then_inc(proj_done, 1)

        @block.scalar
        def _(act):
            act.sem_inc(evac_done, NO)
            for j in range(2):
                act.sem_inc(f_stored[j], fper[j])
            for j in range(4):
                act.sem_inc(t_stored[j], 16 * 4)
            act.sem_inc(u_stored, 16)
            act.wait_ge(g_loaded, 16)
            with act.Fori(0, NTB) as i:
                for g in range(NG):
                    k, h = g // 2, g % 2
                    act.wait_ge(tr_done, NG * i + g + 1)
                    act.activation(xhi[:, k, 512 * h:512 * (h + 1)], c.bank[g % 2][:], ACT.Copy,
                                   scale=gn[:, k:k + 1]).then_inc(hi_done, 1)
                fm = tm = 0
                for n, (si, m, h) in enumerate(outs):
                    name, c0, w = SEGS[si]
                    act.wait_ge(proj_done, at(NO, i, n + 1))
                    bank = c.bank[2 + n % PB]
                    if h is not None:
                        dram, row, scale = dest[name]
                        slot = fm % 2
                        if h == 0:
                            act.wait_ge(f_stored[slot], at(fper[slot], i, 16 * (fm // 2)))
                        func = ACT.Silu if scale is None else ACT.Copy
                        act.activation(fstage[:, slot, 512 * h:512 * (h + 1)], bank[:], func,
                                       scale=1.0 if scale is None else scale).then_inc(evac_done, 1)
                        if h == 1:
                            act.wait_ge(evac_done, at(NO, i, n + 1))
                            r0 = row + m * P
                            act.dma_start(dram[r0:r0 + P, bass.ds(i * TB, TB)], fstage[:, slot, :]
                                          ).then_inc(f_stored[slot], 16)
                            fm += 1
                    elif name == "u":
                        if m == 0:
                            act.wait_ge(u_stored, at(16, i, 0))
                        act.activation(ustage[:, :, m, :], bank[:, 0:WS].rearrange("p (g c) -> p g c", c=GC),
                                       ACT.Copy).then_inc(evac_done, 1)
                        if m == NT - 1:
                            act.wait_ge(evac_done, at(NO, i, n + 1))
                            act.dma_start(c.u_chunks[i], ustage[:].rearrange("p g t c -> p (g t c)")
                                          ).then_inc(u_stored, 16)
                    else:
                        slot = tm % 4
                        act.wait_ge(t_stored[slot], at(64, i, 16 * (tm // 4)))
                        if name == "v":
                            act.activation(c.flogit[:, i * NT + m, :], bank[:, WF:WF + NF], ACT.Copy)
                        act.activation(tstage[:, slot, :], bank[:, 0:WF], ACT.Copy).then_inc(evac_done, 1)
                        act.wait_ge(evac_done, at(NO, i, n + 1))
                        act.dma_start((k_v if name == "k" else v_v)[i, m], tstage[:, slot, :]
                                      ).then_inc(t_stored[slot], 16)
                        tm += 1
            for j in range(2):
                act.wait_ge(f_stored[j], at(fper[j], NTB, 0))
            for j in range(4):
                act.wait_ge(t_stored[j], at(64, NTB, 0))
            act.wait_ge(u_stored, at(16, NTB, 0))


def forget_gates(nc, c, b_f, logf_out):
    NT = T // P
    with ExitStack() as s:
        def sb(name, shape, dt=F32):
            return s.enter_context(nc.sbuf_tensor(name, shape, dt))

        def sem(name):
            return s.enter_context(nc.semaphore(name))

        bf = sb("bf", [P, NF])
        z, zn, za, ez, sp_ = (sb(n, [P, NT, NF]) for n in ("fz", "fzn", "fza", "fez", "fsp"))
        lf = sb("lf", [P, NT, NF])
        pre = sb("lf_prefix", [P, NF, NT])
        prex = sb("lf_before", [P, NT, NF])
        rows = sb("crow_stage", [P, 2, P], F32R)
        loaded, dve_step, act_step, pe_step, stored = sem("bf_loaded"), sem("f_dve"), sem("f_act"), sem("f_pe"), sem("f_stored")
        block = s.enter_context(nc.Block())
        cum = c.bank[0][:, 0:NT * NF]

        @block.sync
        def _(sp):
            with nc.allow_non_contiguous_dma(reason="six forget gates a token"):
                sp.dma_start(bf[:], b_f[0].partition_broadcast(P)).then_inc(loaded, 16)
                sp.wait_ge(dve_step, 5)
                sp.dma_start(logf_out.rearrange("l o (t p) h -> p (l o t) h", p=P), lf[:]).then_inc(stored, 16)
                sp.wait_ge(dve_step, 17)
                sp.dma_start(c.negc_rows.rearrange("h (t p) -> (h t) p", p=P)[0:P], rows[:, 0, :].bitcast(F32)).then_inc(stored, 16)
                sp.dma_start(c.negc_rows.rearrange("h (t p) -> (h t) p", p=P)[P:NF * NT], rows[0:NF * NT - P, 1, :].bitcast(F32)
                             ).then_inc(stored, 16)
            sp.wait_ge(stored, 48)

        @block.vector
        def _(dve):
            n = [0]

            def done(ins):
                n[0] += 1
                ins.then_inc(dve_step, 1)
                dve.wait_ge(dve_step, n[0])

            dve.wait_ge(loaded, 16)
            done(dve.tensor_tensor(z[:], c.flogit[:], bf[:].unsqueeze(1).to_broadcast([P, NT, NF]), ALU.add))
            done(dve.tensor_scalar(zn[:], z[:], -1.0, None, ALU.mult))
            done(dve.tensor_tensor(za[:], z[:], zn[:], ALU.min))
            done(dve.tensor_scalar(zn[:], z[:], 0.0, None, ALU.min))
            dve.wait_ge(act_step, 2)
            done(dve.tensor_tensor(lf[:], zn[:], sp_[:], ALU.subtract))
            for h in range(NF):
                dve.tensor_tensor_scan(pre[:, h, :], c.ones[:, 0:NT], lf[:, :, h], 0.0, ALU.mult,
                                       ALU.add).then_inc(dve_step, 1)
            dve.memset(prex[:, 0, :], 0.0).then_inc(dve_step, 1)
            dve.wait_ge(dve_step, 12)
            dve.tensor_copy(prex[:, 1:NT, :], pre[:, :, 0:NT - 1].rearrange("p h t -> p t h")).then_inc(dve_step, 1)
            dve.wait_ge(pe_step, 1)
            dve.tensor_scalar(c.negc[:], cum.rearrange("p (t h) -> p h t", h=NF), -1.0, None, ALU.mult
                              ).then_inc(dve_step, 1)
            dve.wait_ge(pe_step, 2)
            dve.tensor_copy(rows[:, 0, :], c.bank[1][:, 0:P]).then_inc(dve_step, 1)
            dve.wait_ge(pe_step, 3)
            dve.tensor_copy(rows[0:NF * NT - P, 1, :], c.bank[2][0:NF * NT - P, 0:P]).then_inc(dve_step, 1)
            dve.wait_ge(dve_step, 16)
            dve.sem_inc(dve_step, 1)

        @block.scalar
        def _(act):
            act.wait_ge(dve_step, 3)
            act.activation(ez[:], za[:], ACT.Exp).then_inc(act_step, 1)
            act.wait_ge(act_step, 1)
            act.activation(sp_[:], ez[:], ACT.Ln, bias=1.0).then_inc(act_step, 1)

        @block.tensor
        def _(pe):
            pe.wait_ge(dve_step, 13)
            pe.matmul(cum, c.upper[:], lf[:].rearrange("p t h -> p (t h)"), start=True, stop=False)
            pe.matmul(cum, c.ones[:], prex[:].rearrange("p t h -> p (t h)"), start=False, stop=True
                      ).then_inc(pe_step, 1)
            pe.wait_ge(dve_step, 14)
            negc = c.negc[:].rearrange("p h t -> p (h t)")
            pe.transpose(c.bank[1][:, 0:P], negc[:, 0:P], c.ident[:]).then_inc(pe_step, 1)
            pe.transpose(c.bank[2][0:NF * NT - P, 0:P], negc[:, P:NF * NT], c.ident[:]).then_inc(pe_step, 1)


def fox_prompt(nc, c, k_out, v_out):
    NB = T // 512
    NT = T // P
    k_h = k_out.rearrange("l o (t p) h d -> (l o h) p t d", p=P)
    v_h = v_out.rearrange("l o (t p) h d -> (l o h) p t d", p=P)
    q_h = c.q_t.rearrange("(h d) t -> h d t", d=HD)
    g_h = c.gate_t.rearrange("(h d) t -> h d t", d=HD)
    m_h = c.mix_t.rearrange("(h d) t -> h d t", d=HD)
    NPRE = 3
    pre = [(b, r, ch, 512 if ch < b else (r + 1) * P) for b in range(NB) for r in range(4) for ch in range(b + 1)]
    pre_end = [4 * (b + 1) * (b + 2) // 2 for b in range(NB)]
    main = [(b, j, max(0, (j - 4 * b) * P)) for b in range(NB) for j in range(4 * b + 4)]
    main_end = [sum(4 * x + 4 for x in range(b + 1)) for b in range(NB)]
    NPR, NMN = len(pre), len(main)
    NTR = 8

    with ExitStack() as s:
        def sb(name, shape, dt=F32):
            return s.enter_context(nc.sbuf_tensor(name, shape, dt))

        def sem(name):
            return s.enter_context(nc.semaphore(name))

        q2 = sb("q2", [P, T])
        qhi = sb("qhi", [P, T], F32R)
        qlo = sb("qlo", [HD + 2, T], F32R)
        qone = sb("qone", [HD + 2, T], F32R)
        ktok = sb("ktok", [P, NT, HD])
        khl = sb("khl", [P, NT, 2, HD])
        kst = sb("kst", [P, T], F32R)
        kone = sb("kone", [HD + 2, T], F32R)
        vone = sb("vone", [P, NT, P])
        gate = sb("gate_a", [HD, T])
        ncol = sb("ncol", [P, NT])
        p = sb("p", [P, 3, 512])
        pm = sb("pm", [P, 4, NB])
        nm = sb("nm", [P, 2, 4])
        mrow = sb("mrow", [4, 2, P], F32R)
        rec = sb("rec", [HD, 512])
        on = sb("on", [HD, 512])
        og = sb("og", [HD, 2, 512])
        q_in, k_in, v_in, c_in, g_in = (sem(n) for n in ("q_in", "k_in", "v_in", "c_in", "g_in"))
        ready, ones_set = sem("qk_split"), sem("ones_set")
        khl_done, ktr, kst_done, kone_done = sem("khl_done"), sem("ktr"), sem("kst_done"), sem("kone_done")
        pre_s, pre_max, nm_done, nm_tr, mrow_done, m_in = (sem(n) for n in ("pre_s", "pre_max", "nm_done", "nm_tr", "mrow_done", "m_in"))
        sc, ex, pv = sem("scores"), sem("exp_done"), sem("pv_done")
        o_rec, o_norm, o_gated = sem("o_rec"), sem("o_norm"), sem("o_gated")
        o_stored = [sem("o_stored0"), sem("o_stored1")]
        block = s.enter_context(nc.Block())
        SB, OB, XB = 3, 6, 3

        @block.sync
        def _(sp):
            with sp.Fori(0, NF) as h:
                sp.wait_ge(o_gated, at(NB, h, 0))
                sp.dma_start(q2[0:HD, :], q_h[h]).then_inc(q_in, 16)
                sp.dma_start(q2[HD:P, :], q_h[h]).then_inc(q_in, 16)
                sp.dma_start(ktok[:], k_h[h]).then_inc(k_in, 16)
                sp.dma_start(vone[:, :, 0:HD], v_h[h]).then_inc(v_in, 16)
                sp.dma_start(kone[HD + 1:HD + 2, :].bitcast(F32), c.negc_rows.rearrange("h (o t) -> h o t", o=1)[h]).then_inc(c_in, 16)
                sp.dma_start(gate[:], g_h[h]).then_inc(g_in, 16)
                for b in range(NB + 2):
                    if b >= 2:
                        sp.wait_ge(o_gated, at(NB, h, b - 1))
                        sp.dma_start(m_h[h, :, 512 * (b - 2):512 * (b - 1)], og[:, b % 2, :]).then_inc(o_stored[b % 2], 16)
                    if b >= NB:
                        continue
                    sp.wait_ge(mrow_done, NB * h + b + 1)
                    sp.dma_start(qlo[HD:HD + 1, 512 * b:512 * (b + 1)].bitcast(F32), mrow[:, b % 2, :].bitcast(F32)).then_inc(m_in, 16)
            for j in range(2):
                sp.wait_ge(o_stored[j], at(16 * NB // 2, NF, 0))

        @block.gpsimd
        def _(pool):
            pool.memset(vone[:, :, HD:P], 1.0).then_inc(ones_set, 1)
            pool.wait_ge(ones_set, 1)
            pool.memset(kone[HD:HD + 1, :].bitcast(F32), 1.0).then_inc(ones_set, 1)
            pool.wait_ge(ones_set, 2)
            pool.memset(qlo[HD:HD + 2, :].bitcast(F32), 0.0).then_inc(ones_set, 1)
            pool.wait_ge(ones_set, 3)
            pool.memset(qone[HD:HD + 2, :].bitcast(F32), 1.0).then_inc(ones_set, 1)
            pool.wait_ge(ones_set, 4)
            pool.memset(qone[HD:HD + 1, :].bitcast(F32), 0.0).then_inc(ones_set, 1)

        @block.vector
        def _(dve):
            dve.sem_inc(o_gated, NB)
            dve.sem_inc(pre_max, NPR)
            dve.sem_inc(o_norm, NB)
            for j in range(2):
                dve.sem_inc(o_stored[j], 16 * NB // 2)
            with dve.Fori(0, NF) as h:
                dve.tensor_copy(ncol[:], c.negc[:, h, :]).then_inc(ready, 1)
                dve.wait_ge(k_in, 16 * (h + 1))
                dve.tensor_copy(khl[:, :, 0, :].bitcast(F32R), ktok[:]).then_inc(khl_done, 1)
                dve.wait_ge(khl_done, 2 * h + 1)
                dve.tensor_tensor(khl[:, :, 1, :].bitcast(F32R), ktok[:], khl[:, :, 0, :], ALU.subtract).then_inc(khl_done, 1)
                dve.wait_ge(q_in, 32 * (h + 1))
                dve.tensor_copy(qhi[:], q2[:]).then_inc(ready, 1)
                dve.wait_ge(ready, 4 * h + 2)
                dve.tensor_copy(qone[0:HD, :], qhi[0:HD, :].bitcast(F32)).then_inc(ready, 1)
                dve.tensor_tensor(qlo[0:HD, :], q2[0:HD, :], qhi[0:HD, :].bitcast(F32), ALU.subtract).then_inc(ready, 1)
                for g in range(NTR):
                    dve.wait_ge(kst_done, NTR * h + g + 1)
                    dve.tensor_copy(kone[0:HD, 512 * g:512 * (g + 1)], kst[0:HD, 512 * g:512 * (g + 1)].bitcast(F32)
                                    ).then_inc(kone_done, 1)

                def maxima(n0, n1):
                    for n in range(n0, n1):
                        b, r, ch, w = pre[n]
                        dve.wait_ge(pre_s, NPR * h + n + 1)
                        dve.tensor_reduce(pm[:, r, ch:ch + 1], c.bank[XB + n % NPRE][:, 0:w], AX.X, ALU.max
                                          ).then_inc(pre_max, 1)
                        if n + 1 == pre_end[b]:
                            dve.wait_ge(pre_max, at(NPR, h, n + 1))
                            dve.tensor_reduce(nm[:, b % 2, :], pm[:, :, 0:b + 1], AX.X, ALU.max, negate=True
                                              ).then_inc(nm_done, 1)
                            dve.wait_ge(nm_tr, NB * h + b + 1)
                            dve.tensor_copy(mrow[:, b % 2, :], c.bank[OB + 1][0:4, 384:512]).then_inc(mrow_done, 1)

                maxima(0, pre_end[0])
                for b in range(NB):
                    if b + 1 < NB:
                        maxima(pre_end[b], pre_end[b + 1])
                    dve.wait_ge(pv, at(NMN, h, main_end[b]))
                    ob = c.bank[OB]
                    dve.reciprocal(rec[:], ob[HD:P, :]).then_inc(o_rec, 1)
                    dve.wait_ge(o_rec, NB * h + b + 1)
                    dve.tensor_tensor(on[:], ob[0:HD, :], rec[:], ALU.mult).then_inc(o_norm, 1)
                    dve.wait_ge(o_norm, at(NB, h, b + 1))
                    dve.wait_ge(g_in, 16 * (h + 1))
                    dve.wait_ge(o_stored[b % 2], at(16 * NB // 2, h, 16 * (b // 2)))
                    dve.tensor_tensor(og[:, b % 2, :], on[:], gate[:, 512 * b:512 * (b + 1)], ALU.mult
                                      ).then_inc(o_gated, 1)

        @block.scalar
        def _(act):
            act.sem_inc(ex, NMN)
            with act.Fori(0, NF) as h:
                for g in range(NTR):
                    act.wait_ge(ktr, NTR * h + g + 1)
                    act.activation(kst[:, 512 * g:512 * (g + 1)], c.bank[g % 2][:], ACT.Copy).then_inc(kst_done, 1)
                act.wait_ge(ready, 4 * h + 1)
                for n, (b, j, q0) in enumerate(main):
                    act.wait_ge(sc, NMN * h + n + 1)
                    act.wait_ge(pv, at(NMN, h, n - 2))
                    act.activation(p[:, n % 3, q0:512], c.bank[n % SB][:, q0:512], ACT.Exp,
                                   bias=ncol[:, j:j + 1]).then_inc(ex, 1)

        @block.tensor
        def _(pe):
            pe.sem_inc(pv, NMN)
            pe.wait_ge(ones_set, 5)
            with pe.Fori(0, NF) as h:
                pe.wait_ge(khl_done, 2 * (h + 1))
                for g in range(NTR):
                    if g >= 2:
                        pe.wait_ge(kst_done, NTR * h + g - 1)
                    else:
                        pe.wait_ge(ex, at(NMN, h, 0))
                    for t in range(4):
                        tr = pe.transpose(c.bank[g % 2][:, t * P:(t + 1) * P],
                                          khl[:, 4 * g + t, :, :].rearrange("p a d -> p (a d)"), c.ident[:])
                    tr.then_inc(ktr, 1)
                pe.wait_ge(kst_done, NTR * (h + 1))
                pe.wait_ge(kone_done, NTR * (h + 1))
                pe.wait_ge(ready, 4 * (h + 1))
                pe.wait_ge(c_in, 16 * (h + 1))

                def first_pass(n0, n1):
                    for n in range(n0, n1):
                        b, r, ch, w = pre[n]
                        pe.wait_ge(pre_max, at(NPR, h, n - NPRE + 1))
                        qt = (4 * b + r) * P
                        bank = c.bank[XB + n % NPRE]
                        mm = pe.matmul(bank[:, 0:w], qone[:, qt:qt + P], kone[:, 512 * ch:512 * ch + w],
                                       start=True, stop=True)
                        if ch == b:
                            mm = pe.matmul(bank[:, w - P:w], c.identb[:], c.mask_qk[:], start=False, stop=True,
                                           skip_group_check=True)
                        mm.then_inc(pre_s, 1)

                def maxima_to_rows(b):
                    pe.wait_ge(nm_done, NB * h + b + 1)
                    pe.wait_ge(mrow_done, NB * h + b) if b else None
                    pe.transpose(c.bank[OB + 1][0:4, 384:512], nm[:, b % 2, :], c.ident[:]).then_inc(nm_tr, 1)

                def weighted(n):
                    b, j, q0 = main[n]
                    pe.wait_ge(ex, at(NMN, h, n + 1))
                    if j == 0:
                        pe.wait_ge(o_norm, at(NB, h, b))
                    pe.matmul(c.bank[OB][:, q0:512], vone[:, j, :], p[:, n % 3, q0:512], start=(j == 0),
                              stop=(j == 4 * b + 3), skip_group_check=True).then_inc(pv, 1)

                first_pass(0, pre_end[0])
                maxima_to_rows(0)
                pe.wait_ge(v_in, 16 * (h + 1))
                for b in range(NB):
                    pe.wait_ge(m_in, 16 * (NB * h + b + 1))
                    n_pre, rows_due = pre_end[b], b + 1 < NB
                    for j in range(4 * b + 4):
                        n = (main_end[b - 1] if b else 0) + j
                        q0 = main[n][2]
                        qs = slice(512 * b + q0, 512 * (b + 1))
                        bank = c.bank[n % SB]
                        pe.wait_ge(ex, at(NMN, h, n - SB + 1))
                        pe.matmul(bank[:, q0:512], kst[:, j * P:(j + 1) * P], qhi[:, qs], start=True, stop=False)
                        diag = j >= 4 * b
                        mm = pe.matmul(bank[:, q0:512], kone[:, j * P:(j + 1) * P], qlo[:, qs], start=False, stop=True)
                        if diag:
                            mm = pe.matmul(bank[:, q0:q0 + P], c.identb[:], c.mask_kq[:], start=False, stop=True,
                                           skip_group_check=True)
                        mm.then_inc(sc, 1)
                        if b + 1 < NB:
                            upto = min(n_pre + 2, pre_end[b + 1])
                            first_pass(n_pre, upto)
                            if n_pre == upto and rows_due:
                                maxima_to_rows(b + 1)
                                rows_due = False
                            n_pre = upto
                        if j:
                            weighted(n - 1)
                    weighted(n)
                    if b + 1 < NB and rows_due:
                        maxima_to_rows(b + 1)


def memory_prompt(nc, c, mem, g_mem, w_kv, mk_out, mv_out):
    NB = T // 512
    MT = NMEM // P
    with ExitStack() as s:
        def sb(name, shape, dt=F32):
            return s.enter_context(nc.sbuf_tensor(name, shape, dt))

        def sem(name):
            return s.enter_context(nc.semaphore(name))

        x = sb("mem_x", [P, MT, D])
        w = sb("mem_w", [P, KD, 2 * WM])
        gm = sb("mem_g", [P, KD])
        xt = sb("mem_xt", [P, KD, NMEM])
        junk = sb("mem_junk", [P, D], BF16)
        ss, rin, rstd = sb("mem_ss", [P, MT]), sb("mem_rin", [P, MT]), sb("mem_rstd", [P, MT])
        kv = sb("mem_kv", [P, MT, 2 * WM])
        kt = sb("mem_kt", [P, 2, NMEM])
        q = sb("mem_q", [P, 2, 2, 512])
        gate = sb("mem_gate", [HD, 2, NM, 512])
        nmax, tot, rtot = sb("mem_nmax", [P, 2, NM]), sb("mem_tot", [P, 2, NM]), sb("mem_rtot", [P, 2, NM])
        p = sb("mem_p", [P, 2, NM, NMEM])
        pn = sb("mem_pn", [P, 2, NM, NMEM])
        pt = sb("mem_pt", [P, 2, NM, MT, 512])
        og = sb("mem_og", [HD, 2, NM, 512])
        loaded, step, powed, pe1 = sem("mem_loaded"), sem("mem_step"), sem("mem_powed"), sem("mem_pe")
        q_in = [sem("mem_q_in0"), sem("mem_q_in1")]
        s_done, max_done, exp_done, norm_done, tr_done, pt_done = (
            sem(n) for n in ("mem_s", "mem_max", "mem_exp", "mem_norm", "mem_tr", "mem_ptd"))
        r_done, o_done, og_done = sem("mem_r"), sem("mem_o"), sem("mem_ogd")
        o_stored = [sem("mem_st0"), sem("mem_st1")]
        kv_stored = sem("mem_kv_stored")
        block = s.enter_context(nc.Block())
        NT = 4
        q_v = c.qm_t.rearrange("(a p) (b t) -> b p a t", p=P, t=512)
        g_v = c.gate_t[WF + WS:D].rearrange("(h d) (b t) -> b d h t", d=HD, t=512)
        m_v = c.mix_t[WF + WS:D].rearrange("(h d) (b t) -> b d h t", d=HD, t=512)

        @block.sync
        def _(sp):
            with nc.allow_non_contiguous_dma(reason="1024 gains"):
                sp.dma_start(gm[:], g_mem.rearrange("o (k p) -> p (o k)", p=P)).then_inc(loaded, 16)
            sp.dma_start(x[:], mem.rearrange("o (t p) d -> p (o t) d", p=P)).then_inc(loaded, 16)
            sp.dma_start(w[:], w_kv.rearrange("o (k p) n -> p (o k) n", p=P)).then_inc(loaded, 16)
            with sp.Fori(0, NB // 2) as i:
                for j in range(2):
                    sp.wait_ge(og_done, at(2 * NM, i, (j - 1) * NM + NM))
                    sp.dma_start(q[:, j], q_v[2 * i + j]).then_inc(q_in[j], 16)
                    sp.dma_start(gate[:, j], g_v[2 * i + j]).then_inc(q_in[j], 16)

        @block.gpsimd
        def _(pool):
            pool.wait_ge(step, MT + 1)
            pool.tensor_tensor(rstd[:], rin[:], c.minus_half[:, 0:MT], ALU.pow).then_inc(powed, 1)

        @block.vector
        def _(dve):
            for sem_ in (og_done,):
                dve.sem_inc(sem_, 2 * NM)
            dve.sem_inc(pt_done, 4 * NT)
            dve.sem_inc(norm_done, 2 * NT * NM)
            dve.wait_ge(loaded, 48)
            for t in range(MT):
                dve.tensor_tensor_reduce(junk[:], x[:, t, :], x[:, t, :], 1.0, 0.0, ALU.mult, ALU.add,
                                         ss[:, t:t + 1]).then_inc(step, 1)
                dve.wait_ge(step, t + 1)
            dve.tensor_scalar(rin[:], ss[:], 1.0 / D, EPS, ALU.mult, ALU.add).then_inc(step, 1)
            dve.wait_ge(powed, 1)
            for t in range(MT):
                dve.tensor_scalar(x[:, t, :], x[:, t, :], rstd[:, t:t + 1], None, ALU.mult).then_inc(step, 1)
            for k in range(KD):
                dve.wait_ge(pe1, k + 1)
                dve.tensor_scalar(xt[:, k, :], c.bank[k % 4][:, 0:NMEM], gm[:, k:k + 1], None, ALU.mult
                                  ).then_inc(step, 1)
            for t in range(MT):
                dve.wait_ge(pe1, KD + t + 1)
                dve.tensor_copy(kv[:, t, :], c.bank[4 + t][:]).then_inc(step, 1)
            dve.wait_ge(pe1, KD + MT + 1)
            dve.tensor_copy(kt[:].rearrange("p a n -> p (a n)"), c.bank[0][:]).then_inc(step, 1)

            def prepare(i, j, t):
                n = 4 * j + t
                for a in range(2):
                    dve.wait_ge(s_done, 16 * i + 2 * n + a + 1)
                    dve.tensor_reduce(nmax[:, t % 2, a:NM:2],
                                      c.bank[2 * (t % 2) + a][:].rearrange("p (h k) -> p h k", h=2), AX.X, ALU.max,
                                      negate=True).then_inc(max_done, 1)

            def finish(i, j, t):
                n = 4 * j + t
                dve.wait_ge(exp_done, at(2 * NT * NM, i, NM * (n + 1)))
                dve.reciprocal(rtot[:, t % 2, :], tot[:, t % 2, :]).then_inc(r_done, 1)
                dve.wait_ge(r_done, 8 * i + n + 1)
                dve.wait_ge(tr_done, at(32, i, 4 * (n - 1)))
                for h in range(NM):
                    dve.tensor_scalar(pn[:, t % 2, h, :], p[:, t % 2, h, :], rtot[:, t % 2, h:h + 1], None,
                                      ALU.mult).then_inc(norm_done, 1)
                for b in range(2):
                    dve.wait_ge(tr_done, at(32, i, 4 * n + 2 * b + 2))
                    dve.tensor_copy(pt[:, j, 2 * b:2 * b + 2, :, t * P:(t + 1) * P],
                                    c.bank[4 + b][:].rearrange("p (h k q) -> p h k q", h=2, k=MT)).then_inc(pt_done, 1)

            with dve.Fori(0, NB // 2) as i:
                for j in range(2):
                    prepare(i, j, 0)
                    for t in range(NT):
                        if t + 1 < NT:
                            prepare(i, j, t + 1)
                        finish(i, j, t)
                    dve.wait_ge(q_in[j], 32 * (i + 1))
                    dve.wait_ge(o_stored[j], at(16, i, 0))
                    for h in range(NM):
                        dve.wait_ge(o_done, 2 * NM * i + NM * j + h + 1)
                        dve.tensor_tensor(og[:, j, h, :], c.bank[6 + h % 2][0:HD, :], gate[:, j, h, :], ALU.mult
                                          ).then_inc(og_done, 1)

        @block.scalar
        def _(act):
            act.sem_inc(exp_done, 2 * NT * NM)
            for j in range(2):
                act.sem_inc(o_stored[j], 16)
            act.wait_ge(step, 1 + 2 * MT + KD + MT)
            act.dma_start(mk_out.rearrange("l o (t p) h d -> p (l o t) (h d)", p=P), kv[:, :, 0:WM]).then_inc(kv_stored, 16)
            act.dma_start(mv_out.rearrange("l o (t p) h d -> p (l o t) (h d)", p=P), kv[:, :, WM:]).then_inc(kv_stored, 16)
            with act.Fori(0, NB // 2) as i:
                for j in range(2):
                    for t in range(NT):
                        n = 4 * j + t
                        act.wait_ge(norm_done, at(2 * NT * NM, i, NM * (n - 1)))
                        for h in range(NM):
                            act.wait_ge(max_done, 16 * i + 2 * n + h % 2 + 1)
                            act.activation(p[:, t % 2, h, :], c.bank[2 * (t % 2) + h % 2][:, (h // 2) * NMEM:(h // 2 + 1) * NMEM],
                                           ACT.Exp, bias=nmax[:, t % 2, h:h + 1], accum_out=tot[:, t % 2, h:h + 1]
                                           ).then_inc(exp_done, 1)
                    act.wait_ge(og_done, at(2 * NM, i, NM * (j + 1)))
                    act.dma_start(m_v[2 * i + j], og[:, j]).then_inc(o_stored[j], 16)
            for j in range(2):
                act.wait_ge(o_stored[j], at(16, NB // 2, 0))
            act.wait_ge(kv_stored, 32)

        @block.tensor
        def _(pe):
            pe.sem_inc(tr_done, 32)
            pe.wait_ge(step, 2 * MT + 1)
            for k in range(KD):
                if k >= 4:
                    pe.wait_ge(step, 2 * MT + 1 + k - 3)
                for t in range(MT):
                    tr = pe.transpose(c.bank[k % 4][:, t * P:(t + 1) * P], x[:, t, k * P:(k + 1) * P], c.ident[:])
                tr.then_inc(pe1, 1)
            pe.wait_ge(step, 2 * MT + 1 + KD)
            for t in range(MT):
                for k in range(KD):
                    mm = pe.matmul(c.bank[4 + t][:], xt[:, k, t * P:(t + 1) * P], w[:, k, :], start=(k == 0), stop=(k == KD - 1))
                mm.then_inc(pe1, 1)
            pe.wait_ge(step, 2 * MT + 1 + KD + MT)
            for a in range(2):
                for t in range(MT):
                    tr = pe.transpose(c.bank[0][:, a * NMEM + t * P:a * NMEM + (t + 1) * P], kv[:, t, a * P:(a + 1) * P], c.ident[:])
            tr.then_inc(pe1, 1)
            pe.wait_ge(step, 2 * MT + 2 + KD + MT)

            def scores(i, j, t):
                n = 4 * j + t
                if t == 0:
                    pe.wait_ge(q_in[j], 32 * (i + 1))
                pe.wait_ge(exp_done, at(2 * NT * NM, i, NM * (n - 1)))
                for h in range(NM):
                    r = HD * (h % 2)
                    mm = pe.matmul(c.bank[2 * (t % 2) + h % 2][:, (h // 2) * NMEM:(h // 2 + 1) * NMEM],
                                   q[r:r + HD, j, h // 2, t * P:(t + 1) * P], kt[r:r + HD, h // 2, :], start=True, stop=True)
                    if h >= 2:
                        mm.then_inc(s_done, 1)

            with pe.Fori(0, NB // 2) as i:
                for j in range(2):
                    scores(i, j, 0)
                    for t in range(NT):
                        if t + 1 < NT:
                            scores(i, j, t + 1)
                        n = 4 * j + t
                        for h in range(NM):
                            pe.wait_ge(norm_done, at(2 * NT * NM, i, NM * n + h + 1))
                            if h % 2 == 0:
                                pe.wait_ge(pt_done, at(4 * NT, i, 2 * (n - 1) + h // 2 + 1))
                            for k in range(MT):
                                tr = pe.transpose(c.bank[4 + h // 2][:, ((h % 2) * MT + k) * P:((h % 2) * MT + k + 1) * P],
                                                  pn[:, t % 2, h, k * P:(k + 1) * P], c.ident[:])
                            tr.then_inc(tr_done, 1)
                    pe.wait_ge(pt_done, at(4 * NT, i, 2 * (4 * j + NT)))
                    for h in range(NM):
                        pe.wait_ge(og_done, at(2 * NM, i, NM * j + h - 1))
                        for k in range(MT):
                            mm = pe.matmul(c.bank[6 + h % 2][0:HD, :], kv[:, k, WM + h * HD:WM + (h + 1) * HD], pt[:, j, h, k, :],
                                           start=(k == 0), stop=(k == MT - 1))
                        mm.then_inc(o_done, 1)


def sample_project(nc, c, a, o):
    W = 512
    CH = [(c0, min(W, DIN - c0)) for c0 in range(0, DIN, W)]
    with ExitStack() as s:
        def sb(name, shape, dt=F32):
            return s.enter_context(nc.sbuf_tensor(name, shape, dt))

        def sem(name):
            return s.enter_context(nc.semaphore(name))

        x = sb("sx", [8, D])
        junk = sb("sx_junk", [8, D], BF16)
        ss, rin, rstd = sb("sx_ss", [8, 1]), sb("sx_rin", [8, 1]), sb("sx_rstd", [8, 1])
        gn = sb("sx_g", [P, KD])
        xt = sb("sx_t", [P, KD, 8])
        w = sb("sx_w", [P, 3, KD, W])
        z = sb("sx_z", [8, DIN])
        bf = sb("sx_bf", [8, NF])
        f = [sb(f"sx_f{i}", [8, NF]) for i in range(5)]
        loaded, step, powed, turned, prod, acted, stored = (
            sem(n) for n in ("sx_loaded", "sx_step", "sx_powed", "sx_turned", "sx_prod", "sx_acted", "sx_stored"))
        w_in = [sem(f"sx_w_in{j}") for j in range(3)]
        block = s.enter_context(nc.Block())
        w_v = a["w_in"].rearrange("o (k p) n -> (o p) k n", p=P)
        BASE = 5

        @block.sync
        def _(sp):
            with nc.allow_non_contiguous_dma(reason="1024 gains"):
                sp.dma_start(gn[:], a["g_norm"].rearrange("o (k p) -> p (o k)", p=P)).then_inc(loaded, 16)
            sp.dma_start(x[:], a["x_sample"].rearrange("b o d -> (b o) d")).then_inc(loaded, 16)
            sp.dma_start(bf[:], a["b_f"][0].partition_broadcast(8)).then_inc(loaded, 16)
            for n, (c0, cw) in enumerate(CH):
                if n >= 3:
                    sp.wait_ge(prod, n - 2)
                sp.dma_start(w[:, n % 3, :, 0:cw], w_v[:, :, c0:c0 + cw]).then_inc(w_in[n % 3], 16)
            sp.wait_ge(step, BASE + len(CH))
            sp.dma_start(c.zs, z[:]).then_inc(stored, 16)
            sp.dma_start(o["k_sample"].rearrange("l b o h d -> (l b o) (h d)"), z[:, CK:CK + WF]).then_inc(stored, 16)
            sp.dma_start(o["v_sample"].rearrange("l b o h d -> (l b o) (h d)"), z[:, CV:CV + WF]).then_inc(stored, 16)
            sp.wait_ge(step, BASE + len(CH) + 5)
            sp.dma_start(o["logf_sample"].rearrange("l b o h -> (l b o) h"), c.lfs[:]).then_inc(stored, 16)
            sp.wait_ge(stored, 64)

        @block.gpsimd
        def _(pool):
            pool.wait_ge(step, 2)
            pool.tensor_tensor(rstd[:], rin[:], c.minus_half[0:8, 0:1], ALU.pow).then_inc(powed, 1)

        @block.vector
        def _(dve):
            n = [0]

            def done(ins):
                n[0] += 1
                ins.then_inc(step, 1)
                dve.wait_ge(step, n[0])

            dve.wait_ge(loaded, 48)
            done(dve.tensor_tensor_reduce(junk[:], x[:], x[:], 1.0, 0.0, ALU.mult, ALU.add, ss[:]))
            done(dve.tensor_scalar(rin[:], ss[:], 1.0 / D, EPS, ALU.mult, ALU.add))
            dve.wait_ge(powed, 1)
            done(dve.tensor_scalar(x[:], x[:], rstd[:], None, ALU.mult))
            dve.wait_ge(turned, 1)
            done(dve.tensor_tensor(xt[:], c.bank[0][:, 0:KD * 8].rearrange("p (k b) -> p k b", b=8),
                                   gn[:].unsqueeze(2).to_broadcast([P, KD, 8]), ALU.mult))
            done(dve.tensor_copy(f[0][:], bf[:]))
            for m, (c0, cw) in enumerate(CH):
                dve.wait_ge(prod, m + 1)
                done(dve.tensor_copy(z[:, c0:c0 + cw], c.bank[1 + m % 2][0:8, 0:cw]))
            done(dve.tensor_tensor(f[1][:], z[:, CF:CF + NF], f[0][:], ALU.add))
            done(dve.tensor_scalar(f[2][:], f[1][:], -1.0, None, ALU.mult))
            done(dve.tensor_tensor(f[3][:], f[1][:], f[2][:], ALU.min))
            done(dve.tensor_scalar(f[2][:], f[1][:], 0.0, None, ALU.min))
            dve.wait_ge(acted, 2)
            done(dve.tensor_tensor(c.lfs[:], f[2][:], f[4][:], ALU.subtract))

        @block.scalar
        def _(act):
            act.wait_ge(step, BASE + len(CH) + 3)
            act.activation(f[0][:], f[3][:], ACT.Exp).then_inc(acted, 1)
            act.wait_ge(acted, 1)
            act.activation(f[4][:], f[0][:], ACT.Ln, bias=1.0).then_inc(acted, 1)

        @block.tensor
        def _(pe):
            pe.wait_ge(step, 3)
            for k in range(KD):
                tr = pe.transpose(c.bank[0][:, k * 8:(k + 1) * 8], x[:, k * P:(k + 1) * P], c.ident[0:8, 0:8])
            tr.then_inc(turned, 1)
            pe.wait_ge(step, 4)
            for m, (c0, cw) in enumerate(CH):
                pe.wait_ge(w_in[m % 3], 16 * (m // 3 + 1))
                if m >= 2:
                    pe.wait_ge(step, BASE + m - 1)
                for k in range(KD):
                    mm = pe.matmul(c.bank[1 + m % 2][0:8, 0:cw], xt[:, k, :], w[:, m % 3, k, 0:cw], start=(k == 0), stop=(k == KD - 1))
                mm.then_inc(prod, 1)


STEP = 8
NCH = T // STEP
SC = STEP * GC
O_COS, O_SIN = 0, NCH
O_R = 2 * NCH
O_W1 = O_R + (2 * STEP - 1) * GC
O_W2 = O_W1 + SC
O_CC = O_W2 + SC
O_D = O_CC + GC
O_R8, O_A1, O_B1 = O_D + 1, O_D + 2, O_D + 3
GPW = O_B1 + 1
TWO_PI = 6.283185307179586
PI1 = 6.28125
PI2 = 0.0019350051879882812
PI3 = 3.0199159819567e-07
ROUND = 12582912.0


def ssm_constants(nc, c, a):
    with ExitStack() as s:
        def sb(name, shape, dt=F32):
            return s.enter_context(nc.sbuf_tensor(name, shape, dt))

        def sem(name):
            return s.enter_context(nc.semaphore(name))

        gp = sb("gp", [P, G, GPW])
        lre, lim, ldt = sb("lre", [P, G]), sb("lim", [P, G]), sb("ldt", [P, G])
        b1, b2 = sb("b_ri", [P, G, GC]), sb("b_ir", [P, G, GC])
        cin = sb("c_in", [P, 3, 2, 2, NS])
        cd, ce = sb("c_ri", [P, G, GC]), sb("c_ir", [P, G, GC])
        bb1, bb2 = sb("bb_ri", [P, G, GC]), sb("bb_ir", [P, G, GC])
        sgn = sb("sgn", [P, 2])
        v = {n: sb("v_" + n, [P, G]) for n in
             ("dt", "a", "th", "mag", "t1", "t2", "t3", "sn", "sh", "cs", "lr", "li", "nr", "den", "fr", "fi", "fi2")}
        ar, ai, nai = sb("ar", [P, G, 9]), sb("ai", [P, G, 9]), sb("nai", [P, G, 9])
        uc, us = sb("uc", [P, G, 12]), sb("us", [P, G, 12])
        big = sb("big", [P, G, 256])
        dcol = sb("dcol", [P, G])
        loaded, step, acted, turned, stored = (sem(n) for n in ("sp_loaded", "sp_step", "sp_act", "sp_pe", "sp_stored"))
        signs, ready = sem("sp_signs"), sem("sp_ready")
        block = s.enter_context(nc.Block())
        H = HD
        REDUCED = 8

        @block.sync
        def _(sp):
            with nc.allow_non_contiguous_dma(reason="parameters, states on rows"):
                for r in (0, H):
                    sp.dma_start(lre[r:r + H, :], a["lam_re"].rearrange("o g p -> p (o g)")).then_inc(loaded, 16)
                    sp.dma_start(lim[r:r + H, :], a["lam_im"].rearrange("o g p -> p (o g)")).then_inc(loaded, 16)
                    x, y = ("b_re", "b_im") if r == 0 else ("b_im", "b_re")
                    sp.dma_start(b1[r:r + H], a[x].rearrange("o g p c -> p (o g) c")).then_inc(loaded, 16)
                    sp.dma_start(b2[r:r + H], a[y].rearrange("o g p c -> p (o g) c")).then_inc(loaded, 16)
                sp.dma_start(ldt[:], a["log_dt"][0].partition_broadcast(P)).then_inc(loaded, 16)
                for j, (x, y) in enumerate((("c_re", "c_im"), ("c_im", "c_re"))):
                    sp.dma_start(cin[:, :, j, 0, :], a[x].rearrange("o g c p -> (o g c) p").rearrange("(t q) p -> q t p", q=P)
                                 ).then_inc(loaded, 16)
                    sp.dma_start(cin[:, :, j, 1, :], a[y].rearrange("o g c p -> (o g c) p").rearrange("(t q) p -> q t p", q=P)
                                 ).then_inc(loaded, 16)
                for t in range(STEP):
                    sp.dma_start(dcol[t * GC:(t + 1) * GC, :], a["d_skip"].rearrange("o g c -> c (o g)")).then_inc(loaded, 16)
            sp.wait_ge(ready, 1)
            sp.dma_start(c.ssm_gp.rearrange("g p w -> p g w"), gp[:]).then_inc(stored, 16)
            sp.wait_ge(stored, 16)

        @block.gpsimd
        def _(pool):
            pool.memset(sgn[0:H, 0:1], 1.0).then_inc(signs, 1)
            pool.memset(sgn[H:P, 0:1], -1.0).then_inc(signs, 1)
            pool.wait_ge(signs, 2)
            pool.memset(sgn[0:H, 1:2], -1.0).then_inc(signs, 1)
            pool.memset(sgn[H:P, 1:2], 1.0).then_inc(signs, 1)

        @block.tensor
        def _(pe):
            pe.wait_ge(loaded, 16 * (9 + 4 + STEP))
            for j in range(2):
                for t in range(3):
                    tr = pe.transpose(c.bank[j][:, t * P:(t + 1) * P], cin[:, t, j, :, :].rearrange("q a p -> q (a p)"), c.ident[:])
                tr.then_inc(turned, 1)

        @block.scalar
        def _(act):
            act.wait_ge(loaded, 16 * (9 + 4 + STEP))
            act.activation(v["dt"][:], ldt[:], ACT.Exp).then_inc(acted, 1)
            act.wait_ge(step, 1)
            act.activation(v["mag"][:], v["a"][:], ACT.Exp).then_inc(acted, 1)
            act.activation(gp[:, :, O_R8], v["a"][:], ACT.Exp, scale=float(STEP)).then_inc(acted, 1)
            act.wait_ge(step, REDUCED)
            act.activation(v["sn"][:], v["t2"][:], ACT.Sin).then_inc(acted, 1)
            act.activation(v["sh"][:], v["t2"][:], ACT.Sin, scale=0.5).then_inc(acted, 1)

        @block.vector
        def _(dve):
            n = [0]

            def done(ins):
                n[0] += 1
                ins.then_inc(step, 1)
                dve.wait_ge(step, n[0])

            def tt(out, x, y, op):
                done(dve.tensor_tensor(out, x, y, op))

            def ts(out, x, y, op, y2=None, op2=ALU.bypass):
                done(dve.tensor_scalar(out, x, y, y2, op, op2))

            M, A_, S_ = ALU.mult, ALU.add, ALU.subtract
            w = {k: t[:] for k, t in v.items()}
            dve.wait_ge(loaded, 16 * (9 + 4 + STEP))
            dve.wait_ge(signs, 4)
            sg, ns = sgn[:, 0:1], sgn[:, 1:2]
            dve.wait_ge(acted, 1)
            tt(w["a"], lre[:], w["dt"], M)
            tt(w["th"], lim[:], w["dt"], M)
            ts(w["t1"], w["th"], 1.0 / TWO_PI, M)
            ts(w["t1"], w["t1"], ROUND, A_, -ROUND, A_)
            done(dve.scalar_tensor_tensor(w["t2"], w["t1"], -PI1, w["th"], M, A_))
            done(dve.scalar_tensor_tensor(w["t3"], w["t1"], -PI2, w["t2"], M, A_))
            done(dve.scalar_tensor_tensor(w["den"], w["t1"], -PI3, w["t3"], M, A_))
            ts(w["t2"], w["den"], 3.1415925, ALU.min, -3.1415925, ALU.max)
            assert n[0] == REDUCED
            dve.wait_ge(acted, 5)
            tt(w["t1"], w["sh"], w["sh"], M)
            ts(w["cs"], w["t1"], -2.0, M, 1.0, A_)
            tt(w["lr"], w["mag"], w["cs"], M)
            tt(w["li"], w["mag"], w["sn"], M)
            ts(w["nr"], w["lr"], -1.0, A_)
            tt(w["t1"], lre[:], lre[:], M)
            tt(w["t2"], lim[:], lim[:], M)
            tt(w["t1"], w["t1"], w["t2"], A_)
            done(dve.reciprocal(w["den"], w["t1"]))
            tt(w["t1"], w["nr"], lre[:], M)
            tt(w["t2"], w["li"], lim[:], M)
            tt(w["t1"], w["t1"], w["t2"], A_)
            tt(w["fr"], w["t1"], w["den"], M)
            tt(w["t1"], w["li"], lre[:], M)
            tt(w["t2"], w["nr"], lim[:], M)
            tt(w["t1"], w["t1"], w["t2"], S_)
            tt(w["t2"], w["t1"], w["den"], M)
            ts(w["fi"], w["t2"], ns, M)
            ts(w["fi2"], w["t2"], sg, M)
            bg = [P, G, GC]
            for out, x, y, f in ((bb1, b1, b2, "fi"), (bb2, b2, b1, "fi2")):
                tt(out[:], x[:], w["fr"].unsqueeze(2).to_broadcast(bg), M)
                tt(big[:, :, 0:GC], y[:], w[f].unsqueeze(2).to_broadcast(bg), M)
                tt(out[:], out[:], big[:, :, 0:GC], A_)
            done(dve.memset(ar[:, :, 0], 1.0))
            done(dve.memset(ai[:, :, 0], 0.0))
            for k in range(8):
                tt(ar[:, :, k + 1], ar[:, :, k], w["lr"], M)
                tt(w["t1"], ai[:, :, k], w["li"], M)
                tt(ar[:, :, k + 1], ar[:, :, k + 1], w["t1"], S_)
                tt(ai[:, :, k + 1], ar[:, :, k], w["li"], M)
                tt(w["t1"], ai[:, :, k], w["lr"], M)
                tt(ai[:, :, k + 1], ai[:, :, k + 1], w["t1"], A_)
            ts(nai[:], ai[:], ns, M)
            R = gp[:, :, O_R:O_W1].rearrange("p g (m c) -> p g m c", c=GC)
            done(dve.memset(R[:, :, STEP:], 0.0))
            sc = [P, G, GC]
            for m in range(STEP):
                k = STEP - 1 - m
                tt(R[:, :, m, :], bb1[:], ar[:, :, k:k + 1].to_broadcast(sc), M)
                tt(big[:, :, 0:GC], bb2[:], nai[:, :, k:k + 1].to_broadcast(sc), M)
                tt(R[:, :, m, :], R[:, :, m, :], big[:, :, 0:GC], A_)
            dve.wait_ge(turned, 2)
            done(dve.tensor_copy(cd[:].rearrange("p g c -> p (g c)"), c.bank[0][:, 0:G * GC]))
            done(dve.tensor_copy(ce[:].rearrange("p g c -> p (g c)"), c.bank[1][:, 0:G * GC]))
            ts(gp[:, :, O_CC:O_D], cd[:], sg, M)
            for t in range(STEP):
                k = t + 1
                one, two = gp[:, :, O_W1 + t * GC:O_W1 + (t + 1) * GC], gp[:, :, O_W2 + t * GC:O_W2 + (t + 1) * GC]
                tt(one, gp[:, :, O_CC:O_D], ar[:, :, k:k + 1].to_broadcast(sc), M)
                tt(big[:, :, 0:GC], ce[:], ai[:, :, k:k + 1].to_broadcast(sc), M)
                tt(one, one, big[:, :, 0:GC], S_)
                tt(two, cd[:], nai[:, :, k:k + 1].to_broadcast(sc), M)
                tt(big[:, :, 0:GC], ce[:], ar[:, :, k:k + 1].to_broadcast(sc), M)
                tt(two, two, big[:, :, 0:GC], S_)
            done(dve.tensor_copy(uc[:, :, 0], w["cs"]))
            done(dve.tensor_copy(us[:, :, 0], w["sn"]))
            for j in range(11):
                tt(w["t1"], us[:, :, j], us[:, :, j], M)
                tt(uc[:, :, j + 1], uc[:, :, j], uc[:, :, j], M)
                tt(uc[:, :, j + 1], uc[:, :, j + 1], w["t1"], S_)
                tt(w["t1"], uc[:, :, j], us[:, :, j], M)
                ts(us[:, :, j + 1], w["t1"], 2.0, M)
            cosT, sinT = gp[:, :, O_COS:O_COS + NCH], gp[:, :, O_SIN:O_SIN + NCH]
            done(dve.memset(cosT[:, :, 0:1], 1.0))
            done(dve.memset(sinT[:, :, 0:1], 0.0))
            for j in range(9):
                m = 1 << j
                sh = [P, G, m]
                cj, sj = uc[:, :, j + 3:j + 4].to_broadcast(sh), us[:, :, j + 3:j + 4].to_broadcast(sh)
                lo_c, lo_s, hi_c, hi_s = cosT[:, :, 0:m], sinT[:, :, 0:m], cosT[:, :, m:2 * m], sinT[:, :, m:2 * m]
                tt(hi_c, lo_c, cj, M)
                tt(big[:, :, 0:m], lo_s, sj, M)
                tt(hi_c, hi_c, big[:, :, 0:m], S_)
                tt(hi_s, lo_s, cj, M)
                tt(big[:, :, 0:m], lo_c, sj, M)
                tt(hi_s, hi_s, big[:, :, 0:m], A_)
            done(dve.tensor_copy(gp[:, :, O_D], dcol[:]))
            done(dve.tensor_copy(gp[:, :, O_A1], w["lr"]))
            done(dve.tensor_copy(gp[:, :, O_B1], nai[:, :, 1]))
            dve.sem_inc(ready, 1)



def ssm(nc, c, a, ssm_prompt, ssm_sample):
    NB = 4
    with ExitStack() as s:
        def sb(name, shape, dt=F32):
            return s.enter_context(nc.sbuf_tensor(name, shape, dt))

        def sem(name):
            return s.enter_context(nc.semaphore(name))

        y = sb("ssm_y", [P, NB, STEP, WS])
        gp = sb("ssm_gp", [P, 2, GPW])
        u = sb("ssm_u", [P, 2, NB, SC])
        us = sb("ssm_us", [8, 2, SC])
        ut = sb("ssm_ut", [P, 2, NCH])
        sm = sb("ssm_sm", [P, 2, 2 * SC + 8])
        toep = sb("ssm_toep", [P, 2, SC])
        wj = sb("ssm_wj", [P, 2, SC])
        vc, vs, vr, gs = (sb(n, [P, 2, NCH]) for n in ("ssm_vc", "ssm_vs", "ssm_vr", "ssm_g"))
        cg, sg = sb("ssm_cg", [P, 2, NCH + 1]), sb("ssm_sg", [P, 2, NCH + 1])
        hl = sb("ssm_hl", [P, 2, G])
        h0in = sb("ssm_h0in", [96, 2, NS, 2])
        h0p = sb("ssm_h0p", [96, 2, 2, 2, NS])
        h0, h0s, hn, hm, vsm = (sb(n, [P, 8, G]) for n in ("ssm_h0", "ssm_h0s", "ssm_hn", "ssm_hm", "ssm_vsm"))
        ab = sb("ssm_ab", [P, G, 2])
        yst = sb("ssm_yst", [GC, G, 8])
        hlt = sb("ssm_hlt", [G, 2, P])
        hlo = sb("ssm_hlo", [G, NS, 2])
        hno = sb("ssm_hno", [96, 2, NS, 2])
        g_in = [sem("ssm_in0"), sem("ssm_in1")]
        h_in, prep, prep_pe, zeroed = sem("ssm_h_in"), sem("ssm_prep"), sem("ssm_prep_pe"), sem("ssm_zeroed")
        ut_tr, sm_tr, ut_done, sm_done, toep_done = (sem(n) for n in ("ssm_ut_tr", "ssm_sm_tr", "ssm_ut_d", "ssm_sm_d", "ssm_toep_d"))
        v_done, turned, scanned, cg_done, small = (sem(n) for n in ("ssm_v", "ssm_turned", "ssm_scan", "ssm_cg_d", "ssm_small"))
        y_done, y_out = sem("ssm_y_d"), sem("ssm_y_out")
        tail, tail_pe, ends, stored = sem("ssm_tail"), sem("ssm_tail_pe"), sem("ssm_ends"), sem("ssm_stored")
        block = s.enter_context(nc.Block())
        u_v = c.u_chunks.rearrange("b p (g w) -> g p b w", g=G)
        z_u = c.zs[:, CU:CU + WS].rearrange("b (g c) -> g b c", c=GC)

        @block.sync
        def _(sp):
            sp.dma_start(h0in[:], a["state_ssm"].rearrange("o b g p r -> (o b g) (p r)").rearrange("(t q) w -> q t w", q=96)
                         .rearrange("q t (p r) -> q t p r", r=2)).then_inc(h_in, 16)
            with nc.allow_non_contiguous_dma(reason="two columns of each group"):
                sp.dma_start(ab[:], c.ssm_gp[:, :, O_A1:O_A1 + 2].rearrange("g p w -> p g w")).then_inc(h_in, 16)
            sp.wait_ge(zeroed, 1)
            with sp.Fori(0, G // 2) as i:
                for j in range(2):
                    sp.wait_ge(y_out, at(2, i, j - 1))
                    sp.wait_ge(small, at(2, i, j - 1))
                    sp.dma_start(gp[:, j], c.ssm_gp[2 * i + j]).then_inc(g_in[j], 16)
                    sp.dma_start(u[:, j], u_v[2 * i + j]).then_inc(g_in[j], 16)
                    sp.dma_start(us[:, j, SC - GC:SC], z_u[2 * i + j]).then_inc(g_in[j], 16)
            sp.wait_ge(y_out, at(2, G // 2, 0))
            sp.dma_start(c.y_chunks.rearrange("b p t f -> p b (t f)"), y[:].rearrange("p b t f -> p b (t f)")).then_inc(stored, 16)
            sp.dma_start(c.ys_t.rearrange("(g c) b -> c g b", c=GC), yst[:]).then_inc(stored, 16)
            sp.wait_ge(ends, 5)
            sp.dma_start(ssm_prompt.rearrange("o b g p r -> (o b g) p r"), hlo[:]).then_inc(stored, 16)
            sp.dma_start(ssm_sample.rearrange("o b g p r -> (o b g) (p r)").rearrange("(t q) w -> q t w", q=96), hno[:]
                         .rearrange("q t p r -> q t (p r)")).then_inc(stored, 16)
            sp.wait_ge(stored, 64)

        @block.gpsimd
        def _(pool):
            pool.memset(us[:], 0.0).then_inc(zeroed, 1)

        @block.vector
        def _(dve):
            dve.sem_inc(cg_done, 4)
            dve.sem_inc(small, 2)
            dve.sem_inc(turned, 4)
            dve.sem_inc(toep_done, 2)
            M, A_, S_ = ALU.mult, ALU.add, ALU.subtract
            dve.memset(cg[:, :, 0], 0.0).then_inc(prep, 1)
            dve.memset(sg[:, :, 0], 0.0).then_inc(prep, 1)
            dve.wait_ge(h_in, 32)
            for r in range(2):
                dve.tensor_copy(h0p[:, :, 0, r, :], h0in[:, :, :, r]).then_inc(prep, 1)
                dve.tensor_copy(h0p[:, :, 1, r, :], h0in[:, :, :, 1 - r]).then_inc(prep, 1)
            dve.wait_ge(prep_pe, 1)
            dve.tensor_copy(h0[:].rearrange("p b g -> p (b g)"), c.bank[0][:, 0:8 * G]).then_inc(prep, 1)
            dve.tensor_copy(h0s[:].rearrange("p b g -> p (b g)"), c.bank[1][:, 0:8 * G]).then_inc(prep, 1)
            dve.wait_ge(prep, 8)
            with dve.Fori(0, G // 2) as i:
                for j in range(2):
                    g = 2 * i + j
                    dve.wait_ge(sm_done, at(2, i, j + 1))
                    dve.wait_ge(y_done, at(2, i, j - 1))
                    dve.scalar_tensor_tensor(toep[:, j], c.ident[:], gp[:, j, O_D:O_D + 1], sm[:, j, SC:2 * SC], M, A_)
                    dve.tensor_copy(wj[:, j, 0:HD], sm[:, j, HD:SC])
                    dve.tensor_scalar(wj[:, j, HD:SC], sm[:, j, 0:HD], -1.0, None, M).then_inc(toep_done, 1)
                for j in range(2):
                    g = 2 * i + j
                    cosT, sinT = gp[:, j, O_COS:O_COS + NCH], gp[:, j, O_SIN:O_SIN + NCH]
                    dve.wait_ge(v_done, 2 * i + j + 1)
                    dve.tensor_tensor(vc[:, j], c.bank[4][:], cosT, M).then_inc(turned, 1)
                    dve.tensor_tensor(vs[:, j], c.bank[5][:], sinT, M).then_inc(turned, 1)
                    dve.wait_ge(turned, at(4, i, 2 * j + 2))
                    dve.tensor_tensor(vr[:, j], vc[:, j], vs[:, j], A_).then_inc(scanned, 1)
                    dve.wait_ge(scanned, 4 * i + 2 * j + 1)
                    dve.tensor_tensor_scan(gs[:, j], gp[:, j, O_R8:O_R8 + 1].to_broadcast([P, NCH]), vr[:, j], 0.0, M, A_
                                           ).then_inc(scanned, 1)
                    dve.wait_ge(scanned, 4 * i + 2 * j + 2)
                    dve.wait_ge(y_done, at(2, i, j - 1))
                    dve.tensor_tensor(cg[:, j, 1:NCH + 1], cosT, gs[:, j], M).then_inc(cg_done, 1)
                    dve.tensor_tensor(sg[:, j, 1:NCH + 1], sinT, gs[:, j], M).then_inc(cg_done, 1)
                    dve.wait_ge(cg_done, at(4, i, 2 * j + 2))
                    dve.tensor_copy(hl[:, 0, bass.ds(g, 1)], cg[:, j, NCH:NCH + 1])
                    dve.tensor_copy(hl[:, 1, bass.ds(g, 1)], sg[:, j, NCH:NCH + 1]).then_inc(small, 1)
            bc = [P, 8, G]
            dve.wait_ge(y_out, at(2, G // 2, 0))
            dve.tensor_tensor(hn[:], h0[:], ab[:, :, 0].unsqueeze(1).to_broadcast(bc), M).then_inc(tail, 1)
            dve.tensor_tensor(hm[:], h0s[:], ab[:, :, 1].unsqueeze(1).to_broadcast(bc), M).then_inc(tail, 1)
            dve.wait_ge(tail, 2)
            dve.tensor_tensor(hn[:], hn[:], hm[:], A_).then_inc(tail, 1)
            dve.wait_ge(tail, 3)
            dve.tensor_tensor(hn[:], hn[:], vsm[:], A_).then_inc(tail, 1)
            dve.wait_ge(tail_pe, 1)
            dve.tensor_copy(hlt[:].rearrange("g a w -> g (a w)"), c.bank[0][0:G, 0:2 * P]).then_inc(ends, 1)
            dve.wait_ge(ends, 1)
            dve.tensor_tensor(hlo[:, :, 0], hlt[:, 0, 0:HD], hlt[:, 1, HD:P], S_).then_inc(ends, 1)
            dve.tensor_tensor(hlo[:, :, 1], hlt[:, 0, HD:P], hlt[:, 1, 0:HD], A_).then_inc(ends, 1)
            for r in range(2):
                dve.tensor_copy(hno[:, :, :, r], c.bank[1][0:96, 0:2 * P].rearrange("q (t r p) -> q t p r", t=2, r=2)[:, :, :, r]
                                ).then_inc(ends, 1)

        @block.scalar
        def _(act):
            act.sem_inc(sm_done, 2)
            act.sem_inc(ut_done, 2)
            act.sem_inc(y_out, 2)
            with act.Fori(0, G // 2) as i:
                for j in range(2):
                    act.wait_ge(ut_tr, 2 * i + j + 1)
                    act.wait_ge(y_done, at(2, i, j - 1))
                    act.activation(ut[:, j], c.bank[j][:], ACT.Copy).then_inc(ut_done, 1)
                    act.wait_ge(sm_tr, 2 * i + j + 1)
                    act.activation(sm[:, j], c.bank[2 + j][:, 0:2 * SC + 8], ACT.Copy).then_inc(sm_done, 1)
                for j in range(2):
                    g = 2 * i + j
                    act.wait_ge(y_done, at(2, i, j + 1))
                    act.activation(vsm[:, :, g], c.bank[7][:, 0:8], ACT.Copy)
                    act.activation(yst[:, g, :], c.bank[7][0:GC, 16:24], ACT.Gelu)
                    act.activation(y[:, :, :, bass.ds(g * GC, GC)], c.bank[6][:].rearrange("p (b t c) -> p b t c", b=NB, c=GC),
                                   ACT.Gelu).then_inc(y_out, 1)

        @block.tensor
        def _(pe):
            pe.sem_inc(y_done, 2)
            pe.wait_ge(prep, 6)
            for k in range(2):
                for t in range(2):
                    tr = pe.transpose(c.bank[k][:, t * 96:(t + 1) * 96], h0p[:, t, k, :, :].rearrange("q r p -> q (r p)"), c.ident[0:96, 0:96])
            tr.then_inc(prep_pe, 1)
            pe.wait_ge(prep, 8)
            with pe.Fori(0, G // 2) as i:
                for j in range(2):
                    pe.wait_ge(g_in[j], 48 * (i + 1))
                    pe.wait_ge(ut_done, at(2, i, j - 1))
                    for b in range(NB):
                        tr = pe.transpose(c.bank[j][:, b * P:(b + 1) * P], u[:, j, b, :], c.ident[:])
                    tr.then_inc(ut_tr, 1)
                    pe.wait_ge(sm_done, at(2, i, j - 1))
                    small_b = c.bank[2 + j]
                    pe.transpose(small_b[:, 0:SC], gp[:, j, O_R:O_R + SC], c.ident[:])
                    for t in range(STEP):
                        w0 = O_R + (STEP - 1 - t) * GC
                        pe.matmul(small_b[:, SC + t * GC:SC + (t + 1) * GC], gp[:, j, w0:w0 + SC], gp[:, j, O_CC:O_CC + GC],
                                  start=True, stop=True)
                    pe.transpose(small_b[:, 2 * SC:2 * SC + 8], us[:, j, :], c.ident[0:8, 0:8]).then_inc(sm_tr, 1)
                for j in range(2):
                    g = 2 * i + j
                    pe.wait_ge(ut_done, at(2, i, j + 1))
                    pe.wait_ge(toep_done, at(2, i, j + 1))
                    pe.wait_ge(turned, at(4, i, 2 * j))
                    pe.matmul(c.bank[4][:], sm[:, j, 0:SC], ut[:, j], start=True, stop=True)
                    pe.matmul(c.bank[5][:], wj[:, j], ut[:, j], start=True, stop=True).then_inc(v_done, 1)
                for j in range(2):
                    g = 2 * i + j
                    w1, w2 = gp[:, j, O_W1:O_W1 + SC], gp[:, j, O_W2:O_W2 + SC]
                    pe.wait_ge(cg_done, at(4, i, 2 * j + 2))
                    pe.wait_ge(y_out, at(2, i, j))
                    pe.matmul(c.bank[7][:, 0:8], sm[:, j, 0:SC], sm[:, j, 2 * SC:], start=True, stop=True)
                    for b in range(NB):
                        dst = c.bank[6][:, b * P:(b + 1) * P]
                        pe.matmul(dst, ut[:, j, b * P:(b + 1) * P], toep[:, j], start=True, stop=False)
                        pe.matmul(dst, cg[:, j, b * P:(b + 1) * P], w1, start=False, stop=False)
                        pe.matmul(dst, sg[:, j, b * P:(b + 1) * P], w2, start=False, stop=True)
                    dst = c.bank[7][0:GC, 16:24]
                    pe.matmul(dst, toep[:, j, SC - GC:SC], sm[:, j, 2 * SC:], start=True, stop=False)
                    pe.matmul(dst, w1[:, 0:GC], h0[:, :, g], start=False, stop=True).then_inc(y_done, 1)
            pe.wait_ge(small, at(2, G // 2, 0))
            pe.wait_ge(tail, 4)
            for r in range(2):
                pe.transpose(c.bank[0][0:G, r * P:(r + 1) * P], hl[:, r, :], c.ident[:])
            for t in range(2):
                tr = pe.transpose(c.bank[1][0:96, t * P:(t + 1) * P], hn[:].rearrange("p b g -> p (b g)")[:, t * 96:(t + 1) * 96], c.ident[:])
            tr.then_inc(tail_pe, 1)


def sample_attend(nc, c, a):
    NBS, NPG = a["page_table"].shape
    NPOOL = a["cache_k"].shape[1]
    NMT = NMEM // P
    BH, BM = NBS * NF, NBS * NM
    with ExitStack() as s:
        def sb(name, shape, dt=F32):
            return s.enter_context(nc.sbuf_tensor(name, shape, dt))

        def sem(name):
            return s.enter_context(nc.semaphore(name))

        pages = sb("at_pages", [1, NBS * NPG], I32)
        z = sb("at_z", [NBS, DIN])
        kb, vb = sb("at_k", [P, 2, NPG, WF]), sb("at_v", [P, 2, NPG, WF])
        qb = sb("at_qb", [P, 2, WF])
        prod = sb("at_prod", [P, NPG, WF])
        lf = sb("at_lf", [P, NBS, NPG, NF])
        lfx = sb("at_lfx", [P, NBS, NPG, NF])
        sc = sb("at_s", [P, NBS, NPG, NF])
        mk, mv = sb("at_mk", [P, NBS, NMT, WM]), sb("at_mv", [P, NBS, NMT, WM])
        mq = sb("at_mq", [P, NBS, WM])
        ms = sb("at_ms", [P, NBS, NMT, NM])
        mx = sb("at_mx", [P, BH + BM])
        mxa = sb("at_mxa", [P, BH + BM])
        qk = sb("at_qk", [NBS, WF])
        new = sb("at_new", [NBS, 2, NF])
        newd = sb("at_newd", [NBS, 2, NBS, NF])
        newb = sb("at_newb", [P, 2, NBS, NF])
        pn = sb("at_pn", [P, NBS, NF])
        part = sb("at_part", [P, BH + BM])
        rt = sb("at_rt", [P, BH + BM])
        zt = sb("at_zt", [P, 11, NBS])
        zg = sb("at_zg", [P, 8, NBS])
        of = sb("at_of", [P, 3, NBS])
        t0 = sb("at_t0", [P, 3, NBS])
        loaded, m_in, p_in, lf_in = sem("at_loaded"), sem("at_m_in"), sem("at_p_in"), sem("at_lf_in")
        k_in, v_in = [sem("at_k0"), sem("at_k1")], [sem("at_v0"), sem("at_v1")]
        step, pe_, act_, pool_ = sem("at_step"), sem("at_pe"), sem("at_act"), sem("at_pool")
        k_mul, k_red, ov, o_out = sem("at_kmul"), sem("at_kred"), sem("at_ov"), sem("at_oo")
        block = s.enter_context(nc.Block())
        ck = a["cache_k"].rearrange("o n p h d -> (o n) p (h d)")
        cv = a["cache_v"].rearrange("o n p h d -> (o n) p (h d)")
        cl = a["cache_logf"].rearrange("o n p h -> (o n) p h")
        z_q = c.zs[:, 0:WF]
        LOADS = 16 * 2

        NEWD_AT, LFX_AT, MAX_AT, EXP_AT, SUM_AT, NORM_AT = 6, 15, 23, 27, 30, 35

        @block.sync
        def _(sp):
            sp.dma_start(pages[:], a["page_table"].rearrange("(o b) n -> o (b n)", o=1)).then_inc(p_in, 16)
            sp.dma_start(z[:], c.zs).then_inc(loaded, 16)
            sp.dma_start(mq[:], c.zs[:, CQM:CQM + WM].partition_broadcast(P)).then_inc(loaded, 16)
            sp.dma_start(mk[:], a["cache_mem_k"].rearrange("o b (t p) h d -> p (o b) t (h d)", p=P)).then_inc(m_in, 16)
            sp.dma_start(mv[:], a["cache_mem_v"].rearrange("o b (t p) h d -> p (o b) t (h d)", p=P)).then_inc(m_in, 16)
            sp.wait_ge(p_in, 16)
            with sp.Fori(0, NBS // 2) as i:
                for j in range(2):
                    b = 2 * i + j
                    sp.wait_ge(k_mul, at(2, i, j - 1))
                    sp.dma_start(qb[:, j], z_q[b].partition_broadcast(P)).then_inc(k_in[j], 16)
                    for n in range(NPG):
                        pid = sp.value_load(pages[0:1, bass.ds(b * NPG + n, 1)], min_val=0, max_val=NPOOL - 1)
                        sp.dma_start(kb[:, j, n, :], ck[pid]).then_inc(k_in[j], 16)

        @block.scalar
        def _(act):
            act.wait_ge(p_in, 16)
            with nc.allow_non_contiguous_dma(reason="six log f a key"):
                with act.Fori(0, NBS) as b:
                    for n in range(NPG):
                        pid = act.value_load(pages[0:1, bass.ds(b * NPG + n, 1)], min_val=0, max_val=NPOOL - 1)
                        act.dma_start(lf[:, b, n, :], cl[pid]).then_inc(lf_in, 16)
            act.wait_ge(pe_, 1)
            act.activation(zg[:], c.bank[0][:, 3 * NBS:11 * NBS].rearrange("p (k b) -> p k b", b=NBS), ACT.Silu).then_inc(act_, 1)
            act.wait_ge(step, EXP_AT)
            act.activation(sc[:], sc[:], ACT.Exp).then_inc(act_, 1)
            act.activation(ms[:], ms[:], ACT.Exp, scale=HD ** -0.5).then_inc(act_, 1)
            act.activation(pn[:], pn[:], ACT.Exp).then_inc(act_, 1)
            with act.Fori(0, NBS // 2) as i:
                for j in range(2):
                    act.wait_ge(ov, at(2, i, j - 1))
                    for n in range(NPG):
                        pid = act.value_load(pages[0:1, bass.ds((2 * i + j) * NPG + n, 1)], min_val=0, max_val=NPOOL - 1)
                        act.dma_start(vb[:, j, n, :], cv[pid]).then_inc(v_in[j], 16)

        @block.gpsimd
        def _(pool):
            pool.wait_ge(step, MAX_AT)
            pool.partition_all_reduce(mxa[:], mx[:], P, bass.bass_isa.ReduceOp.max).then_inc(pool_, 1)


        @block.vector
        def _(dve):
            n = [0]
            M, A_, S_ = ALU.mult, ALU.add, ALU.subtract

            def done(ins):
                n[0] += 1
                ins.then_inc(step, 1)
                dve.wait_ge(step, n[0])

            dve.sem_inc(k_mul, 2)
            dve.wait_ge(loaded, LOADS)
            done(dve.tensor_copy(new[:, 1, :], c.lfs[:]))
            done(dve.tensor_tensor(qk[:], z[:, CQ:CQ + WF], z[:, CK:CK + WF], M))
            done(dve.tensor_reduce(new[:, 0, :], qk[:].rearrange("b (h d) -> b h d", d=HD), AX.X, A_))
            done(dve.tensor_scalar(new[:, 0, :], new[:, 0, :], HD ** -0.5, None, M))
            for k in range(2):
                done(dve.tensor_tensor(newd[:, k], c.ident[0:NBS, 0:NBS].unsqueeze(2).to_broadcast([NBS, NBS, NF]),
                                       new[:, k, :].unsqueeze(1).to_broadcast([NBS, NBS, NF]), M))
            assert n[0] == NEWD_AT
            dve.wait_ge(lf_in, 16 * NBS * NPG)
            done(dve.memset(lfx[:, :, NPG - 1, :], 0.0))
            for g in range(NPG - 2, -1, -1):
                done(dve.tensor_tensor(lfx[:, :, g, :], lfx[:, :, g + 1, :], lf[:, :, g + 1, :], A_))
            dve.wait_ge(pe_, 2)
            done(dve.tensor_copy(newb[:].rearrange("p k b h -> p (k b h)"), c.bank[1][:, 0:2 * BH]))
            assert n[0] == LFX_AT
            with dve.Fori(0, NBS // 2) as i:
                for j in range(2):
                    dve.wait_ge(k_in[j], 16 * (NPG + 1) * (i + 1))
                    dve.tensor_tensor(prod[:], kb[:, j], qb[:, j, :].unsqueeze(1).to_broadcast([P, NPG, WF]), M).then_inc(k_mul, 1)
                    dve.wait_ge(k_mul, at(2, i, j + 1))
                    dve.tensor_reduce(sc[:, 2 * i + j], prod[:].rearrange("p n (h d) -> p n h d", d=HD), AX.X, A_).then_inc(k_red, 1)
                    dve.wait_ge(k_red, 2 * i + j + 1)
            dve.wait_ge(pe_, 3)
            bf = c.bank[2][:, 0:NBS * NPG * NF]
            scf = sc[:].rearrange("p b n h -> p (b n h)")
            done(dve.scalar_tensor_tensor(scf, scf, HD ** -0.5, bf, M, A_))
            done(dve.tensor_tensor(sc[:], sc[:], newb[:, 1].unsqueeze(2).to_broadcast([P, NBS, NPG, NF]), A_))
            done(dve.tensor_reduce(mx[:, 0:BH].rearrange("p (b h) -> p b h", h=NF), sc[:].rearrange("p b n h -> p b h n"), AX.X, ALU.max))
            dve.wait_ge(m_in, 32)
            for t in range(NMT):
                done(dve.tensor_tensor(prod[:, :, 0:WM], mk[:, :, t, :], mq[:], M))
                done(dve.tensor_reduce(ms[:, :, t, :], prod[:, :, 0:WM].rearrange("p b (h d) -> p b h d", d=HD), AX.X, A_))
            done(dve.tensor_reduce(mx[:, BH:].rearrange("p (b h) -> p b h", h=NM), ms[:].rearrange("p b t h -> p b h t"), AX.X, ALU.max))
            assert n[0] == MAX_AT, n[0]
            dve.wait_ge(pool_, 1)
            m3 = mxa[:, 0:BH].rearrange("p (b h) -> p b h", h=NF)
            mm3 = mxa[:, BH:].rearrange("p (b h) -> p b h", h=NM)
            done(dve.tensor_tensor(m3, m3, newb[:, 0], ALU.max))
            done(dve.tensor_tensor(sc[:], sc[:], m3.unsqueeze(2).to_broadcast([P, NBS, NPG, NF]), S_))
            done(dve.tensor_tensor(ms[:], ms[:], mm3.unsqueeze(2).to_broadcast([P, NBS, NMT, NM]), S_))
            done(dve.tensor_tensor(pn[:], newb[:, 0], m3, S_))
            assert n[0] == EXP_AT, n[0]
            dve.wait_ge(act_, 4)
            done(dve.tensor_reduce(part[:, 0:BH].rearrange("p (b h) -> p b h", h=NF), sc[:].rearrange("p b n h -> p b h n"), AX.X, A_))
            done(dve.tensor_reduce(part[:, BH:].rearrange("p (b h) -> p b h", h=NM), ms[:].rearrange("p b t h -> p b h t"), AX.X, A_))
            done(dve.tensor_copy(zt[:, 0:3], c.bank[0][:, 0:3 * NBS].rearrange("p (k b) -> p k b", b=NBS)))
            assert n[0] == SUM_AT
            dve.wait_ge(pe_, 4)
            r3, q3 = rt[:, 0:BH].rearrange("p (b h) -> p b h", h=NF), rt[:, BH:].rearrange("p (b h) -> p b h", h=NM)
            done(dve.tensor_tensor(rt[:, 0:BH], c.bank[3][:, 0:BH], pn[:].rearrange("p b h -> p (b h)"), A_))
            done(dve.tensor_copy(rt[:, BH:], c.bank[3][:, BH:BH + BM]))
            done(dve.reciprocal(rt[:], rt[:]))
            done(dve.tensor_tensor(sc[:], sc[:], r3.unsqueeze(2).to_broadcast([P, NBS, NPG, NF]), M))
            done(dve.tensor_tensor(ms[:], ms[:], q3.unsqueeze(2).to_broadcast([P, NBS, NMT, NM]), M))
            assert n[0] == NORM_AT
            done(dve.tensor_tensor(pn[:], pn[:], r3, M))
            for r in range(2):
                rows = slice(HD * r, HD * (r + 1))
                done(dve.tensor_tensor(t0[rows], zt[rows, 0:3], pn[rows].rearrange("p b (k r) -> p r k b", r=2)[:, r], M))
            with dve.Fori(0, NBS // 2) as i:
                for j in range(2):
                    b = 2 * i + j
                    dve.wait_ge(ov, at(2, i, j + 1))
                    o2 = c.bank[4 + j][:, 0:NF].rearrange("p (k r) -> p k r", r=2)
                    for r in range(2):
                        rows = slice(HD * r, HD * (r + 1))
                        dve.tensor_copy(of[rows, :, b], o2[rows, :, r]).then_inc(o_out, 1)
            dve.wait_ge(o_out, 4 + 2 * NBS)
            done(dve.tensor_tensor(of[:], of[:], t0[:], A_))
            done(dve.tensor_tensor(c.mix_s[:, 0:3], of[:], zg[:, 0:3], M))
            dve.wait_ge(pe_, 5)
            om = c.bank[6][:, 0:NBS * NM].rearrange("p (b k r) -> p k b r", r=2, k=2)
            for r in range(2):
                rows = slice(HD * r, HD * (r + 1))
                done(dve.tensor_tensor(c.mix_s[rows, 6:8], om[rows, :, :, r], zg[rows, 6:8], M))
            done(dve.tensor_copy(c.mix_s[:, 3:6], zg[:, 3:6]))

        @block.tensor
        def _(pe):
            pe.sem_inc(ov, 2)
            pe.sem_inc(o_out, 4)
            pe.wait_ge(loaded, LOADS)
            cols = [CV + k * P for k in range(3)] + [CGA + k * P for k in range(3)] + [CGS + k * P for k in range(3)] + \
                   [CGM + k * P for k in range(2)]
            for k, c0 in enumerate(cols):
                tr = pe.transpose(c.bank[0][:, k * NBS:(k + 1) * NBS], z[:, c0:c0 + P], c.ident[0:NBS, 0:NBS])
            tr.then_inc(pe_, 1)
            pe.wait_ge(step, NEWD_AT)
            pe.matmul(c.bank[1][:, 0:2 * BH], c.ones[0:NBS, :], newd[:].rearrange("q k b h -> q (k b h)"), start=True, stop=True
                      ).then_inc(pe_, 1)
            pe.wait_ge(step, LFX_AT)
            bf = c.bank[2][:, 0:NBS * NPG * NF]
            pe.matmul(bf, c.lower_strict[:], lf[:].rearrange("p b n h -> p (b n h)"), start=True, stop=False)
            pe.matmul(bf, c.ones[:], lfx[:].rearrange("p b n h -> p (b n h)"), start=False, stop=True).then_inc(pe_, 1)
            pe.wait_ge(step, SUM_AT)
            pe.matmul(c.bank[3][:, 0:BH + BM], c.ones[:], part[:], start=True, stop=True).then_inc(pe_, 1)
            pe.wait_ge(step, NORM_AT)
            for b in range(NBS):
                for k in range(2):
                    dst = c.bank[6][:, b * NM + 2 * k:b * NM + 2 * k + 2]
                    for t in range(NMT):
                        mm = pe.matmul(dst, mv[:, b, t, k * P:(k + 1) * P], ms[:, b, t, 2 * k:2 * k + 2], start=(t == 0), stop=(t == NMT - 1))
            mm.then_inc(pe_, 1)
            with pe.Fori(0, NBS // 2) as i:
                for j in range(2):
                    b = 2 * i + j
                    pe.wait_ge(v_in[j], 16 * NPG * (i + 1))
                    pe.wait_ge(o_out, at(4, i, 2 * (j - 1)))
                    for k in range(3):
                        for g in range(NPG):
                            mm = pe.matmul(c.bank[4 + j][:, 2 * k:2 * k + 2], vb[:, j, g, k * P:(k + 1) * P],
                                           sc[:, b, g, 2 * k:2 * k + 2], start=(g == 0), stop=(g == NPG - 1))
                    mm.then_inc(ov, 1)


def mix_out(nc, c, a, y_prompt, y_sample):
    NB, TB = T // 512, 512
    NT = TB // P
    NKS = WS // P
    with ExitStack() as s:
        def sb(name, shape, dt=F32):
            return s.enter_context(nc.sbuf_tensor(name, shape, dt))

        def sem(name):
            return s.enter_context(nc.semaphore(name))

        whi, wlo = sb("wo_hi", [P, KD, D], F32R), sb("wo_lo", [P, KD, D], F32R)
        wraw = sb("wo_raw", [P, 2, D])
        wg = sb("w_glu", [P, NKS, WS])
        bg = sb("b_glu", [P, NKS])
        gf = sb("g_fin", [P, D])
        am = sb("mx_am", [P, 5, TB])
        gate = sb("mx_gate", [P, NKS, TB])
        yc = sb("mx_y", [HD, STEP, WS])
        st = sb("mx_st", [P, NKS, TB])
        sig = sb("mx_sig", [P, NKS, TB])
        mhi, mlo = sb("mx_hi", [P, 2, KD, TB], F32R), sb("mx_lo", [P, 2, KD, TB], F32R)
        xr = sb("mx_x", [P, 2, D])
        xo = sb("mx_xo", [P, 2, D])
        ss, rin, rstd = sb("mx_ss", [P, 2]), sb("mx_rin", [P, 2]), sb("mx_rstd", [P, 2])
        junk = sb("mx_junk", [P, D], BF16)
        yss = sb("mx_ys", [P, NKS, 8])
        sgs = sb("mx_sgs", [P, NKS, 8])
        shi, slo = mhi[:, 0, :, 0:8], mlo[:, 0, :, 0:8]
        xs = wraw[0:8, 0]
        w_in = [sem("wo_in0"), sem("wo_in1")]
        p_in, xs_in, w_hi, w_split = sem("mx_p_in"), sem("mx_xs_in"), sem("wo_hi_d"), sem("wo_split")
        step, spe, sact, spool = sem("mx_step"), sem("mx_spe"), sem("mx_sact"), sem("mx_spool")
        in_ = sem("mx_in")
        tr_done, st_done, glu_done, sig_done = sem("mx_tr"), sem("mx_st_d"), sem("mx_glu"), sem("mx_sig_d")
        s_done, hi_done, lo_done = sem("mx_s_d"), sem("mx_hi_d"), sem("mx_lo_d")
        x_in = [sem("mx_x0"), sem("mx_x1")]
        y_st = [sem("mx_y0"), sem("mx_y1")]
        op_done, xo_done, sq_done, mean_done, rs_done, y_done = (
            sem(n) for n in ("mx_op", "mx_xo_d", "mx_sq", "mx_mean", "mx_rs", "mx_y_d"))
        block = s.enter_context(nc.Block())
        wo = a["w_out"].rearrange("o (k p) n -> (o k) p n", p=P)
        m_v = c.mix_t.rearrange("(k p) (b t) -> b p k t", p=P, t=TB)
        g_v = c.gate_t.rearrange("(k p) (b t) -> b p k t", p=P, t=TB)
        y_v = c.y_chunks.rearrange("b (a p) t f -> (b a) p t f", p=HD)
        x_v = a["x_prompt"].rearrange("o (b t p) d -> (o b) t p d", p=P, t=NT)
        o_v = y_prompt.rearrange("o (b t p) d -> (o b) t p d", p=P, t=NT)
        M, A_, S_ = ALU.mult, ALU.add, ALU.subtract

        def schedule(engine, ready, project):
            ready(0, 0)
            with engine.Fori(0, NB // 2 - 1) as i:
                ready(2 * i + 1, 1)
                project(2 * i, 0)
                ready(2 * i + 2, 0)
                project(2 * i + 1, 1)
            ready(NB - 1, 1)
            project(NB - 2, 0)
            project(NB - 1, 1)

        GATED_AT, SPLIT_AT, MEAN_AT, LAST_AT = 6, 8, 12, 14

        @block.sync
        def _(sp):
            with nc.allow_non_contiguous_dma(reason="384 biases"):
                sp.dma_start(bg[:], a["b_glu"].rearrange("o (k p) -> p (o k)", p=P)).then_inc(p_in, 16)
            sp.dma_start(wg[:], a["w_glu"].rearrange("o (k p) n -> p (o k) n", p=P)).then_inc(p_in, 16)
            sp.dma_start(gf[:], a["g_final"].partition_broadcast(P)).then_inc(p_in, 16)
            sp.dma_start(yss[:], c.ys_t.rearrange("(k p) b -> p k b", p=P)).then_inc(p_in, 16)
            for k in range(KD):
                if k >= 2:
                    sp.wait_ge(w_split, k - 1)
                sp.dma_start(wraw[:, k % 2], wo[k]).then_inc(w_in[k % 2], 16)
            sp.wait_ge(w_split, KD)
            sp.dma_start(xs, a["x_sample"].rearrange("b o d -> (b o) d")).then_inc(xs_in, 16)

            def ready(n, j):
                sp.wait_ge(lo_done, at(KD, n, 0))
                sp.dma_start(am[:, 0:3], m_v[n, :, 0:3, :]).then_inc(in_, 16)
                sp.dma_start(am[:, 3:5], m_v[n, :, 6:8, :]).then_inc(in_, 16)
                sp.dma_start(gate[:], g_v[n, :, 3:6, :]).then_inc(in_, 16)
                sp.dma_start(yc[:], y_v[n]).then_inc(in_, 16)

            def project(n, j):
                for t in range(NT):
                    sp.wait_ge(xo_done, at(NT, n, t - 1))
                    sp.dma_start(xr[:, t % 2], x_v[n, t]).then_inc(x_in[t % 2], 16)

            schedule(sp, ready, project)

        @block.gpsimd
        def _(pool):
            pool.wait_ge(step, MEAN_AT)
            pool.tensor_tensor(rstd[0:8, 0:1], rin[0:8, 0:1], c.minus_half[0:8, 0:1], ALU.pow).then_inc(spool, 1)
            with pool.Fori(0, NB) as n:
                for t in range(NT):
                    pool.wait_ge(mean_done, NT * n + t + 1)
                    pool.tensor_tensor(rstd[:, t % 2:t % 2 + 1], rin[:, t % 2:t % 2 + 1], c.minus_half[:, 0:1], ALU.pow
                                       ).then_inc(rs_done, 1)


        @block.vector
        def _(dve):
            n_ = [0]

            def done(ins):
                n_[0] += 1
                ins.then_inc(step, 1)
                dve.wait_ge(step, n_[0])

            dve.sem_inc(lo_done, KD)
            dve.sem_inc(xo_done, NT)
            for k in range(KD):
                dve.wait_ge(w_in[k % 2], 16 * (k // 2 + 1))
                dve.tensor_copy(whi[:, k, :], wraw[:, k % 2]).then_inc(w_hi, 1)
                dve.wait_ge(w_hi, k + 1)
                dve.tensor_tensor(wlo[:, k, :], wraw[:, k % 2], whi[:, k, :].bitcast(F32), S_).then_inc(w_split, 1)
            dve.wait_ge(p_in, 64)
            dve.wait_ge(sact, NKS)
            for k in range(NKS):
                done(dve.tensor_tensor(sgs[:, k], sgs[:, k], yss[:, k], M))
                done(dve.tensor_tensor(c.mix_s[:, 3 + k], c.mix_s[:, 3 + k], sgs[:, k], M))
            assert n_[0] == GATED_AT
            done(dve.tensor_copy(shi, c.mix_s[:]))
            done(dve.tensor_tensor(slo, c.mix_s[:], shi.bitcast(F32), S_))
            assert n_[0] == SPLIT_AT
            dve.wait_ge(xs_in, 16)
            for h in range(2):
                dve.wait_ge(spe, NKS + 1 + h)
                done(dve.tensor_tensor(xs[:, 512 * h:512 * (h + 1)], xs[:, 512 * h:512 * (h + 1)], c.bank[4 + h][0:8, :], A_))
            done(dve.tensor_tensor_reduce(junk[0:8], xs, xs, 1.0, 0.0, M, A_, ss[0:8, 0:1]))
            done(dve.tensor_scalar(rin[0:8, 0:1], ss[0:8, 0:1], 1.0 / D, EPS, M, A_))
            assert n_[0] == MEAN_AT
            dve.wait_ge(spool, 1)
            done(dve.scalar_tensor_tensor(xs, xs, rstd[0:8, 0:1], gf[0:8, :], M, M))
            done(dve.tensor_copy(junk[0:8, 0:8], xs[:, 0:8]))
            assert n_[0] == LAST_AT

            def ready(n, j):
                for k in range(NKS):
                    dve.wait_ge(sig_done, NKS * n + k + 1)
                    dve.tensor_tensor(sig[:, k], sig[:, k], st[:, k], M).then_inc(s_done, 1)
                    dve.wait_ge(s_done, 2 * NKS * n + 2 * k + 1)
                    dve.tensor_tensor(sig[:, k], sig[:, k], gate[:, k], M).then_inc(s_done, 1)
                for m in range(KD):
                    src = am[:, m] if m < 3 else (sig[:, m - 3] if m < 6 else am[:, m - 3])
                    dve.wait_ge(hi_done, at(KD, n, m + 1))
                    dve.tensor_tensor(mlo[:, j, m], src, mhi[:, j, m].bitcast(F32), S_).then_inc(lo_done, 1)

            def project(n, j):
                def finish(t):
                    q = t % 2
                    dve.wait_ge(sq_done, NT * n + t + 1)
                    dve.tensor_scalar(rin[:, q:q + 1], ss[:, q:q + 1], 1.0 / D, EPS, M, A_).then_inc(mean_done, 1)
                    dve.wait_ge(rs_done, NT * n + t + 1)
                    dve.scalar_tensor_tensor(xo[:, q], xo[:, q], rstd[:, q:q + 1], gf[:], M, M).then_inc(y_done, 1)

                for t in range(NT):
                    q = t % 2
                    dve.wait_ge(x_in[q], 16 * (NT // 2) * n + 16 * (t // 2 + 1))
                    dve.wait_ge(y_st[q], at(16 * NT // 2, n, 16 * (t // 2)))
                    for h in range(2):
                        dve.wait_ge(op_done, 2 * NT * n + 2 * t + h + 1)
                        ins = dve.tensor_tensor(xo[:, q, 512 * h:512 * (h + 1)], xr[:, q, 512 * h:512 * (h + 1)],
                                                c.bank[4 + 2 * q + h][:], A_)
                    ins.then_inc(xo_done, 1)
                    if t:
                        finish(t - 1)
                finish(NT - 1)

            schedule(dve, ready, project)

        @block.scalar
        def _(act):
            for j in range(2):
                act.sem_inc(y_st[j], 16 * NT // 2)
            act.sem_inc(hi_done, KD)
            act.wait_ge(p_in, 64)
            for e in range(NKS):
                act.wait_ge(spe, e + 1)
                act.activation(sgs[:, e], c.bank[e][:, 0:8], ACT.Sigmoid, bias=bg[:, e:e + 1]).then_inc(sact, 1)
            act.wait_ge(step, LAST_AT)
            act.dma_start(y_sample.rearrange("b o d -> (b o) d"), xs).then_inc(sact, 16)

            def ready(n, j):
                act.wait_ge(in_, 64 * n + 64)
                for k in range(NKS):
                    act.wait_ge(tr_done, NKS * n + k + 1)
                    act.activation(st[:, k].rearrange("p (c t) -> p t c", t=STEP), c.bank[k % 2][:].rearrange("p (t c) -> p t c", t=STEP),
                                   ACT.Copy).then_inc(st_done, 1)
                for k in range(NKS):
                    act.wait_ge(glu_done, NKS * n + k + 1)
                    act.activation(sig[:, k], c.bank[2 + k % 2][:], ACT.Sigmoid, bias=bg[:, k:k + 1]).then_inc(sig_done, 1)
                for m in range(KD):
                    src = am[:, m] if m < 3 else (sig[:, m - 3] if m < 6 else am[:, m - 3])
                    if 3 <= m < 6:
                        act.wait_ge(s_done, 2 * NKS * n + 2 * (m - 3) + 2)
                    act.activation(mhi[:, j, m], src, ACT.Copy).then_inc(hi_done, 1)

            def project(n, j):
                def store(t):
                    act.wait_ge(y_done, NT * n + t + 1)
                    act.dma_start(o_v[n, t], xo[:, t % 2]).then_inc(y_st[t % 2], 16)

                for t in range(NT):
                    q = t % 2
                    act.wait_ge(xo_done, at(NT, n, t + 1))
                    act.wait_ge(sq_done, NT * n + t)
                    act.activation(junk[:], xo[:, q], ACT.Square, accum_out=ss[:, q:q + 1]).then_inc(sq_done, 1)
                    if t:
                        store(t - 1)
                store(NT - 1)

            schedule(act, ready, project)
            for j in range(2):
                act.wait_ge(y_st[j], at(16 * NT // 2, NB, 0))
            act.wait_ge(sact, NKS + 16)

        @block.tensor
        def _(pe):
            pe.wait_ge(p_in, 64)
            for e in range(NKS):
                for k in range(NKS):
                    mm = pe.matmul(c.bank[e][:, 0:8], wg[:, k, e * P:(e + 1) * P], yss[:, k, :], start=(k == 0), stop=(k == NKS - 1))
                mm.then_inc(spe, 1)
            pe.wait_ge(w_split, KD)
            pe.wait_ge(step, SPLIT_AT)
            for h in range(2):
                for k in range(KD):
                    for ms_, ws_ in ((shi, whi), (slo, whi), (shi, wlo)):
                        mm = pe.matmul(c.bank[4 + h][0:8, :], ms_[:, k, :], ws_[:, k, 512 * h:512 * (h + 1)],
                                       start=(k == 0 and ws_ is whi and ms_ is shi), stop=(k == KD - 1 and ws_ is wlo))
                mm.then_inc(spe, 1)
            pe.wait_ge(step, LAST_AT)

            def ready(n, j):
                pe.wait_ge(in_, 64 * n + 64)
                for k in range(NKS):
                    if k == 0:
                        pe.wait_ge(lo_done, at(KD, n, 0))
                    elif k == 2:
                        pe.wait_ge(st_done, NKS * n + 1)
                    for t in range(STEP):
                        tr = pe.matmul(c.bank[k % 2][:, t * HD:(t + 1) * HD], yc[:, t, k * P:(k + 1) * P], c.ident[0:HD, 0:HD],
                                       start=True, stop=True)
                    tr.then_inc(tr_done, 1)
                pe.wait_ge(st_done, NKS * n + NKS)
                for e in range(NKS):
                    if e == 2:
                        pe.wait_ge(sig_done, NKS * n + 1)
                    for k in range(NKS):
                        mm = pe.matmul(c.bank[2 + e % 2][:], wg[:, k, e * P:(e + 1) * P], st[:, k], start=(k == 0), stop=(k == NKS - 1))
                    mm.then_inc(glu_done, 1)

            def project(n, j):
                pe.wait_ge(lo_done, at(KD, n, KD))
                for t in range(NT):
                    pe.wait_ge(xo_done, at(NT, n, t - 1))
                    for h in range(2):
                        for k in range(KD):
                            for ms_, ws_ in ((mhi, whi), (mlo, whi), (mhi, wlo)):
                                mm = pe.matmul(c.bank[4 + 2 * (t % 2) + h][:], ms_[:, j, k, t * P:(t + 1) * P],
                                               ws_[:, k, 512 * h:512 * (h + 1)], start=(k == 0 and ws_ is whi and ms_ is mhi),
                                               stop=(k == KD - 1 and ws_ is wlo))
                        mm.then_inc(op_done, 1)

            schedule(pe, ready, project)




def build(nc, a, o):
    c = Core()

    def scratch(name, shape):
        return nc.dram_tensor(name, shape, F32).ap()

    c.q_t = scratch("q_t", (WF, T))
    c.qm_t = scratch("qm_t", (WM, T))
    c.gate_t = scratch("gate_t", (D, T))
    c.mix_t = scratch("mix_t", (D, T))
    c.u_chunks = scratch("u_chunks", (4, P, G * 8 * GC))
    c.y_chunks = scratch("y_chunks", (4, P, 8, WS))
    c.negc_rows = scratch("negc_rows", (NF, T))
    c.ssm_gp = scratch("ssm_consts", (G, P, GPW))
    c.zs = scratch("z_sample", (8, DIN))
    c.ys_t = scratch("ys_t", (WS, 8))
    with ExitStack() as s:
        def sb(name, shape, dt=F32):
            return s.enter_context(nc.sbuf_tensor(name, shape, dt))

        c.ident, c.identb = sb("ident", [P, P]), sb("identb", [P, P], BF16)
        c.upper, c.lower_strict = sb("upper", [P, P]), sb("lower_strict", [P, P])
        c.mask_kq, c.mask_qk = sb("mask_kq", [P, P], BF16), sb("mask_qk", [P, P], BF16)
        c.ones = sb("ones", [P, P])
        c.minus_half = sb("minus_half", [P, 8])
        c.flogit = sb("flogit", [P, T // P, NF])
        c.negc = sb("negc", [P, NF, T // P])
        c.lfs = sb("lf_sample", [8, NF])
        c.mix_s = sb("mix_s", [P, KD, 8])
        c.bank = [s.enter_context(nc.psum_tensor(f"bank{i}", [P, 512], F32)) for i in range(8)]
        setup_constants(nc, c)
        project_prompt(nc, c, a["x_prompt"], a["w_in"], a["g_norm"], o["k_prompt"], o["v_prompt"])
        forget_gates(nc, c, a["b_f"], o["logf_prompt"])
        fox_prompt(nc, c, o["k_prompt"], o["v_prompt"])
        memory_prompt(nc, c, a["mem_prompt"], a["g_mem"], a["w_mem_kv"], o["memk_prompt"], o["memv_prompt"])
        sample_project(nc, c, a, o)
        ssm_constants(nc, c, a)
        ssm(nc, c, a, o["ssm_prompt"], o["ssm_sample"])
        sample_attend(nc, c, a)
        mix_out(nc, c, a, o["y_prompt"], o["y_sample"])



INS = ["x_prompt", "x_sample", "mem_prompt", "cache_k", "cache_v", "cache_logf", "state_ssm", "cache_mem_k",
       "cache_mem_v", "page_table", "g_norm", "w_in", "b_f", "lam_re", "lam_im", "log_dt", "b_re", "b_im",
       "c_re", "c_im", "d_skip", "w_glu", "b_glu", "g_mem", "w_mem_kv", "w_out", "g_final"]
OUTS = [("y_prompt", (1, T, D)), ("y_sample", (8, 1, D)),
        ("k_prompt", (1, 1, T, NF, HD)), ("v_prompt", (1, 1, T, NF, HD)), ("logf_prompt", (1, 1, T, NF)),
        ("ssm_prompt", (1, 1, G, NS, 2)), ("memk_prompt", (1, 1, NMEM, NM, HD)),
        ("memv_prompt", (1, 1, NMEM, NM, HD)), ("k_sample", (1, 8, 1, NF, HD)),
        ("v_sample", (1, 8, 1, NF, HD)), ("logf_sample", (1, 8, 1, NF)), ("ssm_sample", (1, 8, G, NS, 2))]


def kernel(**inputs):
    import numpy as np
    import concourse.bacc as bacc
    from concourse.bass_utils import run_bass_kernel_spmd

    nc = bacc.Bacc("TRN2", target_bir_lowering=False, num_devices=1)
    arrays, a, o = {}, {}, {}
    for name in INS:
        x = np.ascontiguousarray(inputs[name])
        arrays[f"in_{name}"] = x
        a[name] = nc.dram_tensor(f"in_{name}", x.shape, mybir.dt.from_np(x.dtype), kind="ExternalInput").ap()
    for name, shape in OUTS:
        o[name] = nc.dram_tensor(f"out_{name}", shape, F32, kind="ExternalOutput").ap()
    build(nc, a, o)
    r = run_bass_kernel_spmd(nc, [arrays], core_ids=[0])
    return tuple(r.results[0][f"out_{name}"] for name, _ in OUTS)
```

```python
from contextlib import ExitStack

import concourse.bass as bass
from concourse import mybir

F32 = mybir.dt.float32
F32R = mybir.dt.float32r
BF16 = mybir.dt.bfloat16
I32 = mybir.dt.int32
I64 = mybir.dt.int64
ALU = mybir.AluOpType
ACT = mybir.ActivationFunctionType
AX = mybir.AxisListType

P = 128
D = 1024
T = 4096
HD = 64
NF, WF = 6, 384
G, GC, NS, WS = 24, 16, 64, 384
NM, WM, NMEM = 4, 256, 256
KD = D // P
EPS = 1e-6
CQ, CK, CV, CF = 0, WF, 2 * WF, 3 * WF
CGA = CF + NF
CU = CGA + WF
CGS = CU + WS
CQM = CGS + WS
CGM = CQM + WM
DIN = CGM + WM
NEG = -1e30


def at(per, i, n):
    return per * (i + 1) + n


class Core:
    pass


def setup_constants(nc, c):
    with ExitStack() as s:
        filled = s.enter_context(nc.semaphore("const_filled"))
        made = s.enter_context(nc.semaphore("const_made"))
        block = s.enter_context(nc.Block())

        @block.gpsimd
        def _(pool):
            fills = [(c.ident, 0.0), (c.identb, 0.0), (c.upper, 1.0), (c.lower_strict, 1.0),
                     (c.mask_kq, 0.0), (c.mask_qk, 0.0), (c.ones, 1.0), (c.minus_half, -0.5)]
            for t, v in fills:
                pool.memset(t[:], v).then_inc(filled, 1)
            pool.wait_ge(filled, len(fills))
            for t in (c.ident, c.identb):
                pool.affine_select(out=t[:], in_=t[:], pattern=[[-1, P]], compare_op=ALU.not_equal,
                                   fill=1.0, base=0, channel_multiplier=1).then_inc(made, 1)
            pool.affine_select(out=c.upper[:], in_=c.upper[:], pattern=[[1, P]], compare_op=ALU.is_ge,
                               fill=0.0, base=0, channel_multiplier=-1).then_inc(made, 1)
            pool.affine_select(out=c.lower_strict[:], in_=c.lower_strict[:], pattern=[[-1, P]],
                               compare_op=ALU.is_gt, fill=0.0, base=0, channel_multiplier=1).then_inc(made, 1)
            pool.affine_select(out=c.mask_kq[:], in_=c.mask_kq[:], pattern=[[1, P]], compare_op=ALU.is_ge,
                               fill=NEG, base=0, channel_multiplier=-1).then_inc(made, 1)
            pool.affine_select(out=c.mask_qk[:], in_=c.mask_qk[:], pattern=[[-1, P]], compare_op=ALU.is_ge,
                               fill=NEG, base=0, channel_multiplier=1).then_inc(made, 1)
            pool.wait_ge(made, 6)


STEP = 8
NCH = T // STEP
SC = STEP * GC
O_COS, O_SIN = 0, NCH
O_R = 2 * NCH
O_W1 = O_R + (2 * STEP - 1) * GC
O_W2 = O_W1 + SC
O_CC = O_W2 + SC
O_D = O_CC + GC
O_R8, O_A1, O_B1 = O_D + 1, O_D + 2, O_D + 3
GPW = O_B1 + 1
TWO_PI = 6.283185307179586
PI1 = 6.28125
PI2 = 0.0019350051879882812
PI3 = 3.0199159819567e-07
ROUND = 12582912.0


class SsmConstants:

    NGB = 4
    SCALAR_LOADS, TABLE_LOADS = 16 * 5, 16 * (4 + 4 + STEP)
    ARG_AT, REDUCED_AT = 1, 8

    def __init__(self, nc, s):
        def sb(name, shape, dt=F32):
            return s.enter_context(nc.sbuf_tensor(name, shape, dt))

        self.sb = sb
        self.v = {n: sb("v_" + n, [P, G]) for n in ("mag", "r8", "cs", "sn", "lr", "li", "den", "fr", "fi", "fi2", "nr", "t1", "t2")}
        self.lre, self.lim = sb("lre", [P, G]), sb("lim", [P, G])
        self.ar, self.ai, self.nai = sb("ar", [P, G, 9]), sb("ai", [P, G, 9]), sb("nai", [P, G, 9])
        self.uc, self.us = sb("uc", [P, G, 12]), sb("us", [P, G, 12])
        self.sgn = sb("sgn", [P, 2])
        self.loaded, self.step, self.acted, self.signs = (
            nc.alloc_semaphore(n) for n in ("sp_loaded", "sp_step", "sp_act", "sp_signs"))
        self.b_in, self.turned, self.c_out, self.made, self.stored = (
            nc.alloc_semaphore(n) for n in ("st_in", "st_pe", "st_c", "st_made", "st_stored"))


    def place_scalars(self, s, nc):
        def sb(name):
            return s.enter_context(nc.sbuf_tensor(name, [P, G], F32))
        self.ldt = sb("ldt")
        self.t = {n: sb("v_" + n) for n in ("dt", "a", "th", "t3", "sh")}

    def load_scalars(self, nc, sp, a):
        with nc.allow_non_contiguous_dma(reason="parameters, states on rows"):
            for r in (0, HD):
                sp.dma_start(self.lre[r:r + HD, :], a["lam_re"].rearrange("o g p -> p (o g)")).then_inc(self.loaded, 16)
                sp.dma_start(self.lim[r:r + HD, :], a["lam_im"].rearrange("o g p -> p (o g)")).then_inc(self.loaded, 16)
            sp.dma_start(self.ldt[:], a["log_dt"][0].partition_broadcast(P)).then_inc(self.loaded, 16)

    def set_signs(self, pool):
        pool.memset(self.sgn[0:HD, 0:1], 1.0).then_inc(self.signs, 1)
        pool.memset(self.sgn[HD:P, 0:1], -1.0).then_inc(self.signs, 1)
        pool.wait_ge(self.signs, 2)
        pool.memset(self.sgn[0:HD, 1:2], -1.0).then_inc(self.signs, 1)
        pool.memset(self.sgn[HD:P, 1:2], 1.0).then_inc(self.signs, 1)
        pool.wait_ge(self.signs, 4)

    def scalar_functions(self, act):
        v, t = self.v, self.t
        act.wait_ge(self.loaded, self.SCALAR_LOADS)
        act.activation(t["dt"][:], self.ldt[:], ACT.Exp).then_inc(self.acted, 1)
        act.wait_ge(self.step, self.ARG_AT)
        act.activation(v["mag"][:], t["a"][:], ACT.Exp).then_inc(self.acted, 1)
        act.activation(v["r8"][:], t["a"][:], ACT.Exp, scale=float(STEP)).then_inc(self.acted, 1)
        act.wait_ge(self.step, self.REDUCED_AT)
        act.activation(v["sn"][:], v["t2"][:], ACT.Sin).then_inc(self.acted, 1)
        act.activation(t["sh"][:], v["t2"][:], ACT.Sin, scale=0.5).then_inc(self.acted, 1)

    def scalars(self, dve):
        n = [0]

        def done(ins):
            n[0] += 1
            ins.then_inc(self.step, 1)
            dve.wait_ge(self.step, n[0])

        def tt(out, x, y, op):
            done(dve.tensor_tensor(out, x, y, op))

        def ts(out, x, y, op, y2=None, op2=ALU.bypass):
            done(dve.tensor_scalar(out, x, y, y2, op, op2))

        M, A_, S_ = ALU.mult, ALU.add, ALU.subtract
        w = {k: t[:] for k, t in {**self.v, **self.t}.items()}
        lre, lim = self.lre[:], self.lim[:]
        dve.wait_ge(self.loaded, self.SCALAR_LOADS)
        dve.wait_ge(self.acted, 1)
        tt(w["a"], lre, w["dt"], M)
        assert n[0] == self.ARG_AT
        tt(w["th"], lim, w["dt"], M)
        ts(w["t1"], w["th"], 1.0 / TWO_PI, M)
        ts(w["t1"], w["t1"], ROUND, A_, -ROUND, A_)
        done(dve.scalar_tensor_tensor(w["t2"], w["t1"], -PI1, w["th"], M, A_))
        done(dve.scalar_tensor_tensor(w["t3"], w["t1"], -PI2, w["t2"], M, A_))
        done(dve.scalar_tensor_tensor(w["den"], w["t1"], -PI3, w["t3"], M, A_))
        ts(w["t2"], w["den"], 3.1415925, ALU.min, -3.1415925, ALU.max)
        assert n[0] == self.REDUCED_AT
        dve.wait_ge(self.acted, 5)
        tt(w["t1"], w["sh"], w["sh"], M)
        ts(w["cs"], w["t1"], -2.0, M, 1.0, A_)
        tt(w["lr"], w["mag"], w["cs"], M)
        tt(w["li"], w["mag"], w["sn"], M)
        tt(w["t1"], lre, lre, M)
        tt(w["t2"], lim, lim, M)
        tt(w["t1"], w["t1"], w["t2"], A_)
        done(dve.reciprocal(w["den"], w["t1"]))


    def place_tables(self, s, nc):
        def sb(name, shape):
            return s.enter_context(nc.sbuf_tensor(name, shape, F32))
        self.gp = sb("gp", [P, self.NGB, GPW])
        self.b1, self.b2 = sb("b_ri", [P, G, GC]), sb("b_ir", [P, G, GC])
        self.cin = sb("c_in", [P, 3, 2, 2, NS])
        self.cd, self.ce = sb("c_ri", [P, G, GC]), sb("c_ir", [P, G, GC])
        self.bb1, self.bb2 = sb("bb_ri", [P, G, GC]), sb("bb_ir", [P, G, GC])
        self.big = sb("st_big", [P, self.NGB, 256])
        self.dcol = sb("dcol", [P, G])

    def load_tables(self, nc, sp, a):
        with nc.allow_non_contiguous_dma(reason="parameters, states on rows"):
            for j, (x, y) in enumerate((("c_re", "c_im"), ("c_im", "c_re"))):
                for k, z in enumerate((x, y)):
                    sp.dma_start(self.cin[:, :, j, k, :], a[z].rearrange("o g c p -> (o g c) p").rearrange("(t q) p -> q t p", q=P)
                                 ).then_inc(self.b_in, 16)
            for r in (0, HD):
                x, y = ("b_re", "b_im") if r == 0 else ("b_im", "b_re")
                sp.dma_start(self.b1[r:r + HD], a[x].rearrange("o g p c -> p (o g) c")).then_inc(self.b_in, 16)
                sp.dma_start(self.b2[r:r + HD], a[y].rearrange("o g p c -> p (o g) c")).then_inc(self.b_in, 16)
            for t in range(STEP):
                sp.dma_start(self.dcol[t * GC:(t + 1) * GC, :], a["d_skip"].rearrange("o g c -> c (o g)")).then_inc(self.b_in, 16)

    def turn_c(self, pe, c):
        pe.wait_ge(self.b_in, self.TABLE_LOADS)
        for j in range(2):
            for t in range(3):
                tr = pe.transpose(c.bank[j][:, t * P:(t + 1) * P], self.cin[:, t, j, :, :].rearrange("q a p -> q (a p)"), c.ident[:])
            tr.then_inc(self.turned, 1)

    def copy_c(self, dve, c):
        dve.wait_ge(self.turned, 2)
        dve.tensor_copy(self.cd[:].rearrange("p g c -> p (g c)"), c.bank[0][:, 0:G * GC]).then_inc(self.c_out, 1)
        dve.tensor_copy(self.ce[:].rearrange("p g c -> p (g c)"), c.bank[1][:, 0:G * GC]).then_inc(self.c_out, 1)

    def tables(self, pool, c):
        n, m_ = [0], self.NGB

        def done(ins):
            n[0] += 1
            ins.then_inc(self.made, 1)
            pool.wait_ge(self.made, n[0])

        def tt(out, x, y, op):
            done(pool.tensor_tensor(out, x, y, op))

        M, A_, S_ = ALU.mult, ALU.add, ALU.subtract
        w = {k: t[:] for k, t in self.v.items()}
        ar, ai, nai, uc, us = self.ar, self.ai, self.nai, self.uc, self.us
        lre, lim = self.lre[:], self.lim[:]
        sg, ns = self.sgn[:, 0:1], self.sgn[:, 1:2]

        def ts(out, x, y, op, y2=None, op2=ALU.bypass):
            done(pool.tensor_scalar(out, x, y, y2, op, op2))

        ts(w["nr"], w["lr"], -1.0, A_)
        tt(w["t1"], w["nr"], lre, M)
        tt(w["t2"], w["li"], lim, M)
        tt(w["t1"], w["t1"], w["t2"], A_)
        tt(w["fr"], w["t1"], w["den"], M)
        tt(w["t1"], w["li"], lre, M)
        tt(w["t2"], w["nr"], lim, M)
        tt(w["t1"], w["t1"], w["t2"], S_)
        tt(w["t2"], w["t1"], w["den"], M)
        ts(w["fi"], w["t2"], ns, M)
        ts(w["fi2"], w["t2"], sg, M)
        done(pool.memset(ar[:, :, 0], 1.0))
        done(pool.memset(ai[:, :, 0], 0.0))
        for k in range(STEP):
            tt(ar[:, :, k + 1], ar[:, :, k], w["lr"], M)
            tt(w["t1"], ai[:, :, k], w["li"], M)
            tt(ar[:, :, k + 1], ar[:, :, k + 1], w["t1"], S_)
            tt(ai[:, :, k + 1], ar[:, :, k], w["li"], M)
            tt(w["t1"], ai[:, :, k], w["lr"], M)
            tt(ai[:, :, k + 1], ai[:, :, k + 1], w["t1"], A_)
        ts(nai[:], ai[:], ns, M)
        done(pool.tensor_copy(uc[:, :, 0], w["cs"]))
        done(pool.tensor_copy(us[:, :, 0], w["sn"]))
        for j in range(11):
            tt(w["t1"], us[:, :, j], us[:, :, j], M)
            tt(uc[:, :, j + 1], uc[:, :, j], uc[:, :, j], M)
            tt(uc[:, :, j + 1], uc[:, :, j + 1], w["t1"], S_)
            tt(w["t1"], uc[:, :, j], us[:, :, j], M)
            ts(us[:, :, j + 1], w["t1"], 2.0, M)
        bb1, bb2, cd, ce, big, gp = self.bb1, self.bb2, self.cd, self.ce, self.big, self.gp
        pool.wait_ge(self.b_in, self.TABLE_LOADS)
        bg = [P, G, GC]
        for out, x, y, f in ((bb1, self.b1, self.b2, "fi"), (bb2, self.b2, self.b1, "fi2")):
            tt(out[:], x[:], w["fr"].unsqueeze(2).to_broadcast(bg), M)
            tmp = gp[:, 0, 0:G * GC].rearrange("p (g c) -> p g c", c=GC)
            tt(tmp, y[:], w[f].unsqueeze(2).to_broadcast(bg), M)
            tt(out[:], out[:], tmp, A_)
        pool.wait_ge(self.c_out, 2)
        for g0 in range(0, G, m_):
            gs = slice(g0, g0 + m_)
            ar, ai, nai, uc, us = (x[:, gs] for x in (self.ar, self.ai, self.nai, self.uc, self.us))
            if g0:
                pool.wait_ge(self.stored, 16 * (g0 // m_))
            sc = [P, m_, GC]
            b16 = big[:, :, 0:GC]
            R = gp[:, :, O_R:O_W1].rearrange("p g (m c) -> p g m c", c=GC)
            done(pool.memset(R[:, :, STEP:], 0.0))
            for m in range(STEP):
                k = STEP - 1 - m
                tt(R[:, :, m, :], bb1[:, gs], ar[:, :, k:k + 1].to_broadcast(sc), M)
                tt(b16, bb2[:, gs], nai[:, :, k:k + 1].to_broadcast(sc), M)
                tt(R[:, :, m, :], R[:, :, m, :], b16, A_)
            done(pool.tensor_scalar(gp[:, :, O_CC:O_D], cd[:, gs], self.sgn[:, 0:1], None, M))
            for t in range(STEP):
                k = t + 1
                one, two = gp[:, :, O_W1 + t * GC:O_W1 + (t + 1) * GC], gp[:, :, O_W2 + t * GC:O_W2 + (t + 1) * GC]
                tt(one, gp[:, :, O_CC:O_D], ar[:, :, k:k + 1].to_broadcast(sc), M)
                tt(b16, ce[:, gs], ai[:, :, k:k + 1].to_broadcast(sc), M)
                tt(one, one, b16, S_)
                tt(two, cd[:, gs], nai[:, :, k:k + 1].to_broadcast(sc), M)
                tt(b16, ce[:, gs], ar[:, :, k:k + 1].to_broadcast(sc), M)
                tt(two, two, b16, S_)
            cosT, sinT = gp[:, :, O_COS:O_COS + NCH], gp[:, :, O_SIN:O_SIN + NCH]
            done(pool.memset(cosT[:, :, 0:1], 1.0))
            done(pool.memset(sinT[:, :, 0:1], 0.0))
            for j in range(9):
                m = 1 << j
                sh = [P, m_, m]
                cj, sj = uc[:, :, j + 3:j + 4].to_broadcast(sh), us[:, :, j + 3:j + 4].to_broadcast(sh)
                lo_c, lo_s, hi_c, hi_s = cosT[:, :, 0:m], sinT[:, :, 0:m], cosT[:, :, m:2 * m], sinT[:, :, m:2 * m]
                tt(hi_c, lo_c, cj, M)
                tt(big[:, :, 0:m], lo_s, sj, M)
                tt(hi_c, hi_c, big[:, :, 0:m], S_)
                tt(hi_s, lo_s, cj, M)
                tt(big[:, :, 0:m], lo_c, sj, M)
                tt(hi_s, hi_s, big[:, :, 0:m], A_)
            done(pool.tensor_copy(gp[:, :, O_D], self.dcol[:, gs]))
            done(pool.tensor_copy(gp[:, :, O_R8], self.v["r8"][:, gs]))
            done(pool.tensor_copy(gp[:, :, O_A1], self.v["lr"][:, gs]))
            done(pool.tensor_copy(gp[:, :, O_B1], nai[:, :, 1]))
            pool.dma_start(c.ssm_gp[gs].rearrange("g p w -> p g w"), gp[:]).then_inc(self.stored, 16)
        pool.wait_ge(self.stored, 16 * (G // m_))


def project_prompt(nc, c, x_prompt, w_in, g_norm, k_out, v_out, ssm_c, a):
    TB = 1024
    NTB = T // TB
    NT = TB // P
    SEGW = WF + NF
    SEGS = [("q", CQ, WF), ("k", CK, WF), ("v", CV, WF + NF), ("ga", CGA, WF), ("u", CU, WS),
            ("gs", CGS, WS), ("qm", CQM, WM), ("gm", CGM, WM)]
    outs = []
    for si, (name, c0, w) in enumerate(SEGS):
        if name in ("k", "v", "u"):
            outs += [(si, t, None) for t in range(NT)]
        else:
            outs += [(si, m, h) for m in range(w // P) for h in range(2)]
    NO = len(outs)
    seg_end = [max(n for n, o in enumerate(outs) if o[0] == si) + 1 for si in range(len(SEGS))]
    PB = 5
    assert NO % PB == 0
    NG = KD * 2
    dest = {"q": (c.q_t, 0, 0.125), "qm": (c.qm_t, 0, 0.125), "ga": (c.gate_t, 0, None),
            "gs": (c.gate_t, WF, None), "gm": (c.gate_t, WF + WS, None)}
    x_v = x_prompt.rearrange("o (b t p) d -> (o b) p t d", p=P, t=NT)
    w_v = w_in.rearrange("o (k p) n -> (o p) k n", p=P)
    k_v = k_out.rearrange("l o (b t p) h d -> (l o b) t p (h d)", p=P, t=NT)
    v_v = v_out.rearrange("l o (b t p) h d -> (l o b) t p (h d)", p=P, t=NT)

    with ExitStack() as s:
        def sb(name, shape, dt=F32):
            return s.enter_context(nc.sbuf_tensor(name, shape, dt))

        def sem(name):
            return s.enter_context(nc.semaphore(name))

        x = sb("x_tok", [P, NT, D])
        xhi, xlo = sb("xhi", [P, KD, TB], F32R), sb("xlo", [P, KD, TB], F32R)
        wraw = sb("wraw", [P, KD, SEGW])
        whi, wlo = sb("whi", [P, 2, KD, SEGW], F32R), sb("wlo", [P, 2, KD, SEGW], F32R)
        fstage = sb("fstage", [P, 2, TB])
        tstage = sb("tstage", [P, 4, WF])
        ustage = sb("ustage", [P, G, 8, GC])
        gn = sb("gn", [P, KD])
        junk = sb("sq_junk", [P, D], BF16)
        ss, rstd = sb("ss", [P, NT]), sb("rstd", [P, NT])
        rstd_in = sb("rstd_in", [P, NT])
        x_loaded, w_loaded, g_loaded = sem("x_loaded"), sem("w_loaded"), sem("g_loaded")
        sq_done, mean_done, rstd_done, xn_done = sem("sq_done"), sem("mean_done"), sem("rstd_done"), sem("xn_done")
        tr_done, hi_done, lo_done = sem("tr_done"), sem("hi_done"), sem("lo_done")
        whi_done, wlo_done, proj_done, evac_done = sem("whi_done"), sem("wlo_done"), sem("proj_done"), sem("evac_done")
        f_stored = [sem(f"f_stored{j}") for j in range(2)]
        t_stored = [sem(f"t_stored{j}") for j in range(4)]
        u_stored = sem("u_stored")
        ssm_c.place_scalars(s, nc)
        block = s.enter_context(nc.Block())
        NSEG = len(SEGS)
        NFM = sum(1 for si, m, h in outs if h == 1)
        fper = [16 * len([f for f in range(NFM) if f % 2 == j]) for j in range(2)]

        @block.sync
        def _(sp):
            with nc.allow_non_contiguous_dma(reason="1024 gains"):
                sp.dma_start(gn[:], g_norm.rearrange("o (k p) -> p (o k)", p=P)).then_inc(g_loaded, 16)
            with sp.Fori(0, NTB) as i:
                sp.wait_ge(lo_done, at(NG, i, 0))
                sp.dma_start(x[:], x_v[i]).then_inc(x_loaded, 16)
                for si, (_, c0, w) in enumerate(SEGS):
                    sp.wait_ge(wlo_done, at(NSEG, i, si))
                    sp.dma_start(wraw[:, :, 0:w], w_v[:, :, c0:c0 + w]).then_inc(w_loaded, 16)

        @block.gpsimd
        def _(pool):
            ssm_c.set_signs(pool)
            with pool.Fori(0, NTB) as i:
                pool.wait_ge(mean_done, i + 1)
                pool.tensor_tensor(rstd[:], rstd_in[:], c.minus_half[:, 0:NT], ALU.pow).then_inc(rstd_done, 1)

        @block.vector
        def _(dve):
            dve.sem_inc(lo_done, NG)
            dve.sem_inc(wlo_done, NSEG)
            dve.wait_ge(g_loaded, 16)
            ssm_c.scalars(dve)

            def split(i, si):
                w = SEGS[si][2]
                dve.wait_ge(w_loaded, 16 * (NSEG * i + si + 1))
                before = seg_end[si - 2] if si >= 2 else seg_end[si - 2] - NO
                dve.wait_ge(proj_done, at(NO, i, before))
                dve.tensor_copy(whi[:, si % 2, :, 0:w], wraw[:, :, 0:w]).then_inc(whi_done, 1)
                dve.wait_ge(whi_done, NSEG * i + si + 1)
                hi = whi[:, si % 2, :, 0:w]
                dve.tensor_tensor(wlo[:, si % 2, :, 0:w], wraw[:, :, 0:w], hi.bitcast(F32),
                                  ALU.subtract).then_inc(wlo_done, 1)

            with dve.Fori(0, NTB) as i:
                dve.wait_ge(x_loaded, 16 * (i + 1))
                for t in range(NT):
                    if t:
                        dve.wait_ge(sq_done, NT * i + t)
                    dve.tensor_tensor_reduce(junk[:], x[:, t, :], x[:, t, :], 1.0, 0.0, ALU.mult, ALU.add,
                                             ss[:, t:t + 1]).then_inc(sq_done, 1)
                dve.wait_ge(sq_done, NT * (i + 1))
                dve.tensor_scalar(rstd_in[:], ss[:], 1.0 / D, EPS, ALU.mult, ALU.add).then_inc(mean_done, 1)
                dve.wait_ge(rstd_done, i + 1)
                for t in range(NT):
                    dve.tensor_scalar(x[:, t, :], x[:, t, :], rstd[:, t:t + 1], None,
                                      ALU.mult).then_inc(xn_done, 1)
                split(i, 0)
                for g in range(NG):
                    k, h = g // 2, g % 2
                    dve.wait_ge(hi_done, NG * i + g + 1)
                    hi = xhi[:, k, 512 * h:512 * (h + 1)]
                    dve.scalar_tensor_tensor(xlo[:, k, 512 * h:512 * (h + 1)], c.bank[g % 2][:], gn[:, k:k + 1],
                                             hi.bitcast(F32), ALU.mult, ALU.subtract).then_inc(lo_done, 1)
                for si in range(1, NSEG):
                    split(i, si)

        @block.tensor
        def _(pe):
            pe.sem_inc(proj_done, NO)
            with pe.Fori(0, NTB) as i:
                pe.wait_ge(xn_done, NT * (i + 1))
                for g in range(NG):
                    k, h = g // 2, g % 2
                    pe.wait_ge(lo_done, at(NG, i, g - 1))
                    for t in range(4):
                        tr = pe.transpose(c.bank[g % 2][:, t * P:(t + 1) * P],
                                          x[:, 4 * h + t, k * P:(k + 1) * P], c.ident[:])
                    tr.then_inc(tr_done, 1)
                pe.wait_ge(lo_done, at(NG, i, NG))
                for n, (si, m, h) in enumerate(outs):
                    w = SEGS[si][2]
                    if n == 0 or outs[n - 1][0] != si:
                        pe.wait_ge(wlo_done, at(NSEG, i, si + 1))
                    pe.wait_ge(evac_done, at(NO, i, n - PB + 1))
                    bank = c.bank[2 + n % PB]
                    b = si % 2
                    for k in range(KD):
                        for xs, ws in ((xhi, whi), (xlo, whi), (xhi, wlo)):
                            if h is not None:
                                lhsT, rhs = ws[:, b, k, m * P:(m + 1) * P], xs[:, k, 512 * h:512 * (h + 1)]
                                dst = bank[:, :]
                            elif SEGS[si][0] == "u":
                                lhsT, rhs, dst = xs[:, k, m:TB:8], ws[:, b, k, 0:w], bank[:, 0:w]
                            else:
                                lhsT, rhs, dst = xs[:, k, m * P:(m + 1) * P], ws[:, b, k, 0:w], bank[:, 0:w]
                            last = pe.matmul(dst, lhsT, rhs, start=(k == 0 and ws is whi and xs is xhi),
                                             stop=(k == KD - 1 and ws is wlo))
                    last.then_inc(proj_done, 1)

        @block.scalar
        def _(act):
            act.sem_inc(evac_done, NO)
            for j in range(2):
                act.sem_inc(f_stored[j], fper[j])
            for j in range(4):
                act.sem_inc(t_stored[j], 16 * 4)
            act.sem_inc(u_stored, 16)
            ssm_c.load_scalars(nc, act, a)
            ssm_c.scalar_functions(act)
            act.wait_ge(g_loaded, 16)
            with act.Fori(0, NTB) as i:
                for g in range(NG):
                    k, h = g // 2, g % 2
                    act.wait_ge(tr_done, NG * i + g + 1)
                    act.activation(xhi[:, k, 512 * h:512 * (h + 1)], c.bank[g % 2][:], ACT.Copy,
                                   scale=gn[:, k:k + 1]).then_inc(hi_done, 1)
                fm = tm = 0
                for n, (si, m, h) in enumerate(outs):
                    name, c0, w = SEGS[si]
                    act.wait_ge(proj_done, at(NO, i, n + 1))
                    bank = c.bank[2 + n % PB]
                    if h is not None:
                        dram, row, scale = dest[name]
                        slot = fm % 2
                        if h == 0:
                            act.wait_ge(f_stored[slot], at(fper[slot], i, 16 * (fm // 2)))
                        func = ACT.Silu if scale is None else ACT.Copy
                        act.activation(fstage[:, slot, 512 * h:512 * (h + 1)], bank[:], func,
                                       scale=1.0 if scale is None else scale).then_inc(evac_done, 1)
                        if h == 1:
                            act.wait_ge(evac_done, at(NO, i, n + 1))
                            r0 = row + m * P
                            act.dma_start(dram[r0:r0 + P, bass.ds(i * TB, TB)], fstage[:, slot, :]
                                          ).then_inc(f_stored[slot], 16)
                            fm += 1
                    elif name == "u":
                        if m == 0:
                            act.wait_ge(u_stored, at(16, i, 0))
                        act.activation(ustage[:, :, m, :], bank[:, 0:WS].rearrange("p (g c) -> p g c", c=GC),
                                       ACT.Copy).then_inc(evac_done, 1)
                        if m == NT - 1:
                            act.wait_ge(evac_done, at(NO, i, n + 1))
                            act.dma_start(c.u_chunks[i], ustage[:].rearrange("p g t c -> p (g t c)")
                                          ).then_inc(u_stored, 16)
                    else:
                        slot = tm % 4
                        act.wait_ge(t_stored[slot], at(64, i, 16 * (tm // 4)))
                        if name == "v":
                            act.activation(c.flogit[:, i * NT + m, :], bank[:, WF:WF + NF], ACT.Copy)
                        act.activation(tstage[:, slot, :], bank[:, 0:WF], ACT.Copy).then_inc(evac_done, 1)
                        act.wait_ge(evac_done, at(NO, i, n + 1))
                        act.dma_start((k_v if name == "k" else v_v)[i, m], tstage[:, slot, :]
                                      ).then_inc(t_stored[slot], 16)
                        tm += 1
            for j in range(2):
                act.wait_ge(f_stored[j], at(fper[j], NTB, 0))
            for j in range(4):
                act.wait_ge(t_stored[j], at(64, NTB, 0))
            act.wait_ge(u_stored, at(16, NTB, 0))


def forget_gates(nc, c, b_f, logf_out):
    NT = T // P
    with ExitStack() as s:
        def sb(name, shape, dt=F32):
            return s.enter_context(nc.sbuf_tensor(name, shape, dt))

        def sem(name):
            return s.enter_context(nc.semaphore(name))

        bf = sb("bf", [P, NF])
        z, zn, za, ez, sp_ = (sb(n, [P, NT, NF]) for n in ("fz", "fzn", "fza", "fez", "fsp"))
        lf = sb("lf", [P, NT, NF])
        pre = sb("lf_prefix", [P, NF, NT])
        prex = sb("lf_before", [P, NT, NF])
        rows = sb("crow_stage", [P, 2, P], F32R)
        loaded, dve_step, act_step, pe_step, stored = sem("bf_loaded"), sem("f_dve"), sem("f_act"), sem("f_pe"), sem("f_stored")
        block = s.enter_context(nc.Block())
        cum = c.bank[0][:, 0:NT * NF]

        @block.sync
        def _(sp):
            with nc.allow_non_contiguous_dma(reason="six forget gates a token"):
                sp.dma_start(bf[:], b_f[0].partition_broadcast(P)).then_inc(loaded, 16)
                sp.wait_ge(dve_step, 5)
                sp.dma_start(logf_out.rearrange("l o (t p) h -> p (l o t) h", p=P), lf[:]).then_inc(stored, 16)
                sp.wait_ge(dve_step, 17)
                sp.dma_start(c.negc_rows.rearrange("h (t p) -> (h t) p", p=P)[0:P], rows[:, 0, :].bitcast(F32)).then_inc(stored, 16)
                sp.dma_start(c.negc_rows.rearrange("h (t p) -> (h t) p", p=P)[P:NF * NT], rows[0:NF * NT - P, 1, :].bitcast(F32)
                             ).then_inc(stored, 16)
            sp.wait_ge(stored, 48)

        @block.vector
        def _(dve):
            n = [0]

            def done(ins):
                n[0] += 1
                ins.then_inc(dve_step, 1)
                dve.wait_ge(dve_step, n[0])

            dve.wait_ge(loaded, 16)
            done(dve.tensor_tensor(z[:], c.flogit[:], bf[:].unsqueeze(1).to_broadcast([P, NT, NF]), ALU.add))
            done(dve.tensor_scalar(zn[:], z[:], -1.0, None, ALU.mult))
            done(dve.tensor_tensor(za[:], z[:], zn[:], ALU.min))
            done(dve.tensor_scalar(zn[:], z[:], 0.0, None, ALU.min))
            dve.wait_ge(act_step, 2)
            done(dve.tensor_tensor(lf[:], zn[:], sp_[:], ALU.subtract))
            for h in range(NF):
                dve.tensor_tensor_scan(pre[:, h, :], c.ones[:, 0:NT], lf[:, :, h], 0.0, ALU.mult,
                                       ALU.add).then_inc(dve_step, 1)
            dve.memset(prex[:, 0, :], 0.0).then_inc(dve_step, 1)
            dve.wait_ge(dve_step, 12)
            dve.tensor_copy(prex[:, 1:NT, :], pre[:, :, 0:NT - 1].rearrange("p h t -> p t h")).then_inc(dve_step, 1)
            dve.wait_ge(pe_step, 1)
            dve.tensor_scalar(c.negc[:], cum.rearrange("p (t h) -> p h t", h=NF), -1.0, None, ALU.mult
                              ).then_inc(dve_step, 1)
            dve.wait_ge(pe_step, 2)
            dve.tensor_copy(rows[:, 0, :], c.bank[1][:, 0:P]).then_inc(dve_step, 1)
            dve.wait_ge(pe_step, 3)
            dve.tensor_copy(rows[0:NF * NT - P, 1, :], c.bank[2][0:NF * NT - P, 0:P]).then_inc(dve_step, 1)
            dve.wait_ge(dve_step, 16)
            dve.sem_inc(dve_step, 1)

        @block.scalar
        def _(act):
            act.wait_ge(dve_step, 3)
            act.activation(ez[:], za[:], ACT.Exp).then_inc(act_step, 1)
            act.wait_ge(act_step, 1)
            act.activation(sp_[:], ez[:], ACT.Ln, bias=1.0).then_inc(act_step, 1)

        @block.tensor
        def _(pe):
            pe.wait_ge(dve_step, 13)
            pe.matmul(cum, c.upper[:], lf[:].rearrange("p t h -> p (t h)"), start=True, stop=False)
            pe.matmul(cum, c.ones[:], prex[:].rearrange("p t h -> p (t h)"), start=False, stop=True
                      ).then_inc(pe_step, 1)
            pe.wait_ge(dve_step, 14)
            negc = c.negc[:].rearrange("p h t -> p (h t)")
            pe.transpose(c.bank[1][:, 0:P], negc[:, 0:P], c.ident[:]).then_inc(pe_step, 1)
            pe.transpose(c.bank[2][0:NF * NT - P, 0:P], negc[:, P:NF * NT], c.ident[:]).then_inc(pe_step, 1)


def fox_prompt(nc, c, k_out, v_out, ssm_c, a):
    NB = T // 512
    NT = T // P
    KG = 4
    k_h = k_out.rearrange("l o (t p) h d -> (l o h) p t d", p=P)
    v_h = v_out.rearrange("l o (g t p) h d -> (l o h) g p t d", p=P, t=KG)
    q_h = c.q_t.rearrange("(h d) t -> h d t", d=HD)
    g_h = c.gate_t.rearrange("(h d) t -> h d t", d=HD)
    m_h = c.mix_t.rearrange("(h d) t -> h d t", d=HD)
    c_h = c.negc_rows.rearrange("h (o t) -> h o t", o=1)
    SB, XB, NPRE, TB, OB = 2, 2, 3, 5, 6
    pre = [(b, r, ch, 512 if ch < b else (r + 1) * P) for b in range(NB) for r in range(4) for ch in range(b + 1)]
    pre_end = [4 * (b + 1) * (b + 2) // 2 for b in range(NB)]
    main = [(b, j, max(0, (j - 4 * b) * P)) for b in range(NB) for j in range(4 * b + 4)]
    main_end = [sum(4 * x + 4 for x in range(b + 1)) for b in range(NB)]
    NPR, NMN = len(pre), len(main)
    NG = NT // KG
    LASTB = NB - 1
    QS = 4

    with ExitStack() as s:
        def sb(name, shape, dt=F32):
            return s.enter_context(nc.sbuf_tensor(name, shape, dt))

        def sem(name):
            return nc.alloc_semaphore(name)

        q2 = sb("q2", [P, 2, 512])
        qhi = sb("qhi", [P, QS, 512], F32R)
        qlo = sb("qlo", [HD + 2, QS, 512], F32R)
        qone = sb("qone", [HD + 2, QS, 512], F32R)
        ktok = sb("ktok", [P, NT, HD])
        khl = sb("khl", [P, NT, 2, HD])
        kst = sb("kst", [P, T], F32R)
        kone = sb("kone", [HD + 2, T], F32R)
        vone = sb("vone", [P, NT, P])
        gate = sb("gate_a", [HD, T])
        ncol = sb("ncol", [P, NT])
        p = sb("p", [P, 3, 512])
        pm = sb("pm", [P, 4, NB])
        nm = sb("nm", [P, 2, 4])
        mrow = sb("mrow", [4, 2, P], F32R)
        rec = sb("rec", [HD, 512])
        on = sb("on", [HD, 512])
        og = sb("og", [HD, 2, 512])
        q_in = [sem("q_in0"), sem("q_in1")]
        g_in = [sem(f"g_in{b}") for b in range(NB)]
        k_in, ones_set = sem("k_in"), sem("ones_set")
        vc_in = [sem(f"vc_in{g}") for g in range(NG)]
        q_ready, khl_done, ktr, kst_done, kone_done = (sem(n) for n in ("q_ready", "khl_done", "ktr", "kst_done", "kone_done"))
        pre_s, pre_max, nm_done, nm_tr, mrow_done = (sem(n) for n in ("pre_s", "pre_max", "nm_done", "nm_tr", "mrow_done"))
        m_in = [sem("m_in0"), sem("m_in1")]
        sc, ex, pv = sem("scores"), sem("exp_done"), sem("pv_done")
        s_turn = sem("store_turn")
        o_rec, o_norm, o_gated = sem("o_rec"), sem("o_norm"), sem("o_gated")
        o_stored = [sem("o_stored0"), sem("o_stored1")]
        ssm_c.place_tables(s, nc)
        block = s.enter_context(nc.Block())

        def heads(engine, body):
            with engine.Fori(0, NF - 1) as h:
                body(h, False)
            body(NF - 1, True)

        @block.sync
        def _(sp):
            def load_q(h, b):
                sp.dma_start(q2[0:HD, b % 2, :], q_h[h, :, 512 * b:512 * (b + 1)]).then_inc(q_in[b % 2], 16)
                sp.dma_start(q2[HD:P, b % 2, :], q_h[h, :, 512 * b:512 * (b + 1)]).then_inc(q_in[b % 2], 16)
                sp.dma_start(gate[:, 512 * b:512 * (b + 1)], g_h[h, :, 512 * b:512 * (b + 1)]).then_inc(g_in[b], 16)

            def load_vc(h, g):
                sp.dma_start(vone[:, KG * g:KG * (g + 1), 0:HD], v_h[h, g]).then_inc(vc_in[g], 16)
                sp.dma_start(kone[HD + 1:HD + 2, 512 * g:512 * (g + 1)].bitcast(F32), c_h[h, :, 512 * g:512 * (g + 1)]
                             ).then_inc(vc_in[g], 16)

            def m_row(h, b):
                sp.wait_ge(mrow_done, NB * h + b + 1)
                sp.dma_start(qlo[HD:HD + 1, b % QS, :].bitcast(F32), mrow[:, b % 2, :].bitcast(F32)).then_inc(m_in[b % 2], 16)

            def store(h, b):
                sp.wait_ge(o_gated, NB * h + b + 1)
                sp.sem_inc(s_turn, 1)
                sp.dma_start(m_h[h, :, 512 * b:512 * (b + 1)], og[:, b % 2, :]).then_inc(o_stored[b % 2], 16)

            def body(h, last):
                for b in range(NB):
                    if b == 1 and not last:
                        sp.wait_ge(khl_done, 2 * (h + 1))
                        sp.dma_start(ktok[:], k_h[h + 1]).then_inc(k_in, 16)
                    if b + 3 < NB or not last:
                        sp.wait_ge(q_ready, 3 * (NB * h + b + 2))
                        load_q(h + (b + 3) // NB, (b + 3) % NB)
                    if b:
                        store(h, b - 1)
                    if b + 2 < NB:
                        m_row(h, b + 2)
                if not last:
                    for g in range(NG):
                        sp.wait_ge(pv, at(NMN, h, main_end[LASTB - 1] + KG * (g + 1)))
                        load_vc(h + 1, g)
                        if g in (2, 5):
                            m_row(h + 1, g // 3)
                store(h, LASTB)

            sp.dma_start(ktok[:], k_h[0]).then_inc(k_in, 16)
            load_q(0, 0)
            load_q(0, 1)
            sp.wait_ge(ones_set, 5)
            for g in range(NG):
                load_vc(0, g)
            m_row(0, 0)
            sp.wait_ge(q_ready, 3)
            load_q(0, 2)
            m_row(0, 1)
            heads(sp, body)
            for j in range(2):
                sp.wait_ge(o_stored[j], at(16 * NB // 2, NF, 0))

        @block.gpsimd
        def _(pool):
            pool.memset(vone[:, :, HD:P], 1.0).then_inc(ones_set, 1)
            pool.wait_ge(ones_set, 1)
            pool.memset(kone[HD:HD + 2, :].bitcast(F32), 1.0).then_inc(ones_set, 1)
            pool.wait_ge(ones_set, 2)
            pool.memset(qlo[HD:HD + 2, :, :].bitcast(F32), 0.0).then_inc(ones_set, 1)
            pool.wait_ge(ones_set, 3)
            pool.memset(qone[HD:HD + 2, :, :].bitcast(F32), 1.0).then_inc(ones_set, 1)
            pool.wait_ge(ones_set, 4)
            pool.memset(qone[HD:HD + 1, :, :].bitcast(F32), 0.0).then_inc(ones_set, 1)
            pool.wait_ge(ones_set, 5)
            ssm_c.tables(pool, c)

        @block.vector
        def _(dve):
            dve.sem_inc(pre_max, 2 * NPR)
            dve.sem_inc(o_norm, NB)
            for j in range(2):
                dve.sem_inc(o_stored[j], 16 * NB // 2)

            def split_k(h):
                dve.wait_ge(k_in, 16 * (h + 1))
                dve.tensor_copy(khl[:, :, 0, :].bitcast(F32R), ktok[:]).then_inc(khl_done, 1)
                dve.wait_ge(khl_done, 2 * h + 1)
                dve.tensor_tensor(khl[:, :, 1, :].bitcast(F32R), ktok[:], khl[:, :, 0, :], ALU.subtract).then_inc(khl_done, 1)

            def split_q(h, b):
                n, d = 3 * (NB * h + b), b % QS
                dve.wait_ge(q_in[b % 2], 32 * (NB // 2 * h + b // 2 + 1))
                dve.tensor_copy(qhi[:, d, :], q2[:, b % 2, :]).then_inc(q_ready, 1)
                dve.wait_ge(q_ready, n + 1)
                dve.tensor_copy(qone[0:HD, d, :], qhi[0:HD, d, :].bitcast(F32)).then_inc(q_ready, 1)
                dve.tensor_tensor(qlo[0:HD, d, :], q2[0:HD, b % 2, :], qhi[0:HD, d, :].bitcast(F32), ALU.subtract).then_inc(q_ready, 1)

            def k_one(h, g):
                dve.wait_ge(kst_done, NG * h + g + 1)
                dve.tensor_copy(ncol[:, KG * g:KG * (g + 1)], c.negc[:, h, KG * g:KG * (g + 1)]).then_inc(kone_done, 1)
                dve.tensor_copy(kone[0:HD, 512 * g:512 * (g + 1)], kst[0:HD, 512 * g:512 * (g + 1)].bitcast(F32)
                                ).then_inc(kone_done, 1)

            def maxima(h, n0, n1):
                for n in range(n0, n1):
                    b, r, ch, w = pre[n]
                    dve.wait_ge(pre_s, NPR * h + n + 1)
                    dve.tensor_reduce(pm[:, r, ch:ch + 1], c.bank[XB + n % NPRE][:, 0:w], AX.X, ALU.max
                                      ).then_inc(pre_max, 1)
                    if n + 1 == pre_end[b]:
                        dve.wait_ge(pre_max, at(NPR, h + 1, n + 1))
                        dve.tensor_reduce(nm[:, b % 2, :], pm[:, :, 0:b + 1], AX.X, ALU.max, negate=True
                                          ).then_inc(nm_done, 1)
                        dve.wait_ge(nm_tr, NB * h + b + 1)
                        dve.tensor_copy(mrow[:, b % 2, :], c.bank[TB][0:4, 0:P]).then_inc(mrow_done, 1)

            def finish(h, b):
                dve.wait_ge(pv, at(NMN, h, main_end[b]))
                ob = c.bank[OB + b % 2]
                dve.reciprocal(rec[:], ob[HD:P, :]).then_inc(o_rec, 1)
                dve.wait_ge(o_rec, NB * h + b + 1)
                dve.tensor_tensor(on[:], ob[0:HD, :], rec[:], ALU.mult).then_inc(o_norm, 1)
                dve.wait_ge(o_norm, at(NB, h, b + 1))
                dve.wait_ge(g_in[b], 16 * (h + 1))
                dve.wait_ge(o_stored[b % 2], at(16 * NB // 2, h, 16 * (b // 2)))
                dve.tensor_tensor(og[:, b % 2, :], on[:], gate[:, 512 * b:512 * (b + 1)], ALU.mult
                                  ).then_inc(o_gated, 1)

            def body(h, last):
                for b in range(NB):
                    if b + 2 < NB:
                        first = pre_end[b + 1] + NPRE
                        maxima(h, pre_end[b + 1], first)
                        if b:
                            finish(h, b - 1)
                        maxima(h, first, pre_end[b + 2])
                    else:
                        finish(h, b - 1)
                    if b == 4 and not last:
                        split_k(h + 1)
                    if b == LASTB and not last:
                        k_one(h + 1, 0)
                        maxima(h + 1, 0, pre_end[0])
                        for g in range(1, 4):
                            k_one(h + 1, g)
                        maxima(h + 1, pre_end[0], pre_end[1])
                        for g in range(4, NG):
                            k_one(h + 1, g)
                    if b + 3 < NB or not last:
                        split_q(h + (b + 3) // NB, (b + 3) % NB)
                finish(h, LASTB)

            split_k(0)
            split_q(0, 0)
            split_q(0, 1)
            dve.wait_ge(ones_set, 5)
            k_one(0, 0)
            maxima(0, 0, pre_end[0])
            k_one(0, 1)
            maxima(0, pre_end[0], pre_end[1])
            for g in range(2, NG):
                k_one(0, g)
            split_q(0, 2)
            ssm_c.copy_c(dve, c)
            heads(dve, body)

        @block.scalar
        def _(act):
            ssm_c.load_tables(nc, act, a)
            act.sem_inc(ex, NMN)

            def k_turned(h, g):
                act.wait_ge(ktr, NG * h + g + 1)
                act.activation(kst[:, 512 * g:512 * (g + 1)], c.bank[TB][:], ACT.Copy).then_inc(kst_done, 1)

            def body(h, last):
                for n, (b, j, q0) in enumerate(main):
                    if j == 0:
                        act.wait_ge(kone_done, 2 * (NG * h + b + 1))
                    act.wait_ge(sc, NMN * h + n + 1)
                    act.wait_ge(pv, at(NMN, h, n - 2))
                    act.activation(p[:, n % 3, q0:512], c.bank[n % SB][:, q0:512], ACT.Exp,
                                   bias=ncol[:, j:j + 1]).then_inc(ex, 1)
                    if b == LASTB and not last and j and j % KG == 0:
                        k_turned(h + 1, j // KG - 1)
                if not last:
                    k_turned(h + 1, NG - 1)

            for g in range(NG):
                k_turned(0, g)
            heads(act, body)

        @block.tensor
        def _(pe):
            pe.sem_inc(pv, NMN)

            def turn_k(h, g):
                pe.wait_ge(khl_done, 2 * (h + 1))
                if not (isinstance(h, int) and h == 0 and g == 0):
                    pe.wait_ge(kst_done, NG * h + g)
                for t in range(KG):
                    tr = pe.transpose(c.bank[TB][:, t * P:(t + 1) * P],
                                      khl[:, KG * g + t, :, :].rearrange("p a d -> p (a d)"), c.ident[:])
                tr.then_inc(ktr, 1)

            def maxima_to_rows(h, b, turned):
                pe.wait_ge(nm_done, NB * h + b + 1)
                pe.wait_ge(kst_done, turned)
                pe.transpose(c.bank[TB][0:4, 0:P], nm[:, b % 2, :], c.ident[:]).then_inc(nm_tr, 1)

            def first_pass(h, n0, n1):
                for n in range(n0, n1):
                    b, r, ch, w = pre[n]
                    if r == 0 and ch == 0:
                        pe.wait_ge(q_ready, 3 * (NB * h + b + 1))
                        pe.wait_ge(kone_done, 2 * (NG * h + b + 1))
                        pe.wait_ge(vc_in[b], 32 * (h + 1))
                    pe.wait_ge(pre_max, at(NPR, h + 1, n - NPRE + 1))
                    q = slice(r * P, (r + 1) * P)
                    bank = c.bank[XB + n % NPRE]
                    mm = pe.matmul(bank[:, 0:w], qone[:, b % QS, q], kone[:, 512 * ch:512 * ch + w],
                                   start=True, stop=True)
                    if ch == b:
                        mm = pe.matmul(bank[:, w - P:w], c.identb[:], c.mask_qk[:], start=False, stop=True,
                                       skip_group_check=True)
                    mm.then_inc(pre_s, 1)

            def weighted(h, n):
                b, j, q0 = main[n]
                pe.wait_ge(ex, at(NMN, h, n + 1))
                if j == 0:
                    pe.wait_ge(o_norm, at(NB, h, b - 1))
                pe.matmul(c.bank[OB + b % 2][:, q0:512], vone[:, j, :], p[:, n % 3, q0:512], start=(j == 0),
                          stop=(j == 4 * b + 3), skip_group_check=True).then_inc(pv, 1)

            def body(h, last):
                for n, (b, j, q0) in enumerate(main):
                    if j == 0:
                        pe.wait_ge(m_in[b % 2], 16 * (NB // 2 * h + b // 2 + 1))
                        n_pre = pre_end[b + 1] if b + 2 < NB else NPR
                        rows_due = b + 2 < NB
                    bank = c.bank[n % SB]
                    pe.wait_ge(ex, at(NMN, h, n - SB + 1))
                    pe.matmul(bank[:, q0:512], kst[:, j * P:(j + 1) * P], qhi[:, b % QS, q0:512], start=True, stop=False)
                    mm = pe.matmul(bank[:, q0:512], kone[:, j * P:(j + 1) * P], qlo[:, b % QS, q0:512], start=False, stop=True)
                    if j >= 4 * b:
                        mm = pe.matmul(bank[:, q0:q0 + P], c.identb[:], c.mask_kq[:], start=False, stop=True,
                                       skip_group_check=True)
                    mm.then_inc(sc, 1)
                    if b + 2 < NB:
                        if n_pre == pre_end[b + 2] and rows_due:
                            maxima_to_rows(h, b + 2, NG * (h + 1))
                            rows_due = False
                        rate = 3 if b < 3 else (0 if j in (2, 3) else 1 if j == 1 else 2)
                        upto = min(n_pre + rate, pre_end[b + 2])
                        first_pass(h, n_pre, upto)
                        n_pre = upto
                    elif b == LASTB and not last:
                        if 2 * KG <= j < 3 * KG:
                            first_pass(h + 1, j - 2 * KG, j - 2 * KG + 1)
                        elif 4 * KG <= j < 6 * KG:
                            first_pass(h + 1, j - 3 * KG, j - 3 * KG + 1)
                        elif j in (3 * KG + 2, 6 * KG + 2):
                            maxima_to_rows(h + 1, j // (3 * KG) - 1, NG * (h + 1) + j // KG)
                    if n:
                        weighted(h, n - 1)
                    if b + 2 < NB and j == 4 * b + 3 and rows_due:
                        maxima_to_rows(h, b + 2, NG * (h + 1))
                    if b == LASTB and not last and j and j % KG == 0:
                        if j in (4 * KG, 7 * KG):
                            pe.wait_ge(mrow_done, NB * (h + 1) + j // (4 * KG) + j // (7 * KG))
                        turn_k(h + 1, j // KG - 1)
                weighted(h, NMN - 1)
                if not last:
                    turn_k(h + 1, NG - 1)

            turn_k(0, 0)
            pe.wait_ge(ones_set, 5)
            first_pass(0, 0, pre_end[0])
            maxima_to_rows(0, 0, 1)
            pe.wait_ge(mrow_done, 1)
            turn_k(0, 1)
            first_pass(0, pre_end[0], pre_end[1])
            maxima_to_rows(0, 1, 2)
            pe.wait_ge(mrow_done, 2)
            for g in range(2, NG):
                turn_k(0, g)
            ssm_c.turn_c(pe, c)
            pe.wait_ge(ssm_c.c_out, 2)
            heads(pe, body)


def memory_prompt(nc, c, mem, g_mem, w_kv, mk_out, mv_out):
    NB = T // 512
    MT = NMEM // P
    with ExitStack() as s:
        def sb(name, shape, dt=F32):
            return s.enter_context(nc.sbuf_tensor(name, shape, dt))

        def sem(name):
            return s.enter_context(nc.semaphore(name))

        x = sb("mem_x", [P, MT, D])
        w = sb("mem_w", [P, KD, 2 * WM])
        gm = sb("mem_g", [P, KD])
        xt = sb("mem_xt", [P, KD, NMEM])
        junk = sb("mem_junk", [P, D], BF16)
        ss, rin, rstd = sb("mem_ss", [P, MT]), sb("mem_rin", [P, MT]), sb("mem_rstd", [P, MT])
        kv = sb("mem_kv", [P, MT, 2 * WM])
        kt = sb("mem_kt", [P, 2, NMEM])
        q = sb("mem_q", [P, 2, 2, 512])
        gate = sb("mem_gate", [HD, 2, NM, 512])
        nmax, tot, rtot = sb("mem_nmax", [P, 2, NM]), sb("mem_tot", [P, 2, NM]), sb("mem_rtot", [P, 2, NM])
        p = sb("mem_p", [P, 2, NM, NMEM])
        pn = sb("mem_pn", [P, 2, NM, NMEM])
        pt = sb("mem_pt", [P, 2, NM, MT, 512])
        og = sb("mem_og", [HD, 2, NM, 512])
        loaded, step, powed, pe1 = sem("mem_loaded"), sem("mem_step"), sem("mem_powed"), sem("mem_pe")
        q_in = [sem("mem_q_in0"), sem("mem_q_in1")]
        s_done, max_done, exp_done, norm_done, tr_done, pt_done = (
            sem(n) for n in ("mem_s", "mem_max", "mem_exp", "mem_norm", "mem_tr", "mem_ptd"))
        r_done, o_done, og_done = sem("mem_r"), sem("mem_o"), sem("mem_ogd")
        o_stored = [sem("mem_st0"), sem("mem_st1")]
        kv_stored = sem("mem_kv_stored")
        block = s.enter_context(nc.Block())
        NT = 4
        q_v = c.qm_t.rearrange("(a p) (b t) -> b p a t", p=P, t=512)
        g_v = c.gate_t[WF + WS:D].rearrange("(h d) (b t) -> b d h t", d=HD, t=512)
        m_v = c.mix_t[WF + WS:D].rearrange("(h d) (b t) -> b d h t", d=HD, t=512)

        @block.sync
        def _(sp):
            with nc.allow_non_contiguous_dma(reason="1024 gains"):
                sp.dma_start(gm[:], g_mem.rearrange("o (k p) -> p (o k)", p=P)).then_inc(loaded, 16)
            sp.dma_start(x[:], mem.rearrange("o (t p) d -> p (o t) d", p=P)).then_inc(loaded, 16)
            sp.dma_start(w[:], w_kv.rearrange("o (k p) n -> p (o k) n", p=P)).then_inc(loaded, 16)
            with sp.Fori(0, NB // 2) as i:
                for j in range(2):
                    sp.wait_ge(og_done, at(2 * NM, i, (j - 1) * NM + NM))
                    sp.dma_start(q[:, j], q_v[2 * i + j]).then_inc(q_in[j], 16)
                    sp.dma_start(gate[:, j], g_v[2 * i + j]).then_inc(q_in[j], 16)

        @block.gpsimd
        def _(pool):
            pool.wait_ge(step, MT + 1)
            pool.tensor_tensor(rstd[:], rin[:], c.minus_half[:, 0:MT], ALU.pow).then_inc(powed, 1)

        @block.vector
        def _(dve):
            for sem_ in (og_done,):
                dve.sem_inc(sem_, 2 * NM)
            dve.sem_inc(pt_done, 4 * NT)
            dve.sem_inc(norm_done, 2 * NT * NM)
            dve.wait_ge(loaded, 48)
            for t in range(MT):
                dve.tensor_tensor_reduce(junk[:], x[:, t, :], x[:, t, :], 1.0, 0.0, ALU.mult, ALU.add,
                                         ss[:, t:t + 1]).then_inc(step, 1)
                dve.wait_ge(step, t + 1)
            dve.tensor_scalar(rin[:], ss[:], 1.0 / D, EPS, ALU.mult, ALU.add).then_inc(step, 1)
            dve.wait_ge(powed, 1)
            for t in range(MT):
                dve.tensor_scalar(x[:, t, :], x[:, t, :], rstd[:, t:t + 1], None, ALU.mult).then_inc(step, 1)
            for k in range(KD):
                dve.wait_ge(pe1, k + 1)
                dve.tensor_scalar(xt[:, k, :], c.bank[k % 4][:, 0:NMEM], gm[:, k:k + 1], None, ALU.mult
                                  ).then_inc(step, 1)
            for t in range(MT):
                dve.wait_ge(pe1, KD + t + 1)
                dve.tensor_copy(kv[:, t, :], c.bank[4 + t][:]).then_inc(step, 1)
            dve.wait_ge(pe1, KD + MT + 1)
            dve.tensor_copy(kt[:].rearrange("p a n -> p (a n)"), c.bank[0][:]).then_inc(step, 1)

            def prepare(i, j, t):
                n = 4 * j + t
                for a in range(2):
                    dve.wait_ge(s_done, 16 * i + 2 * n + a + 1)
                    dve.tensor_reduce(nmax[:, t % 2, a:NM:2],
                                      c.bank[2 * (t % 2) + a][:].rearrange("p (h k) -> p h k", h=2), AX.X, ALU.max,
                                      negate=True).then_inc(max_done, 1)

            def finish(i, j, t):
                n = 4 * j + t
                dve.wait_ge(exp_done, at(2 * NT * NM, i, NM * (n + 1)))
                dve.reciprocal(rtot[:, t % 2, :], tot[:, t % 2, :]).then_inc(r_done, 1)
                dve.wait_ge(r_done, 8 * i + n + 1)
                dve.wait_ge(tr_done, at(32, i, 4 * (n - 1)))
                for h in range(NM):
                    dve.tensor_scalar(pn[:, t % 2, h, :], p[:, t % 2, h, :], rtot[:, t % 2, h:h + 1], None,
                                      ALU.mult).then_inc(norm_done, 1)
                for b in range(2):
                    dve.wait_ge(tr_done, at(32, i, 4 * n + 2 * b + 2))
                    dve.tensor_copy(pt[:, j, 2 * b:2 * b + 2, :, t * P:(t + 1) * P],
                                    c.bank[4 + b][:].rearrange("p (h k q) -> p h k q", h=2, k=MT)).then_inc(pt_done, 1)

            with dve.Fori(0, NB // 2) as i:
                for j in range(2):
                    prepare(i, j, 0)
                    for t in range(NT):
                        if t + 1 < NT:
                            prepare(i, j, t + 1)
                        finish(i, j, t)
                    dve.wait_ge(q_in[j], 32 * (i + 1))
                    dve.wait_ge(o_stored[j], at(16, i, 0))
                    for h in range(NM):
                        dve.wait_ge(o_done, 2 * NM * i + NM * j + h + 1)
                        dve.tensor_tensor(og[:, j, h, :], c.bank[6 + h % 2][0:HD, :], gate[:, j, h, :], ALU.mult
                                          ).then_inc(og_done, 1)

        @block.scalar
        def _(act):
            act.sem_inc(exp_done, 2 * NT * NM)
            for j in range(2):
                act.sem_inc(o_stored[j], 16)
            act.wait_ge(step, 1 + 2 * MT + KD + MT)
            act.dma_start(mk_out.rearrange("l o (t p) h d -> p (l o t) (h d)", p=P), kv[:, :, 0:WM]).then_inc(kv_stored, 16)
            act.dma_start(mv_out.rearrange("l o (t p) h d -> p (l o t) (h d)", p=P), kv[:, :, WM:]).then_inc(kv_stored, 16)
            with act.Fori(0, NB // 2) as i:
                for j in range(2):
                    for t in range(NT):
                        n = 4 * j + t
                        act.wait_ge(norm_done, at(2 * NT * NM, i, NM * (n - 1)))
                        for h in range(NM):
                            act.wait_ge(max_done, 16 * i + 2 * n + h % 2 + 1)
                            act.activation(p[:, t % 2, h, :], c.bank[2 * (t % 2) + h % 2][:, (h // 2) * NMEM:(h // 2 + 1) * NMEM],
                                           ACT.Exp, bias=nmax[:, t % 2, h:h + 1], accum_out=tot[:, t % 2, h:h + 1]
                                           ).then_inc(exp_done, 1)
                    act.wait_ge(og_done, at(2 * NM, i, NM * (j + 1)))
                    act.dma_start(m_v[2 * i + j], og[:, j]).then_inc(o_stored[j], 16)
            for j in range(2):
                act.wait_ge(o_stored[j], at(16, NB // 2, 0))
            act.wait_ge(kv_stored, 32)

        @block.tensor
        def _(pe):
            pe.sem_inc(tr_done, 32)
            pe.wait_ge(step, 2 * MT + 1)
            for k in range(KD):
                if k >= 4:
                    pe.wait_ge(step, 2 * MT + 1 + k - 3)
                for t in range(MT):
                    tr = pe.transpose(c.bank[k % 4][:, t * P:(t + 1) * P], x[:, t, k * P:(k + 1) * P], c.ident[:])
                tr.then_inc(pe1, 1)
            pe.wait_ge(step, 2 * MT + 1 + KD)
            for t in range(MT):
                for k in range(KD):
                    mm = pe.matmul(c.bank[4 + t][:], xt[:, k, t * P:(t + 1) * P], w[:, k, :], start=(k == 0), stop=(k == KD - 1))
                mm.then_inc(pe1, 1)
            pe.wait_ge(step, 2 * MT + 1 + KD + MT)
            for a in range(2):
                for t in range(MT):
                    tr = pe.transpose(c.bank[0][:, a * NMEM + t * P:a * NMEM + (t + 1) * P], kv[:, t, a * P:(a + 1) * P], c.ident[:])
            tr.then_inc(pe1, 1)
            pe.wait_ge(step, 2 * MT + 2 + KD + MT)

            def scores(i, j, t):
                n = 4 * j + t
                if t == 0:
                    pe.wait_ge(q_in[j], 32 * (i + 1))
                pe.wait_ge(exp_done, at(2 * NT * NM, i, NM * (n - 1)))
                for h in range(NM):
                    r = HD * (h % 2)
                    mm = pe.matmul(c.bank[2 * (t % 2) + h % 2][:, (h // 2) * NMEM:(h // 2 + 1) * NMEM],
                                   q[r:r + HD, j, h // 2, t * P:(t + 1) * P], kt[r:r + HD, h // 2, :], start=True, stop=True)
                    if h >= 2:
                        mm.then_inc(s_done, 1)

            with pe.Fori(0, NB // 2) as i:
                for j in range(2):
                    scores(i, j, 0)
                    for t in range(NT):
                        if t + 1 < NT:
                            scores(i, j, t + 1)
                        n = 4 * j + t
                        for h in range(NM):
                            pe.wait_ge(norm_done, at(2 * NT * NM, i, NM * n + h + 1))
                            if h % 2 == 0:
                                pe.wait_ge(pt_done, at(4 * NT, i, 2 * (n - 1) + h // 2 + 1))
                            for k in range(MT):
                                tr = pe.transpose(c.bank[4 + h // 2][:, ((h % 2) * MT + k) * P:((h % 2) * MT + k + 1) * P],
                                                  pn[:, t % 2, h, k * P:(k + 1) * P], c.ident[:])
                            tr.then_inc(tr_done, 1)
                    pe.wait_ge(pt_done, at(4 * NT, i, 2 * (4 * j + NT)))
                    for h in range(NM):
                        pe.wait_ge(og_done, at(2 * NM, i, NM * j + h - 1))
                        for k in range(MT):
                            mm = pe.matmul(c.bank[6 + h % 2][0:HD, :], kv[:, k, WM + h * HD:WM + (h + 1) * HD], pt[:, j, h, k, :],
                                           start=(k == 0), stop=(k == MT - 1))
                        mm.then_inc(o_done, 1)


def sample_project(nc, c, a, o):
    W = 512
    CH = [(c0, min(W, DIN - c0)) for c0 in range(0, DIN, W)]
    with ExitStack() as s:
        def sb(name, shape, dt=F32):
            return s.enter_context(nc.sbuf_tensor(name, shape, dt))

        def sem(name):
            return s.enter_context(nc.semaphore(name))

        x = sb("sx", [8, D])
        junk = sb("sx_junk", [8, D], BF16)
        ss, rin, rstd = sb("sx_ss", [8, 1]), sb("sx_rin", [8, 1]), sb("sx_rstd", [8, 1])
        gn = sb("sx_g", [P, KD])
        xt = sb("sx_t", [P, KD, 8])
        w = sb("sx_w", [P, 3, KD, W])
        z = sb("sx_z", [8, DIN])
        bf = sb("sx_bf", [8, NF])
        f = [sb(f"sx_f{i}", [8, NF]) for i in range(5)]
        loaded, step, powed, turned, prod, acted, stored = (
            sem(n) for n in ("sx_loaded", "sx_step", "sx_powed", "sx_turned", "sx_prod", "sx_acted", "sx_stored"))
        w_in = [sem(f"sx_w_in{j}") for j in range(3)]
        block = s.enter_context(nc.Block())
        w_v = a["w_in"].rearrange("o (k p) n -> (o p) k n", p=P)
        BASE = 5

        @block.sync
        def _(sp):
            with nc.allow_non_contiguous_dma(reason="1024 gains"):
                sp.dma_start(gn[:], a["g_norm"].rearrange("o (k p) -> p (o k)", p=P)).then_inc(loaded, 16)
            sp.dma_start(x[:], a["x_sample"].rearrange("b o d -> (b o) d")).then_inc(loaded, 16)
            sp.dma_start(bf[:], a["b_f"][0].partition_broadcast(8)).then_inc(loaded, 16)
            for n, (c0, cw) in enumerate(CH):
                if n >= 3:
                    sp.wait_ge(prod, n - 2)
                sp.dma_start(w[:, n % 3, :, 0:cw], w_v[:, :, c0:c0 + cw]).then_inc(w_in[n % 3], 16)
            sp.wait_ge(step, BASE + len(CH))
            sp.dma_start(c.zs, z[:]).then_inc(stored, 16)
            sp.dma_start(o["k_sample"].rearrange("l b o h d -> (l b o) (h d)"), z[:, CK:CK + WF]).then_inc(stored, 16)
            sp.dma_start(o["v_sample"].rearrange("l b o h d -> (l b o) (h d)"), z[:, CV:CV + WF]).then_inc(stored, 16)
            sp.wait_ge(step, BASE + len(CH) + 5)
            sp.dma_start(o["logf_sample"].rearrange("l b o h -> (l b o) h"), c.lfs[:]).then_inc(stored, 16)
            sp.wait_ge(stored, 64)

        @block.gpsimd
        def _(pool):
            pool.wait_ge(step, 2)
            pool.tensor_tensor(rstd[:], rin[:], c.minus_half[0:8, 0:1], ALU.pow).then_inc(powed, 1)

        @block.vector
        def _(dve):
            n = [0]

            def done(ins):
                n[0] += 1
                ins.then_inc(step, 1)
                dve.wait_ge(step, n[0])

            dve.wait_ge(loaded, 48)
            done(dve.tensor_tensor_reduce(junk[:], x[:], x[:], 1.0, 0.0, ALU.mult, ALU.add, ss[:]))
            done(dve.tensor_scalar(rin[:], ss[:], 1.0 / D, EPS, ALU.mult, ALU.add))
            dve.wait_ge(powed, 1)
            done(dve.tensor_scalar(x[:], x[:], rstd[:], None, ALU.mult))
            dve.wait_ge(turned, 1)
            done(dve.tensor_tensor(xt[:], c.bank[0][:, 0:KD * 8].rearrange("p (k b) -> p k b", b=8),
                                   gn[:].unsqueeze(2).to_broadcast([P, KD, 8]), ALU.mult))
            done(dve.tensor_copy(f[0][:], bf[:]))
            for m, (c0, cw) in enumerate(CH):
                dve.wait_ge(prod, m + 1)
                done(dve.tensor_copy(z[:, c0:c0 + cw], c.bank[1 + m % 2][0:8, 0:cw]))
            done(dve.tensor_tensor(f[1][:], z[:, CF:CF + NF], f[0][:], ALU.add))
            done(dve.tensor_scalar(f[2][:], f[1][:], -1.0, None, ALU.mult))
            done(dve.tensor_tensor(f[3][:], f[1][:], f[2][:], ALU.min))
            done(dve.tensor_scalar(f[2][:], f[1][:], 0.0, None, ALU.min))
            dve.wait_ge(acted, 2)
            done(dve.tensor_tensor(c.lfs[:], f[2][:], f[4][:], ALU.subtract))

        @block.scalar
        def _(act):
            act.wait_ge(step, BASE + len(CH) + 3)
            act.activation(f[0][:], f[3][:], ACT.Exp).then_inc(acted, 1)
            act.wait_ge(acted, 1)
            act.activation(f[4][:], f[0][:], ACT.Ln, bias=1.0).then_inc(acted, 1)

        @block.tensor
        def _(pe):
            pe.wait_ge(step, 3)
            for k in range(KD):
                tr = pe.transpose(c.bank[0][:, k * 8:(k + 1) * 8], x[:, k * P:(k + 1) * P], c.ident[0:8, 0:8])
            tr.then_inc(turned, 1)
            pe.wait_ge(step, 4)
            for m, (c0, cw) in enumerate(CH):
                pe.wait_ge(w_in[m % 3], 16 * (m // 3 + 1))
                if m >= 2:
                    pe.wait_ge(step, BASE + m - 1)
                for k in range(KD):
                    mm = pe.matmul(c.bank[1 + m % 2][0:8, 0:cw], xt[:, k, :], w[:, m % 3, k, 0:cw], start=(k == 0), stop=(k == KD - 1))
                mm.then_inc(prod, 1)


def ssm(nc, c, a, ssm_prompt, ssm_sample):
    NB = 4
    with ExitStack() as s:
        def sb(name, shape, dt=F32):
            return s.enter_context(nc.sbuf_tensor(name, shape, dt))

        def sem(name):
            return s.enter_context(nc.semaphore(name))

        y = sb("ssm_y", [P, NB, STEP, WS])
        gp = sb("ssm_gp", [P, 2, GPW])
        u = sb("ssm_u", [P, 2, NB, SC])
        us = sb("ssm_us", [8, 2, SC])
        ut = sb("ssm_ut", [P, 2, NCH])
        sm = sb("ssm_sm", [P, 2, 2 * SC + 8])
        toep = sb("ssm_toep", [P, 2, SC])
        wj = sb("ssm_wj", [P, 2, SC])
        vc, vs, vr, gs = (sb(n, [P, 2, NCH]) for n in ("ssm_vc", "ssm_vs", "ssm_vr", "ssm_g"))
        cg, sg = sb("ssm_cg", [P, 2, NCH + 1]), sb("ssm_sg", [P, 2, NCH + 1])
        hl = sb("ssm_hl", [P, 2, G])
        h0in = sb("ssm_h0in", [96, 2, NS, 2])
        h0p = sb("ssm_h0p", [96, 2, 2, 2, NS])
        h0, h0s, hn, hm, vsm = (sb(n, [P, 8, G]) for n in ("ssm_h0", "ssm_h0s", "ssm_hn", "ssm_hm", "ssm_vsm"))
        ab = sb("ssm_ab", [P, G, 2])
        yst = sb("ssm_yst", [GC, G, 8])
        hlt = sb("ssm_hlt", [G, 2, P])
        hlo = sb("ssm_hlo", [G, NS, 2])
        hno = sb("ssm_hno", [96, 2, NS, 2])
        g_in = [sem("ssm_in0"), sem("ssm_in1")]
        h_in, prep, prep_pe, zeroed = sem("ssm_h_in"), sem("ssm_prep"), sem("ssm_prep_pe"), sem("ssm_zeroed")
        ut_tr, sm_tr, ut_done, sm_done, toep_done = (sem(n) for n in ("ssm_ut_tr", "ssm_sm_tr", "ssm_ut_d", "ssm_sm_d", "ssm_toep_d"))
        v_done, turned, scanned, cg_done, small = (sem(n) for n in ("ssm_v", "ssm_turned", "ssm_scan", "ssm_cg_d", "ssm_small"))
        y_done, y_out = sem("ssm_y_d"), sem("ssm_y_out")
        tail, tail_pe, ends, stored = sem("ssm_tail"), sem("ssm_tail_pe"), sem("ssm_ends"), sem("ssm_stored")
        block = s.enter_context(nc.Block())
        u_v = c.u_chunks.rearrange("b p (g w) -> g p b w", g=G)
        z_u = c.zs[:, CU:CU + WS].rearrange("b (g c) -> g b c", c=GC)

        @block.sync
        def _(sp):
            sp.dma_start(h0in[:], a["state_ssm"].rearrange("o b g p r -> (o b g) (p r)").rearrange("(t q) w -> q t w", q=96)
                         .rearrange("q t (p r) -> q t p r", r=2)).then_inc(h_in, 16)
            with nc.allow_non_contiguous_dma(reason="two columns of each group"):
                sp.dma_start(ab[:], c.ssm_gp[:, :, O_A1:O_A1 + 2].rearrange("g p w -> p g w")).then_inc(h_in, 16)
            sp.wait_ge(zeroed, 1)
            with sp.Fori(0, G // 2) as i:
                for j in range(2):
                    sp.wait_ge(y_out, at(2, i, j - 1))
                    sp.wait_ge(small, at(2, i, j - 1))
                    sp.dma_start(gp[:, j], c.ssm_gp[2 * i + j]).then_inc(g_in[j], 16)
                    sp.dma_start(u[:, j], u_v[2 * i + j]).then_inc(g_in[j], 16)
                    sp.dma_start(us[:, j, SC - GC:SC], z_u[2 * i + j]).then_inc(g_in[j], 16)
            sp.wait_ge(y_out, at(2, G // 2, 0))
            sp.dma_start(c.y_chunks.rearrange("b p t f -> p b (t f)"), y[:].rearrange("p b t f -> p b (t f)")).then_inc(stored, 16)
            sp.dma_start(c.ys_t.rearrange("(g c) b -> c g b", c=GC), yst[:]).then_inc(stored, 16)
            sp.wait_ge(ends, 5)
            sp.dma_start(ssm_prompt.rearrange("o b g p r -> (o b g) p r"), hlo[:]).then_inc(stored, 16)
            sp.dma_start(ssm_sample.rearrange("o b g p r -> (o b g) (p r)").rearrange("(t q) w -> q t w", q=96), hno[:]
                         .rearrange("q t p r -> q t (p r)")).then_inc(stored, 16)
            sp.wait_ge(stored, 64)

        @block.gpsimd
        def _(pool):
            pool.memset(us[:], 0.0).then_inc(zeroed, 1)

        @block.vector
        def _(dve):
            dve.sem_inc(cg_done, 4)
            dve.sem_inc(small, 2)
            dve.sem_inc(turned, 4)
            dve.sem_inc(toep_done, 2)
            M, A_, S_ = ALU.mult, ALU.add, ALU.subtract
            dve.memset(cg[:, :, 0], 0.0).then_inc(prep, 1)
            dve.memset(sg[:, :, 0], 0.0).then_inc(prep, 1)
            dve.wait_ge(h_in, 32)
            for r in range(2):
                dve.tensor_copy(h0p[:, :, 0, r, :], h0in[:, :, :, r]).then_inc(prep, 1)
                dve.tensor_copy(h0p[:, :, 1, r, :], h0in[:, :, :, 1 - r]).then_inc(prep, 1)
            dve.wait_ge(prep_pe, 1)
            dve.tensor_copy(h0[:].rearrange("p b g -> p (b g)"), c.bank[0][:, 0:8 * G]).then_inc(prep, 1)
            dve.tensor_copy(h0s[:].rearrange("p b g -> p (b g)"), c.bank[1][:, 0:8 * G]).then_inc(prep, 1)
            dve.wait_ge(prep, 8)
            with dve.Fori(0, G // 2) as i:
                for j in range(2):
                    g = 2 * i + j
                    dve.wait_ge(sm_done, at(2, i, j + 1))
                    dve.wait_ge(y_done, at(2, i, j - 1))
                    dve.scalar_tensor_tensor(toep[:, j], c.ident[:], gp[:, j, O_D:O_D + 1], sm[:, j, SC:2 * SC], M, A_)
                    dve.tensor_copy(wj[:, j, 0:HD], sm[:, j, HD:SC])
                    dve.tensor_scalar(wj[:, j, HD:SC], sm[:, j, 0:HD], -1.0, None, M).then_inc(toep_done, 1)
                for j in range(2):
                    g = 2 * i + j
                    cosT, sinT = gp[:, j, O_COS:O_COS + NCH], gp[:, j, O_SIN:O_SIN + NCH]
                    dve.wait_ge(v_done, 2 * i + j + 1)
                    dve.tensor_tensor(vc[:, j], c.bank[4][:], cosT, M).then_inc(turned, 1)
                    dve.tensor_tensor(vs[:, j], c.bank[5][:], sinT, M).then_inc(turned, 1)
                    dve.wait_ge(turned, at(4, i, 2 * j + 2))
                    dve.tensor_tensor(vr[:, j], vc[:, j], vs[:, j], A_).then_inc(scanned, 1)
                    dve.wait_ge(scanned, 4 * i + 2 * j + 1)
                    dve.tensor_tensor_scan(gs[:, j], gp[:, j, O_R8:O_R8 + 1].to_broadcast([P, NCH]), vr[:, j], 0.0, M, A_
                                           ).then_inc(scanned, 1)
                    dve.wait_ge(scanned, 4 * i + 2 * j + 2)
                    dve.wait_ge(y_done, at(2, i, j - 1))
                    dve.tensor_tensor(cg[:, j, 1:NCH + 1], cosT, gs[:, j], M).then_inc(cg_done, 1)
                    dve.tensor_tensor(sg[:, j, 1:NCH + 1], sinT, gs[:, j], M).then_inc(cg_done, 1)
                    dve.wait_ge(cg_done, at(4, i, 2 * j + 2))
                    dve.tensor_copy(hl[:, 0, bass.ds(g, 1)], cg[:, j, NCH:NCH + 1])
                    dve.tensor_copy(hl[:, 1, bass.ds(g, 1)], sg[:, j, NCH:NCH + 1]).then_inc(small, 1)
            bc = [P, 8, G]
            dve.wait_ge(y_out, at(2, G // 2, 0))
            dve.tensor_tensor(hn[:], h0[:], ab[:, :, 0].unsqueeze(1).to_broadcast(bc), M).then_inc(tail, 1)
            dve.tensor_tensor(hm[:], h0s[:], ab[:, :, 1].unsqueeze(1).to_broadcast(bc), M).then_inc(tail, 1)
            dve.wait_ge(tail, 2)
            dve.tensor_tensor(hn[:], hn[:], hm[:], A_).then_inc(tail, 1)
            dve.wait_ge(tail, 3)
            dve.tensor_tensor(hn[:], hn[:], vsm[:], A_).then_inc(tail, 1)
            dve.wait_ge(tail_pe, 1)
            dve.tensor_copy(hlt[:].rearrange("g a w -> g (a w)"), c.bank[0][0:G, 0:2 * P]).then_inc(ends, 1)
            dve.wait_ge(ends, 1)
            dve.tensor_tensor(hlo[:, :, 0], hlt[:, 0, 0:HD], hlt[:, 1, HD:P], S_).then_inc(ends, 1)
            dve.tensor_tensor(hlo[:, :, 1], hlt[:, 0, HD:P], hlt[:, 1, 0:HD], A_).then_inc(ends, 1)
            for r in range(2):
                dve.tensor_copy(hno[:, :, :, r], c.bank[1][0:96, 0:2 * P].rearrange("q (t r p) -> q t p r", t=2, r=2)[:, :, :, r]
                                ).then_inc(ends, 1)

        @block.scalar
        def _(act):
            act.sem_inc(sm_done, 2)
            act.sem_inc(ut_done, 2)
            act.sem_inc(y_out, 2)
            with act.Fori(0, G // 2) as i:
                for j in range(2):
                    act.wait_ge(ut_tr, 2 * i + j + 1)
                    act.wait_ge(y_done, at(2, i, j - 1))
                    act.activation(ut[:, j], c.bank[j][:], ACT.Copy).then_inc(ut_done, 1)
                    act.wait_ge(sm_tr, 2 * i + j + 1)
                    act.activation(sm[:, j], c.bank[2 + j][:, 0:2 * SC + 8], ACT.Copy).then_inc(sm_done, 1)
                for j in range(2):
                    g = 2 * i + j
                    act.wait_ge(y_done, at(2, i, j + 1))
                    act.activation(vsm[:, :, g], c.bank[7][:, 0:8], ACT.Copy)
                    act.activation(yst[:, g, :], c.bank[7][0:GC, 16:24], ACT.Gelu)
                    act.activation(y[:, :, :, bass.ds(g * GC, GC)], c.bank[6][:].rearrange("p (b t c) -> p b t c", b=NB, c=GC),
                                   ACT.Gelu).then_inc(y_out, 1)

        @block.tensor
        def _(pe):
            pe.sem_inc(y_done, 2)
            pe.wait_ge(prep, 6)
            for k in range(2):
                for t in range(2):
                    tr = pe.transpose(c.bank[k][:, t * 96:(t + 1) * 96], h0p[:, t, k, :, :].rearrange("q r p -> q (r p)"), c.ident[0:96, 0:96])
            tr.then_inc(prep_pe, 1)
            pe.wait_ge(prep, 8)
            with pe.Fori(0, G // 2) as i:
                for j in range(2):
                    pe.wait_ge(g_in[j], 48 * (i + 1))
                    pe.wait_ge(ut_done, at(2, i, j - 1))
                    for b in range(NB):
                        tr = pe.transpose(c.bank[j][:, b * P:(b + 1) * P], u[:, j, b, :], c.ident[:])
                    tr.then_inc(ut_tr, 1)
                    pe.wait_ge(sm_done, at(2, i, j - 1))
                    small_b = c.bank[2 + j]
                    pe.transpose(small_b[:, 0:SC], gp[:, j, O_R:O_R + SC], c.ident[:])
                    for t in range(STEP):
                        w0 = O_R + (STEP - 1 - t) * GC
                        pe.matmul(small_b[:, SC + t * GC:SC + (t + 1) * GC], gp[:, j, w0:w0 + SC], gp[:, j, O_CC:O_CC + GC],
                                  start=True, stop=True)
                    pe.transpose(small_b[:, 2 * SC:2 * SC + 8], us[:, j, :], c.ident[0:8, 0:8]).then_inc(sm_tr, 1)
                for j in range(2):
                    g = 2 * i + j
                    pe.wait_ge(ut_done, at(2, i, j + 1))
                    pe.wait_ge(toep_done, at(2, i, j + 1))
                    pe.wait_ge(turned, at(4, i, 2 * j))
                    pe.matmul(c.bank[4][:], sm[:, j, 0:SC], ut[:, j], start=True, stop=True)
                    pe.matmul(c.bank[5][:], wj[:, j], ut[:, j], start=True, stop=True).then_inc(v_done, 1)
                for j in range(2):
                    g = 2 * i + j
                    w1, w2 = gp[:, j, O_W1:O_W1 + SC], gp[:, j, O_W2:O_W2 + SC]
                    pe.wait_ge(cg_done, at(4, i, 2 * j + 2))
                    pe.wait_ge(y_out, at(2, i, j))
                    pe.matmul(c.bank[7][:, 0:8], sm[:, j, 0:SC], sm[:, j, 2 * SC:], start=True, stop=True)
                    for b in range(NB):
                        dst = c.bank[6][:, b * P:(b + 1) * P]
                        pe.matmul(dst, ut[:, j, b * P:(b + 1) * P], toep[:, j], start=True, stop=False)
                        pe.matmul(dst, cg[:, j, b * P:(b + 1) * P], w1, start=False, stop=False)
                        pe.matmul(dst, sg[:, j, b * P:(b + 1) * P], w2, start=False, stop=True)
                    dst = c.bank[7][0:GC, 16:24]
                    pe.matmul(dst, toep[:, j, SC - GC:SC], sm[:, j, 2 * SC:], start=True, stop=False)
                    pe.matmul(dst, w1[:, 0:GC], h0[:, :, g], start=False, stop=True).then_inc(y_done, 1)
            pe.wait_ge(small, at(2, G // 2, 0))
            pe.wait_ge(tail, 4)
            for r in range(2):
                pe.transpose(c.bank[0][0:G, r * P:(r + 1) * P], hl[:, r, :], c.ident[:])
            for t in range(2):
                tr = pe.transpose(c.bank[1][0:96, t * P:(t + 1) * P], hn[:].rearrange("p b g -> p (b g)")[:, t * 96:(t + 1) * 96], c.ident[:])
            tr.then_inc(tail_pe, 1)


def sample_attend(nc, c, a):
    NBS, NPG = a["page_table"].shape
    NPOOL = a["cache_k"].shape[1]
    NMT = NMEM // P
    BH, BM = NBS * NF, NBS * NM
    with ExitStack() as s:
        def sb(name, shape, dt=F32):
            return s.enter_context(nc.sbuf_tensor(name, shape, dt))

        def sem(name):
            return s.enter_context(nc.semaphore(name))

        pages = sb("at_pages", [1, NBS * NPG], I32)
        z = sb("at_z", [NBS, DIN])
        kb, vb = sb("at_k", [P, 2, NPG, WF]), sb("at_v", [P, 2, NPG, WF])
        qb = sb("at_qb", [P, 2, WF])
        prod = sb("at_prod", [P, NPG, WF])
        lf = sb("at_lf", [P, NBS, NPG, NF])
        lfx = sb("at_lfx", [P, NBS, NPG, NF])
        sc = sb("at_s", [P, NBS, NPG, NF])
        mk, mv = sb("at_mk", [P, NBS, NMT, WM]), sb("at_mv", [P, NBS, NMT, WM])
        mq = sb("at_mq", [P, NBS, WM])
        ms = sb("at_ms", [P, NBS, NMT, NM])
        mx = sb("at_mx", [P, BH + BM])
        mxa = sb("at_mxa", [P, BH + BM])
        qk = sb("at_qk", [NBS, WF])
        new = sb("at_new", [NBS, 2, NF])
        newd = sb("at_newd", [NBS, 2, NBS, NF])
        newb = sb("at_newb", [P, 2, NBS, NF])
        pn = sb("at_pn", [P, NBS, NF])
        part = sb("at_part", [P, BH + BM])
        rt = sb("at_rt", [P, BH + BM])
        zt = sb("at_zt", [P, 11, NBS])
        zg = sb("at_zg", [P, 8, NBS])
        of = sb("at_of", [P, 3, NBS])
        t0 = sb("at_t0", [P, 3, NBS])
        loaded, m_in, p_in, lf_in = sem("at_loaded"), sem("at_m_in"), sem("at_p_in"), sem("at_lf_in")
        k_in, v_in = [sem("at_k0"), sem("at_k1")], [sem("at_v0"), sem("at_v1")]
        step, pe_, act_, pool_ = sem("at_step"), sem("at_pe"), sem("at_act"), sem("at_pool")
        k_mul, k_red, ov, o_out = sem("at_kmul"), sem("at_kred"), sem("at_ov"), sem("at_oo")
        block = s.enter_context(nc.Block())
        ck = a["cache_k"].rearrange("o n p h d -> (o n) p (h d)")
        cv = a["cache_v"].rearrange("o n p h d -> (o n) p (h d)")
        cl = a["cache_logf"].rearrange("o n p h -> (o n) p h")
        z_q = c.zs[:, 0:WF]
        LOADS = 16 * 2

        NEWD_AT, LFX_AT, MAX_AT, EXP_AT, SUM_AT, NORM_AT = 6, 15, 23, 27, 30, 35

        @block.sync
        def _(sp):
            sp.dma_start(pages[:], a["page_table"].rearrange("(o b) n -> o (b n)", o=1)).then_inc(p_in, 16)
            sp.dma_start(z[:], c.zs).then_inc(loaded, 16)
            sp.dma_start(mq[:], c.zs[:, CQM:CQM + WM].partition_broadcast(P)).then_inc(loaded, 16)
            sp.dma_start(mk[:], a["cache_mem_k"].rearrange("o b (t p) h d -> p (o b) t (h d)", p=P)).then_inc(m_in, 16)
            sp.dma_start(mv[:], a["cache_mem_v"].rearrange("o b (t p) h d -> p (o b) t (h d)", p=P)).then_inc(m_in, 16)
            sp.wait_ge(p_in, 16)
            with sp.Fori(0, NBS // 2) as i:
                for j in range(2):
                    b = 2 * i + j
                    sp.wait_ge(k_mul, at(2, i, j - 1))
                    sp.dma_start(qb[:, j], z_q[b].partition_broadcast(P)).then_inc(k_in[j], 16)
                    for n in range(NPG):
                        pid = sp.value_load(pages[0:1, bass.ds(b * NPG + n, 1)], min_val=0, max_val=NPOOL - 1)
                        sp.dma_start(kb[:, j, n, :], ck[pid]).then_inc(k_in[j], 16)

        @block.scalar
        def _(act):
            act.wait_ge(p_in, 16)
            with nc.allow_non_contiguous_dma(reason="six log f a key"):
                with act.Fori(0, NBS) as b:
                    for n in range(NPG):
                        pid = act.value_load(pages[0:1, bass.ds(b * NPG + n, 1)], min_val=0, max_val=NPOOL - 1)
                        act.dma_start(lf[:, b, n, :], cl[pid]).then_inc(lf_in, 16)
            act.wait_ge(pe_, 1)
            act.activation(zg[:], c.bank[0][:, 3 * NBS:11 * NBS].rearrange("p (k b) -> p k b", b=NBS), ACT.Silu).then_inc(act_, 1)
            act.wait_ge(step, EXP_AT)
            act.activation(sc[:], sc[:], ACT.Exp).then_inc(act_, 1)
            act.activation(ms[:], ms[:], ACT.Exp, scale=HD ** -0.5).then_inc(act_, 1)
            act.activation(pn[:], pn[:], ACT.Exp).then_inc(act_, 1)
            with act.Fori(0, NBS // 2) as i:
                for j in range(2):
                    act.wait_ge(ov, at(2, i, j - 1))
                    for n in range(NPG):
                        pid = act.value_load(pages[0:1, bass.ds((2 * i + j) * NPG + n, 1)], min_val=0, max_val=NPOOL - 1)
                        act.dma_start(vb[:, j, n, :], cv[pid]).then_inc(v_in[j], 16)

        @block.gpsimd
        def _(pool):
            pool.wait_ge(step, MAX_AT)
            pool.partition_all_reduce(mxa[:], mx[:], P, bass.bass_isa.ReduceOp.max).then_inc(pool_, 1)


        @block.vector
        def _(dve):
            n = [0]
            M, A_, S_ = ALU.mult, ALU.add, ALU.subtract

            def done(ins):
                n[0] += 1
                ins.then_inc(step, 1)
                dve.wait_ge(step, n[0])

            dve.sem_inc(k_mul, 2)
            dve.wait_ge(loaded, LOADS)
            done(dve.tensor_copy(new[:, 1, :], c.lfs[:]))
            done(dve.tensor_tensor(qk[:], z[:, CQ:CQ + WF], z[:, CK:CK + WF], M))
            done(dve.tensor_reduce(new[:, 0, :], qk[:].rearrange("b (h d) -> b h d", d=HD), AX.X, A_))
            done(dve.tensor_scalar(new[:, 0, :], new[:, 0, :], HD ** -0.5, None, M))
            for k in range(2):
                done(dve.tensor_tensor(newd[:, k], c.ident[0:NBS, 0:NBS].unsqueeze(2).to_broadcast([NBS, NBS, NF]),
                                       new[:, k, :].unsqueeze(1).to_broadcast([NBS, NBS, NF]), M))
            assert n[0] == NEWD_AT
            dve.wait_ge(lf_in, 16 * NBS * NPG)
            done(dve.memset(lfx[:, :, NPG - 1, :], 0.0))
            for g in range(NPG - 2, -1, -1):
                done(dve.tensor_tensor(lfx[:, :, g, :], lfx[:, :, g + 1, :], lf[:, :, g + 1, :], A_))
            dve.wait_ge(pe_, 2)
            done(dve.tensor_copy(newb[:].rearrange("p k b h -> p (k b h)"), c.bank[1][:, 0:2 * BH]))
            assert n[0] == LFX_AT
            with dve.Fori(0, NBS // 2) as i:
                for j in range(2):
                    dve.wait_ge(k_in[j], 16 * (NPG + 1) * (i + 1))
                    dve.tensor_tensor(prod[:], kb[:, j], qb[:, j, :].unsqueeze(1).to_broadcast([P, NPG, WF]), M).then_inc(k_mul, 1)
                    dve.wait_ge(k_mul, at(2, i, j + 1))
                    dve.tensor_reduce(sc[:, 2 * i + j], prod[:].rearrange("p n (h d) -> p n h d", d=HD), AX.X, A_).then_inc(k_red, 1)
                    dve.wait_ge(k_red, 2 * i + j + 1)
            dve.wait_ge(pe_, 3)
            bf = c.bank[2][:, 0:NBS * NPG * NF]
            scf = sc[:].rearrange("p b n h -> p (b n h)")
            done(dve.scalar_tensor_tensor(scf, scf, HD ** -0.5, bf, M, A_))
            done(dve.tensor_tensor(sc[:], sc[:], newb[:, 1].unsqueeze(2).to_broadcast([P, NBS, NPG, NF]), A_))
            done(dve.tensor_reduce(mx[:, 0:BH].rearrange("p (b h) -> p b h", h=NF), sc[:].rearrange("p b n h -> p b h n"), AX.X, ALU.max))
            dve.wait_ge(m_in, 32)
            for t in range(NMT):
                done(dve.tensor_tensor(prod[:, :, 0:WM], mk[:, :, t, :], mq[:], M))
                done(dve.tensor_reduce(ms[:, :, t, :], prod[:, :, 0:WM].rearrange("p b (h d) -> p b h d", d=HD), AX.X, A_))
            done(dve.tensor_reduce(mx[:, BH:].rearrange("p (b h) -> p b h", h=NM), ms[:].rearrange("p b t h -> p b h t"), AX.X, ALU.max))
            assert n[0] == MAX_AT, n[0]
            dve.wait_ge(pool_, 1)
            m3 = mxa[:, 0:BH].rearrange("p (b h) -> p b h", h=NF)
            mm3 = mxa[:, BH:].rearrange("p (b h) -> p b h", h=NM)
            done(dve.tensor_tensor(m3, m3, newb[:, 0], ALU.max))
            done(dve.tensor_tensor(sc[:], sc[:], m3.unsqueeze(2).to_broadcast([P, NBS, NPG, NF]), S_))
            done(dve.tensor_tensor(ms[:], ms[:], mm3.unsqueeze(2).to_broadcast([P, NBS, NMT, NM]), S_))
            done(dve.tensor_tensor(pn[:], newb[:, 0], m3, S_))
            assert n[0] == EXP_AT, n[0]
            dve.wait_ge(act_, 4)
            done(dve.tensor_reduce(part[:, 0:BH].rearrange("p (b h) -> p b h", h=NF), sc[:].rearrange("p b n h -> p b h n"), AX.X, A_))
            done(dve.tensor_reduce(part[:, BH:].rearrange("p (b h) -> p b h", h=NM), ms[:].rearrange("p b t h -> p b h t"), AX.X, A_))
            done(dve.tensor_copy(zt[:, 0:3], c.bank[0][:, 0:3 * NBS].rearrange("p (k b) -> p k b", b=NBS)))
            assert n[0] == SUM_AT
            dve.wait_ge(pe_, 4)
            r3, q3 = rt[:, 0:BH].rearrange("p (b h) -> p b h", h=NF), rt[:, BH:].rearrange("p (b h) -> p b h", h=NM)
            done(dve.tensor_tensor(rt[:, 0:BH], c.bank[3][:, 0:BH], pn[:].rearrange("p b h -> p (b h)"), A_))
            done(dve.tensor_copy(rt[:, BH:], c.bank[3][:, BH:BH + BM]))
            done(dve.reciprocal(rt[:], rt[:]))
            done(dve.tensor_tensor(sc[:], sc[:], r3.unsqueeze(2).to_broadcast([P, NBS, NPG, NF]), M))
            done(dve.tensor_tensor(ms[:], ms[:], q3.unsqueeze(2).to_broadcast([P, NBS, NMT, NM]), M))
            assert n[0] == NORM_AT
            done(dve.tensor_tensor(pn[:], pn[:], r3, M))
            for r in range(2):
                rows = slice(HD * r, HD * (r + 1))
                done(dve.tensor_tensor(t0[rows], zt[rows, 0:3], pn[rows].rearrange("p b (k r) -> p r k b", r=2)[:, r], M))
            with dve.Fori(0, NBS // 2) as i:
                for j in range(2):
                    b = 2 * i + j
                    dve.wait_ge(ov, at(2, i, j + 1))
                    o2 = c.bank[4 + j][:, 0:NF].rearrange("p (k r) -> p k r", r=2)
                    for r in range(2):
                        rows = slice(HD * r, HD * (r + 1))
                        dve.tensor_copy(of[rows, :, b], o2[rows, :, r]).then_inc(o_out, 1)
            dve.wait_ge(o_out, 4 + 2 * NBS)
            done(dve.tensor_tensor(of[:], of[:], t0[:], A_))
            done(dve.tensor_tensor(c.mix_s[:, 0:3], of[:], zg[:, 0:3], M))
            dve.wait_ge(pe_, 5)
            om = c.bank[6][:, 0:NBS * NM].rearrange("p (b k r) -> p k b r", r=2, k=2)
            for r in range(2):
                rows = slice(HD * r, HD * (r + 1))
                done(dve.tensor_tensor(c.mix_s[rows, 6:8], om[rows, :, :, r], zg[rows, 6:8], M))
            done(dve.tensor_copy(c.mix_s[:, 3:6], zg[:, 3:6]))

        @block.tensor
        def _(pe):
            pe.sem_inc(ov, 2)
            pe.sem_inc(o_out, 4)
            pe.wait_ge(loaded, LOADS)
            cols = [CV + k * P for k in range(3)] + [CGA + k * P for k in range(3)] + [CGS + k * P for k in range(3)] + \
                   [CGM + k * P for k in range(2)]
            for k, c0 in enumerate(cols):
                tr = pe.transpose(c.bank[0][:, k * NBS:(k + 1) * NBS], z[:, c0:c0 + P], c.ident[0:NBS, 0:NBS])
            tr.then_inc(pe_, 1)
            pe.wait_ge(step, NEWD_AT)
            pe.matmul(c.bank[1][:, 0:2 * BH], c.ones[0:NBS, :], newd[:].rearrange("q k b h -> q (k b h)"), start=True, stop=True
                      ).then_inc(pe_, 1)
            pe.wait_ge(step, LFX_AT)
            bf = c.bank[2][:, 0:NBS * NPG * NF]
            pe.matmul(bf, c.lower_strict[:], lf[:].rearrange("p b n h -> p (b n h)"), start=True, stop=False)
            pe.matmul(bf, c.ones[:], lfx[:].rearrange("p b n h -> p (b n h)"), start=False, stop=True).then_inc(pe_, 1)
            pe.wait_ge(step, SUM_AT)
            pe.matmul(c.bank[3][:, 0:BH + BM], c.ones[:], part[:], start=True, stop=True).then_inc(pe_, 1)
            pe.wait_ge(step, NORM_AT)
            for b in range(NBS):
                for k in range(2):
                    dst = c.bank[6][:, b * NM + 2 * k:b * NM + 2 * k + 2]
                    for t in range(NMT):
                        mm = pe.matmul(dst, mv[:, b, t, k * P:(k + 1) * P], ms[:, b, t, 2 * k:2 * k + 2], start=(t == 0), stop=(t == NMT - 1))
            mm.then_inc(pe_, 1)
            with pe.Fori(0, NBS // 2) as i:
                for j in range(2):
                    b = 2 * i + j
                    pe.wait_ge(v_in[j], 16 * NPG * (i + 1))
                    pe.wait_ge(o_out, at(4, i, 2 * (j - 1)))
                    for k in range(3):
                        for g in range(NPG):
                            mm = pe.matmul(c.bank[4 + j][:, 2 * k:2 * k + 2], vb[:, j, g, k * P:(k + 1) * P],
                                           sc[:, b, g, 2 * k:2 * k + 2], start=(g == 0), stop=(g == NPG - 1))
                    mm.then_inc(ov, 1)


def mix_out(nc, c, a, y_prompt, y_sample):
    NB, TB = T // 512, 512
    NT = TB // P
    NKS = WS // P
    with ExitStack() as s:
        def sb(name, shape, dt=F32):
            return s.enter_context(nc.sbuf_tensor(name, shape, dt))

        def sem(name):
            return s.enter_context(nc.semaphore(name))

        whi, wlo = sb("wo_hi", [P, KD, D], F32R), sb("wo_lo", [P, KD, D], F32R)
        wraw = sb("wo_raw", [P, 2, D])
        wg = sb("w_glu", [P, NKS, WS])
        bg = sb("b_glu", [P, NKS])
        gf = sb("g_fin", [P, D])
        am = sb("mx_am", [P, 5, TB])
        gate = sb("mx_gate", [P, NKS, TB])
        yc = sb("mx_y", [HD, STEP, WS])
        st = sb("mx_st", [P, NKS, TB])
        sig = sb("mx_sig", [P, NKS, TB])
        mhi, mlo = sb("mx_hi", [P, 2, KD, TB], F32R), sb("mx_lo", [P, 2, KD, TB], F32R)
        xr = sb("mx_x", [P, 2, D])
        xo = sb("mx_xo", [P, 2, D])
        stats = sb("mx_stats", [P, 3, 2])
        ss, rin, rstd = (stats[:, k] for k in range(3))
        junk = sb("mx_junk", [P, D], BF16)
        yss = sb("mx_ys", [P, NKS, 8])
        sgs = sb("mx_sgs", [P, NKS, 8])
        shi, slo = sb("mx_shi", [P, KD, 8], F32R), sb("mx_slo", [P, KD, 8], F32R)
        xs = wraw[0:8, 0]
        w_in = [sem("wo_in0"), sem("wo_in1")]
        p_in, xs_in, w_hi, w_split = sem("mx_p_in"), sem("mx_xs_in"), sem("wo_hi_d"), sem("wo_split")
        step, spe, sact, spool = sem("mx_step"), sem("mx_spe"), sem("mx_sact"), sem("mx_spool")
        in_ = sem("mx_in")
        tr_done, st_done, glu_done, sig_done = sem("mx_tr"), sem("mx_st_d"), sem("mx_glu"), sem("mx_sig_d")
        s_done, hi_done, lo_done = sem("mx_s_d"), sem("mx_hi_d"), sem("mx_lo_d")
        x_in = [sem("mx_x0"), sem("mx_x1")]
        y_st = [sem("mx_y0"), sem("mx_y1")]
        op_done, xo_done, sq_done, mean_done, rs_done, y_done = (
            sem(n) for n in ("mx_op", "mx_xo_d", "mx_sq", "mx_mean", "mx_rs", "mx_y_d"))
        block = s.enter_context(nc.Block())
        wo = a["w_out"].rearrange("o (k p) n -> (o k) p n", p=P)
        m_v = c.mix_t.rearrange("(k p) (b t) -> b p k t", p=P, t=TB)
        g_v = c.gate_t.rearrange("(k p) (b t) -> b p k t", p=P, t=TB)
        y_v = c.y_chunks.rearrange("b (a p) t f -> (b a) p t f", p=HD)
        x_v = a["x_prompt"].rearrange("o (b t p) d -> (o b) t p d", p=P, t=NT)
        o_v = y_prompt.rearrange("o (b t p) d -> (o b) t p d", p=P, t=NT)
        M, A_, S_ = ALU.mult, ALU.add, ALU.subtract

        def schedule(engine, ready, project, gate_samples, project_samples):
            ready(0, 0)
            with engine.Fori(0, NB // 2 - 1) as i:
                ready(2 * i + 1, 1)
                project(2 * i, 0)
                ready(2 * i + 2, 0)
                project(2 * i + 1, 1)
            ready(NB - 1, 1)
            gate_samples()
            project(NB - 2, 0)
            project_samples()
            project(NB - 1, 1)

        GATED_AT, SPLIT_AT, ADDED_AT, MEAN_AT, LAST_AT = 6, 8, 10, 12, 13

        @block.sync
        def _(sp):
            with nc.allow_non_contiguous_dma(reason="384 biases"):
                sp.dma_start(bg[:], a["b_glu"].rearrange("o (k p) -> p (o k)", p=P)).then_inc(p_in, 16)
            sp.dma_start(wg[:], a["w_glu"].rearrange("o (k p) n -> p (o k) n", p=P)).then_inc(p_in, 16)
            sp.dma_start(gf[:], a["g_final"].partition_broadcast(P)).then_inc(p_in, 16)
            sp.dma_start(yss[:], c.ys_t.rearrange("(k p) b -> p k b", p=P)).then_inc(p_in, 16)

            def ready(n, j):
                sp.wait_ge(lo_done, at(KD, n, 0))
                sp.dma_start(am[:, 0:3], m_v[n, :, 0:3, :]).then_inc(in_, 16)
                sp.dma_start(am[:, 3:5], m_v[n, :, 6:8, :]).then_inc(in_, 16)
                sp.dma_start(gate[:], g_v[n, :, 3:6, :]).then_inc(in_, 16)
                sp.dma_start(yc[:], y_v[n]).then_inc(in_, 16)

            def project(n, j):
                for t in range(NT):
                    sp.wait_ge(xo_done, at(NT, n, t - 1))
                    sp.dma_start(xr[:, t % 2], x_v[n, t]).then_inc(x_in[t % 2], 16)

            schedule(sp, ready, project, lambda: None, lambda: None)

        @block.gpsimd
        def _(pool):
            for k in range(KD):
                if k >= 2:
                    pool.wait_ge(w_split, k - 1)
                pool.dma_start(wraw[:, k % 2], wo[k]).then_inc(w_in[k % 2], 16)
            pool.wait_ge(w_split, KD)
            pool.dma_start(xs, a["x_sample"].rearrange("b o d -> (b o) d")).then_inc(xs_in, 16)

            def means(n):
                for t in range(NT):
                    pool.wait_ge(mean_done, NT * n + t + 1)
                    pool.tensor_tensor(rstd[:, t % 2:t % 2 + 1], rin[:, t % 2:t % 2 + 1], c.minus_half[:, 0:1], ALU.pow
                                       ).then_inc(rs_done, 1)

            with pool.Fori(0, NB - 1) as n:
                means(n)
            pool.wait_ge(step, MEAN_AT)
            pool.tensor_tensor(rstd[0:8, 0:1], rin[0:8, 0:1], c.minus_half[0:8, 0:1], ALU.pow).then_inc(spool, 1)
            means(NB - 1)

        @block.vector
        def _(dve):
            n_ = [0]

            def done(ins):
                n_[0] += 1
                ins.then_inc(step, 1)
                dve.wait_ge(step, n_[0])

            dve.sem_inc(lo_done, KD)
            dve.sem_inc(xo_done, NT)
            for k in range(KD):
                dve.wait_ge(w_in[k % 2], 16 * (k // 2 + 1))
                dve.tensor_copy(whi[:, k, :], wraw[:, k % 2]).then_inc(w_hi, 1)
                dve.wait_ge(w_hi, k + 1)
                dve.tensor_tensor(wlo[:, k, :], wraw[:, k % 2], whi[:, k, :].bitcast(F32), S_).then_inc(w_split, 1)

            def ready(n, j):
                for k in range(NKS):
                    dve.wait_ge(sig_done, NKS * n + k + 1)
                    dve.tensor_tensor(sig[:, k], sig[:, k], st[:, k], M).then_inc(s_done, 1)
                    dve.wait_ge(s_done, 2 * NKS * n + 2 * k + 1)
                    dve.tensor_tensor(sig[:, k], sig[:, k], gate[:, k], M).then_inc(s_done, 1)
                for m in range(KD):
                    src = am[:, m] if m < 3 else (sig[:, m - 3] if m < 6 else am[:, m - 3])
                    dve.wait_ge(hi_done, at(KD, n, m + 1))
                    dve.tensor_tensor(mlo[:, j, m], src, mhi[:, j, m].bitcast(F32), S_).then_inc(lo_done, 1)

            def project(n, j):
                def finish(t):
                    q = t % 2
                    dve.wait_ge(sq_done, at(NT, n, t + 1))
                    dve.tensor_scalar(rin[:, q:q + 1], ss[:, q:q + 1], 1.0 / D, EPS, M, A_).then_inc(mean_done, 1)
                    dve.wait_ge(rs_done, NT * n + t + 1)
                    dve.scalar_tensor_tensor(xo[:, q], xo[:, q], rstd[:, q:q + 1], gf[:], M, M).then_inc(y_done, 1)

                for t in range(NT):
                    q = t % 2
                    dve.wait_ge(x_in[q], 16 * (NT // 2) * n + 16 * (t // 2 + 1))
                    dve.wait_ge(y_st[q], at(16 * NT // 2, n, 16 * (t // 2)))
                    for h in range(2):
                        dve.wait_ge(op_done, 2 * NT * n + 2 * t + h + 1)
                        ins = dve.tensor_tensor(xo[:, q, 512 * h:512 * (h + 1)], xr[:, q, 512 * h:512 * (h + 1)],
                                                c.bank[4 + 2 * q + h][:], A_)
                    ins.then_inc(xo_done, 1)
                    if t:
                        finish(t - 1)
                finish(NT - 1)

            def gate_samples():
                dve.wait_ge(p_in, 64)
                dve.wait_ge(sact, NKS)
                for k in range(NKS):
                    done(dve.tensor_tensor(sgs[:, k], sgs[:, k], yss[:, k], M))
                    done(dve.tensor_tensor(c.mix_s[:, 3 + k], c.mix_s[:, 3 + k], sgs[:, k], M))
                assert n_[0] == GATED_AT
                done(dve.tensor_copy(shi[:], c.mix_s[:]))
                done(dve.tensor_tensor(slo[:], c.mix_s[:], shi[:].bitcast(F32), S_))
                assert n_[0] == SPLIT_AT

            def project_samples():
                dve.wait_ge(xs_in, 16)
                for h in range(2):
                    dve.wait_ge(spe, NKS + 1 + h)
                    done(dve.tensor_tensor(xs[:, 512 * h:512 * (h + 1)], xs[:, 512 * h:512 * (h + 1)], c.bank[4 + h][0:8, :], A_))
                assert n_[0] == ADDED_AT
                done(dve.tensor_tensor_reduce(junk[0:8], xs, xs, 1.0, 0.0, M, A_, ss[0:8, 0:1]))
                done(dve.tensor_scalar(rin[0:8, 0:1], ss[0:8, 0:1], 1.0 / D, EPS, M, A_))
                assert n_[0] == MEAN_AT
                dve.wait_ge(spool, 1)
                done(dve.scalar_tensor_tensor(xs, xs, rstd[0:8, 0:1], gf[0:8, :], M, M))
                assert n_[0] == LAST_AT

            schedule(dve, ready, project, gate_samples, project_samples)

        @block.scalar
        def _(act):
            for j in range(2):
                act.sem_inc(y_st[j], 16 * NT // 2)
            act.sem_inc(hi_done, KD)
            act.sem_inc(sq_done, NT)
            act.wait_ge(p_in, 64)

            def ready(n, j):
                act.wait_ge(in_, 64 * n + 64)
                for k in range(NKS):
                    act.wait_ge(tr_done, NKS * n + k + 1)
                    act.activation(st[:, k].rearrange("p (c t) -> p t c", t=STEP), c.bank[k % 2][:].rearrange("p (t c) -> p t c", t=STEP),
                                   ACT.Copy).then_inc(st_done, 1)
                for k in range(NKS):
                    act.wait_ge(glu_done, NKS * n + k + 1)
                    act.activation(sig[:, k], c.bank[2 + k % 2][:], ACT.Sigmoid, bias=bg[:, k:k + 1]).then_inc(sig_done, 1)
                for m in range(KD):
                    src = am[:, m] if m < 3 else (sig[:, m - 3] if m < 6 else am[:, m - 3])
                    if 3 <= m < 6:
                        act.wait_ge(s_done, 2 * NKS * n + 2 * (m - 3) + 2)
                    act.activation(mhi[:, j, m], src, ACT.Copy).then_inc(hi_done, 1)

            def project(n, j):
                def store(t):
                    act.wait_ge(y_done, NT * n + t + 1)
                    act.dma_start(o_v[n, t], xo[:, t % 2]).then_inc(y_st[t % 2], 16)

                for t in range(NT):
                    q = t % 2
                    act.wait_ge(xo_done, at(NT, n, t + 1))
                    act.wait_ge(sq_done, at(NT, n, t))
                    act.activation(junk[:], xo[:, q], ACT.Square, accum_out=ss[:, q:q + 1]).then_inc(sq_done, 1)
                    if t:
                        store(t - 1)
                store(NT - 1)

            def gate_samples():
                for e in range(NKS):
                    act.wait_ge(spe, e + 1)
                    act.activation(sgs[:, e], c.bank[e][:, 0:8], ACT.Sigmoid, bias=bg[:, e:e + 1]).then_inc(sact, 1)

            def project_samples():
                act.wait_ge(step, LAST_AT)
                act.dma_start(y_sample.rearrange("b o d -> (b o) d"), xs).then_inc(sact, 16)

            schedule(act, ready, project, gate_samples, project_samples)
            for j in range(2):
                act.wait_ge(y_st[j], at(16 * NT // 2, NB, 0))
            act.wait_ge(sact, NKS + 16)

        @block.tensor
        def _(pe):
            pe.wait_ge(p_in, 64)

            def ready(n, j):
                pe.wait_ge(in_, 64 * n + 64)
                for k in range(NKS):
                    if k == 0:
                        pe.wait_ge(lo_done, at(KD, n, 0))
                    elif k == 2:
                        pe.wait_ge(st_done, NKS * n + 1)
                    for t in range(STEP):
                        tr = pe.matmul(c.bank[k % 2][:, t * HD:(t + 1) * HD], yc[:, t, k * P:(k + 1) * P], c.ident[0:HD, 0:HD],
                                       start=True, stop=True)
                    tr.then_inc(tr_done, 1)
                pe.wait_ge(st_done, NKS * n + NKS)
                for e in range(NKS):
                    if e == 2:
                        pe.wait_ge(sig_done, NKS * n + 1)
                    for k in range(NKS):
                        mm = pe.matmul(c.bank[2 + e % 2][:], wg[:, k, e * P:(e + 1) * P], st[:, k], start=(k == 0), stop=(k == NKS - 1))
                    mm.then_inc(glu_done, 1)

            def project(n, j):
                pe.wait_ge(w_split, KD)
                pe.wait_ge(lo_done, at(KD, n, KD))
                for t in range(NT):
                    pe.wait_ge(xo_done, at(NT, n, t - 1))
                    for h in range(2):
                        for k in range(KD):
                            for ms_, ws_ in ((mhi, whi), (mlo, whi), (mhi, wlo)):
                                mm = pe.matmul(c.bank[4 + 2 * (t % 2) + h][:], ms_[:, j, k, t * P:(t + 1) * P],
                                               ws_[:, k, 512 * h:512 * (h + 1)], start=(k == 0 and ws_ is whi and ms_ is mhi),
                                               stop=(k == KD - 1 and ws_ is wlo))
                        mm.then_inc(op_done, 1)

            def gate_samples():
                pe.wait_ge(sig_done, NKS * NB)
                for e in range(NKS):
                    for k in range(NKS):
                        mm = pe.matmul(c.bank[e][:, 0:8], wg[:, k, e * P:(e + 1) * P], yss[:, k, :], start=(k == 0), stop=(k == NKS - 1))
                    mm.then_inc(spe, 1)

            def project_samples():
                pe.wait_ge(xo_done, at(NT, NB - 1, 0))
                pe.wait_ge(step, SPLIT_AT)
                for h in range(2):
                    for k in range(KD):
                        for ms_, ws_ in ((shi, whi), (slo, whi), (shi, wlo)):
                            mm = pe.matmul(c.bank[4 + h][0:8, :], ms_[:, k, :], ws_[:, k, 512 * h:512 * (h + 1)],
                                           start=(k == 0 and ws_ is whi and ms_ is shi), stop=(k == KD - 1 and ws_ is wlo))
                    mm.then_inc(spe, 1)
                pe.wait_ge(step, ADDED_AT)

            schedule(pe, ready, project, gate_samples, project_samples)




def build(nc, a, o):
    c = Core()

    def scratch(name, shape):
        return nc.dram_tensor(name, shape, F32).ap()

    c.q_t = scratch("q_t", (WF, T))
    c.qm_t = scratch("qm_t", (WM, T))
    c.gate_t = scratch("gate_t", (D, T))
    c.mix_t = scratch("mix_t", (D, T))
    c.u_chunks = scratch("u_chunks", (4, P, G * 8 * GC))
    c.y_chunks = scratch("y_chunks", (4, P, 8, WS))
    c.negc_rows = scratch("negc_rows", (NF, T))
    c.ssm_gp = scratch("ssm_consts", (G, P, GPW))
    c.zs = scratch("z_sample", (8, DIN))
    c.ys_t = scratch("ys_t", (WS, 8))
    with ExitStack() as s:
        def sb(name, shape, dt=F32):
            return s.enter_context(nc.sbuf_tensor(name, shape, dt))

        c.ident, c.identb = sb("ident", [P, P]), sb("identb", [P, P], BF16)
        c.upper, c.lower_strict = sb("upper", [P, P]), sb("lower_strict", [P, P])
        c.mask_kq, c.mask_qk = sb("mask_kq", [P, P], BF16), sb("mask_qk", [P, P], BF16)
        c.ones = sb("ones", [P, P])
        c.minus_half = sb("minus_half", [P, 8])
        c.flogit = sb("flogit", [P, T // P, NF])
        c.negc = sb("negc", [P, NF, T // P])
        c.lfs = sb("lf_sample", [8, NF])
        c.mix_s = sb("mix_s", [P, KD, 8])
        c.bank = [s.enter_context(nc.psum_tensor(f"bank{i}", [P, 512], F32)) for i in range(8)]
        setup_constants(nc, c)
        with nc.cleanup_on_exit(), ExitStack() as s2:
            ssm_c = SsmConstants(nc, s2)
            project_prompt(nc, c, a["x_prompt"], a["w_in"], a["g_norm"], o["k_prompt"], o["v_prompt"], ssm_c, a)
            forget_gates(nc, c, a["b_f"], o["logf_prompt"])
            fox_prompt(nc, c, o["k_prompt"], o["v_prompt"], ssm_c, a)
        memory_prompt(nc, c, a["mem_prompt"], a["g_mem"], a["w_mem_kv"], o["memk_prompt"], o["memv_prompt"])
        sample_project(nc, c, a, o)
        ssm(nc, c, a, o["ssm_prompt"], o["ssm_sample"])
        sample_attend(nc, c, a)
        mix_out(nc, c, a, o["y_prompt"], o["y_sample"])



INS = ["x_prompt", "x_sample", "mem_prompt", "cache_k", "cache_v", "cache_logf", "state_ssm", "cache_mem_k",
       "cache_mem_v", "page_table", "g_norm", "w_in", "b_f", "lam_re", "lam_im", "log_dt", "b_re", "b_im",
       "c_re", "c_im", "d_skip", "w_glu", "b_glu", "g_mem", "w_mem_kv", "w_out", "g_final"]
OUTS = [("y_prompt", (1, T, D)), ("y_sample", (8, 1, D)),
        ("k_prompt", (1, 1, T, NF, HD)), ("v_prompt", (1, 1, T, NF, HD)), ("logf_prompt", (1, 1, T, NF)),
        ("ssm_prompt", (1, 1, G, NS, 2)), ("memk_prompt", (1, 1, NMEM, NM, HD)),
        ("memv_prompt", (1, 1, NMEM, NM, HD)), ("k_sample", (1, 8, 1, NF, HD)),
        ("v_sample", (1, 8, 1, NF, HD)), ("logf_sample", (1, 8, 1, NF)), ("ssm_sample", (1, 8, G, NS, 2))]


def kernel(**inputs):
    import numpy as np
    import concourse.bacc as bacc
    from concourse.bass_utils import run_bass_kernel_spmd

    nc = bacc.Bacc("TRN2", target_bir_lowering=False, num_devices=1)
    arrays, a, o = {}, {}, {}
    for name in INS:
        x = np.ascontiguousarray(inputs[name])
        arrays[f"in_{name}"] = x
        a[name] = nc.dram_tensor(f"in_{name}", x.shape, mybir.dt.from_np(x.dtype), kind="ExternalInput").ap()
    for name, shape in OUTS:
        o[name] = nc.dram_tensor(f"out_{name}", shape, F32, kind="ExternalOutput").ap()
    build(nc, a, o)
    r = run_bass_kernel_spmd(nc, [arrays], core_ids=[0])
    return tuple(r.results[0][f"out_{name}"] for name, _ in OUTS)
```

```python
from contextlib import ExitStack

import concourse.bass as bass
from concourse import mybir

F32 = mybir.dt.float32
F32R = mybir.dt.float32r
BF16 = mybir.dt.bfloat16
I32 = mybir.dt.int32
ALU = mybir.AluOpType
ACT = mybir.ActivationFunctionType
AX = mybir.AxisListType

P = 128
D = 1024
T = 4096
HD = 64
NF, WF = 6, 384
G, GC, NS, WS = 24, 16, 64, 384
NM, WM, NMEM = 4, 256, 256
KD = D // P
EPS = 1e-6
CQ, CK, CV, CF = 0, WF, 2 * WF, 3 * WF
CGA = CF + NF
CU = CGA + WF
CGS = CU + WS
CQM = CGS + WS
CGM = CQM + WM
DIN = CGM + WM
NEG = -1e30


def at(per, i, n):
    return per * (i + 1) + n


class Core:
    pass


def setup_constants(nc, c):
    with ExitStack() as s:
        filled = s.enter_context(nc.semaphore("const_filled"))
        made = s.enter_context(nc.semaphore("const_made"))
        block = s.enter_context(nc.Block())

        @block.gpsimd
        def _(pool):
            fills = [(c.ident, 0.0), (c.identb, 0.0), (c.upper, 1.0), (c.lower_strict, 1.0),
                     (c.mask_kq, 0.0), (c.mask_qk, 0.0), (c.ones, 1.0), (c.minus_half, -0.5)]
            for t, v in fills:
                pool.memset(t[:], v).then_inc(filled, 1)
            pool.wait_ge(filled, len(fills))
            for t in (c.ident, c.identb):
                pool.affine_select(out=t[:], in_=t[:], pattern=[[-1, P]], compare_op=ALU.not_equal,
                                   fill=1.0, base=0, channel_multiplier=1).then_inc(made, 1)
            pool.affine_select(out=c.upper[:], in_=c.upper[:], pattern=[[1, P]], compare_op=ALU.is_ge,
                               fill=0.0, base=0, channel_multiplier=-1).then_inc(made, 1)
            pool.affine_select(out=c.lower_strict[:], in_=c.lower_strict[:], pattern=[[-1, P]],
                               compare_op=ALU.is_gt, fill=0.0, base=0, channel_multiplier=1).then_inc(made, 1)
            pool.affine_select(out=c.mask_kq[:], in_=c.mask_kq[:], pattern=[[1, P]], compare_op=ALU.is_ge,
                               fill=NEG, base=0, channel_multiplier=-1).then_inc(made, 1)
            pool.affine_select(out=c.mask_qk[:], in_=c.mask_qk[:], pattern=[[-1, P]], compare_op=ALU.is_ge,
                               fill=NEG, base=0, channel_multiplier=1).then_inc(made, 1)
            pool.wait_ge(made, 6)


STEP = 8
NCH = T // STEP
SC = STEP * GC
O_COS, O_SIN = 0, NCH
O_R = 2 * NCH
O_W1 = O_R + (2 * STEP - 1) * GC
O_W2 = O_W1 + SC
O_CC = O_W2 + SC
O_D = O_CC + GC
O_R8, O_A1, O_B1 = O_D + 1, O_D + 2, O_D + 3
GPW = O_B1 + 1
TWO_PI = 6.283185307179586
PI1 = 6.28125
PI2 = 0.0019350051879882812
PI3 = 3.0199159819567e-07
ROUND = 12582912.0


class SsmConstants:

    NGB = 4
    SCALAR_LOADS, TABLE_LOADS = 16 * 5, 16 * (4 + 4 + STEP)
    ND = 9
    ARG_AT, REDUCED_AT, TURNS_AT = 1, 8, 8 + 9 + 6

    def __init__(self, nc, s):
        def sb(name, shape, dt=F32):
            return s.enter_context(nc.sbuf_tensor(name, shape, dt))

        self.sb = sb
        self.v = {n: sb("v_" + n, [P, G]) for n in ("mag", "r8", "cs", "sn", "lr", "li", "den", "fr", "fi", "fi2", "nr", "t1", "t2")}
        self.lre, self.lim = sb("lre", [P, G]), sb("lim", [P, G])
        self.ar, self.ai, self.nai = sb("ar", [P, G, 9]), sb("ai", [P, G, 9]), sb("nai", [P, G, 9])
        self.uc, self.us = sb("uc", [P, G, self.ND]), sb("us", [P, G, self.ND])
        self.sgn = sb("sgn", [P, 2])
        self.loaded, self.step, self.acted, self.signs = (
            nc.alloc_semaphore(n) for n in ("sp_loaded", "sp_step", "sp_act", "sp_signs"))
        self.b_in, self.turned, self.c_out, self.made, self.stored = (
            nc.alloc_semaphore(n) for n in ("st_in", "st_pe", "st_c", "st_made", "st_stored"))


    def place_scalars(self, s, nc):
        def sb(name):
            return s.enter_context(nc.sbuf_tensor(name, [P, G], F32))
        self.ldt = sb("ldt")
        self.turns = [s.enter_context(nc.sbuf_tensor(f"sp_turns{k}", [P, G, self.ND], F32)) for k in range(3)]
        self.t = {n: sb("v_" + n) for n in ("dt", "a", "th", "t3", "sh")}

    def load_scalars(self, nc, sp, a):
        with nc.allow_non_contiguous_dma(reason="parameters, states on rows"):
            for r in (0, HD):
                sp.dma_start(self.lre[r:r + HD, :], a["lam_re"].rearrange("o g p -> p (o g)")).then_inc(self.loaded, 16)
                sp.dma_start(self.lim[r:r + HD, :], a["lam_im"].rearrange("o g p -> p (o g)")).then_inc(self.loaded, 16)
            sp.dma_start(self.ldt[:], a["log_dt"][0].partition_broadcast(P)).then_inc(self.loaded, 16)

    def set_signs(self, pool):
        pool.memset(self.sgn[0:HD, 0:1], 1.0).then_inc(self.signs, 1)
        pool.memset(self.sgn[HD:P, 0:1], -1.0).then_inc(self.signs, 1)
        pool.wait_ge(self.signs, 2)
        pool.memset(self.sgn[0:HD, 1:2], -1.0).then_inc(self.signs, 1)
        pool.memset(self.sgn[HD:P, 1:2], 1.0).then_inc(self.signs, 1)
        pool.wait_ge(self.signs, 4)

    def scalar_functions(self, act):
        v, t = self.v, self.t
        act.wait_ge(self.loaded, self.SCALAR_LOADS)
        act.activation(t["dt"][:], self.ldt[:], ACT.Exp).then_inc(self.acted, 1)
        act.wait_ge(self.step, self.ARG_AT)
        act.activation(v["mag"][:], t["a"][:], ACT.Exp).then_inc(self.acted, 1)
        act.activation(v["r8"][:], t["a"][:], ACT.Exp, scale=float(STEP)).then_inc(self.acted, 1)
        act.wait_ge(self.step, self.REDUCED_AT)
        act.activation(v["sn"][:], v["t2"][:], ACT.Sin).then_inc(self.acted, 1)
        act.activation(t["sh"][:], v["t2"][:], ACT.Sin, scale=0.5).then_inc(self.acted, 1)
        act.wait_ge(self.step, self.TURNS_AT)
        act.activation(self.us[:], self.turns[0][:], ACT.Sin).then_inc(self.acted, 1)
        act.activation(self.uc[:], self.turns[0][:], ACT.Sin, scale=0.5).then_inc(self.acted, 1)

    def scalars(self, dve):
        n = [0]

        def done(ins):
            n[0] += 1
            ins.then_inc(self.step, 1)
            dve.wait_ge(self.step, n[0])

        def tt(out, x, y, op):
            done(dve.tensor_tensor(out, x, y, op))

        def ts(out, x, y, op, y2=None, op2=ALU.bypass):
            done(dve.tensor_scalar(out, x, y, y2, op, op2))

        M, A_, S_ = ALU.mult, ALU.add, ALU.subtract
        w = {k: t[:] for k, t in {**self.v, **self.t}.items()}
        lre, lim = self.lre[:], self.lim[:]
        dve.wait_ge(self.loaded, self.SCALAR_LOADS)
        dve.wait_ge(self.acted, 1)
        tt(w["a"], lre, w["dt"], M)
        assert n[0] == self.ARG_AT
        tt(w["th"], lim, w["dt"], M)
        ts(w["t1"], w["th"], 1.0 / TWO_PI, M)
        ts(w["t1"], w["t1"], ROUND, A_, -ROUND, A_)
        done(dve.scalar_tensor_tensor(w["t2"], w["t1"], -PI1, w["th"], M, A_))
        done(dve.scalar_tensor_tensor(w["t3"], w["t1"], -PI2, w["t2"], M, A_))
        done(dve.scalar_tensor_tensor(w["den"], w["t1"], -PI3, w["t3"], M, A_))
        ts(w["t2"], w["den"], 3.1415925, ALU.min, -3.1415925, ALU.max)
        assert n[0] == self.REDUCED_AT
        a0, a1, a2 = (x[:] for x in self.turns)
        for j in range(self.ND):
            ts(a0[:, :, j], w["t2"], float(STEP << j), M)
        ts(a1, a0, 1.0 / TWO_PI, M)
        ts(a1, a1, ROUND, A_, -ROUND, A_)
        done(dve.scalar_tensor_tensor(a2, a1, -PI1, a0, M, A_))
        done(dve.scalar_tensor_tensor(a0, a1, -PI2, a2, M, A_))
        done(dve.scalar_tensor_tensor(a2, a1, -PI3, a0, M, A_))
        ts(a0, a2, 3.1415925, ALU.min, -3.1415925, ALU.max)
        assert n[0] == self.TURNS_AT
        dve.wait_ge(self.acted, 5)
        tt(w["t1"], w["sh"], w["sh"], M)
        ts(w["cs"], w["t1"], -2.0, M, 1.0, A_)
        tt(w["lr"], w["mag"], w["cs"], M)
        tt(w["li"], w["mag"], w["sn"], M)
        tt(w["t1"], lre, lre, M)
        tt(w["t2"], lim, lim, M)
        tt(w["t1"], w["t1"], w["t2"], A_)
        done(dve.reciprocal(w["den"], w["t1"]))


    def place_tables(self, s, nc):
        def sb(name, shape):
            return s.enter_context(nc.sbuf_tensor(name, shape, F32))
        self.gp = sb("gp", [P, self.NGB, GPW])
        self.b1, self.b2 = sb("b_ri", [P, G, GC]), sb("b_ir", [P, G, GC])
        self.cin = sb("c_in", [P, 3, 2, 2, NS])
        self.cd, self.ce = sb("c_ri", [P, G, GC]), sb("c_ir", [P, G, GC])
        self.bb1, self.bb2 = sb("bb_ri", [P, G, GC]), sb("bb_ir", [P, G, GC])
        self.big = sb("st_big", [P, self.NGB, 256])
        self.dcol = sb("dcol", [P, G])

    def load_tables(self, nc, sp, a):
        with nc.allow_non_contiguous_dma(reason="parameters, states on rows"):
            for j, (x, y) in enumerate((("c_re", "c_im"), ("c_im", "c_re"))):
                for k, z in enumerate((x, y)):
                    sp.dma_start(self.cin[:, :, j, k, :], a[z].rearrange("o g c p -> (o g c) p").rearrange("(t q) p -> q t p", q=P)
                                 ).then_inc(self.b_in, 16)
            for r in (0, HD):
                x, y = ("b_re", "b_im") if r == 0 else ("b_im", "b_re")
                sp.dma_start(self.b1[r:r + HD], a[x].rearrange("o g p c -> p (o g) c")).then_inc(self.b_in, 16)
                sp.dma_start(self.b2[r:r + HD], a[y].rearrange("o g p c -> p (o g) c")).then_inc(self.b_in, 16)
            for t in range(STEP):
                sp.dma_start(self.dcol[t * GC:(t + 1) * GC, :], a["d_skip"].rearrange("o g c -> c (o g)")).then_inc(self.b_in, 16)

    def turn_c(self, pe, c):
        pe.wait_ge(self.b_in, self.TABLE_LOADS)
        for j in range(2):
            for t in range(3):
                tr = pe.transpose(c.bank[j][:, t * P:(t + 1) * P], self.cin[:, t, j, :, :].rearrange("q a p -> q (a p)"), c.ident[:])
            tr.then_inc(self.turned, 1)

    def copy_c(self, dve, c):
        dve.wait_ge(self.turned, 2)
        dve.tensor_copy(self.cd[:].rearrange("p g c -> p (g c)"), c.bank[0][:, 0:G * GC]).then_inc(self.c_out, 1)
        dve.tensor_copy(self.ce[:].rearrange("p g c -> p (g c)"), c.bank[1][:, 0:G * GC]).then_inc(self.c_out, 1)

    def tables(self, pool, c):
        n, m_ = [0], self.NGB

        def done(ins):
            n[0] += 1
            ins.then_inc(self.made, 1)
            pool.wait_ge(self.made, n[0])

        def tt(out, x, y, op):
            done(pool.tensor_tensor(out, x, y, op))

        M, A_, S_ = ALU.mult, ALU.add, ALU.subtract
        w = {k: t[:] for k, t in self.v.items()}
        ar, ai, nai, uc, us = self.ar, self.ai, self.nai, self.uc, self.us
        lre, lim = self.lre[:], self.lim[:]
        sg, ns = self.sgn[:, 0:1], self.sgn[:, 1:2]

        def ts(out, x, y, op, y2=None, op2=ALU.bypass):
            done(pool.tensor_scalar(out, x, y, y2, op, op2))

        ts(w["nr"], w["lr"], -1.0, A_)
        tt(w["t1"], w["nr"], lre, M)
        tt(w["t2"], w["li"], lim, M)
        tt(w["t1"], w["t1"], w["t2"], A_)
        tt(w["fr"], w["t1"], w["den"], M)
        tt(w["t1"], w["li"], lre, M)
        tt(w["t2"], w["nr"], lim, M)
        tt(w["t1"], w["t1"], w["t2"], S_)
        tt(w["t2"], w["t1"], w["den"], M)
        ts(w["fi"], w["t2"], ns, M)
        ts(w["fi2"], w["t2"], sg, M)
        done(pool.memset(ar[:, :, 0], 1.0))
        done(pool.memset(ai[:, :, 0], 0.0))
        for k in range(STEP):
            tt(ar[:, :, k + 1], ar[:, :, k], w["lr"], M)
            tt(w["t1"], ai[:, :, k], w["li"], M)
            tt(ar[:, :, k + 1], ar[:, :, k + 1], w["t1"], S_)
            tt(ai[:, :, k + 1], ar[:, :, k], w["li"], M)
            tt(w["t1"], ai[:, :, k], w["lr"], M)
            tt(ai[:, :, k + 1], ai[:, :, k + 1], w["t1"], A_)
        ts(nai[:], ai[:], ns, M)
        tt(uc[:], uc[:], uc[:], M)
        ts(uc[:], uc[:], -2.0, M, 1.0, A_)
        bb1, bb2, cd, ce, big, gp = self.bb1, self.bb2, self.cd, self.ce, self.big, self.gp
        pool.wait_ge(self.b_in, self.TABLE_LOADS)
        bg = [P, G, GC]
        for out, x, y, f in ((bb1, self.b1, self.b2, "fi"), (bb2, self.b2, self.b1, "fi2")):
            tt(out[:], x[:], w["fr"].unsqueeze(2).to_broadcast(bg), M)
            tmp = gp[:, 0, 0:G * GC].rearrange("p (g c) -> p g c", c=GC)
            tt(tmp, y[:], w[f].unsqueeze(2).to_broadcast(bg), M)
            tt(out[:], out[:], tmp, A_)
        pool.wait_ge(self.c_out, 2)
        for g0 in range(0, G, m_):
            gs = slice(g0, g0 + m_)
            ar, ai, nai, uc, us = (x[:, gs] for x in (self.ar, self.ai, self.nai, self.uc, self.us))
            if g0:
                pool.wait_ge(self.stored, 16 * (g0 // m_))
            sc = [P, m_, GC]
            b16 = big[:, :, 0:GC]
            R = gp[:, :, O_R:O_W1].rearrange("p g (m c) -> p g m c", c=GC)
            done(pool.memset(R[:, :, STEP:], 0.0))
            for m in range(STEP):
                k = STEP - 1 - m
                tt(R[:, :, m, :], bb1[:, gs], ar[:, :, k:k + 1].to_broadcast(sc), M)
                tt(b16, bb2[:, gs], nai[:, :, k:k + 1].to_broadcast(sc), M)
                tt(R[:, :, m, :], R[:, :, m, :], b16, A_)
            done(pool.tensor_scalar(gp[:, :, O_CC:O_D], cd[:, gs], self.sgn[:, 0:1], None, M))
            for t in range(STEP):
                k = t + 1
                one, two = gp[:, :, O_W1 + t * GC:O_W1 + (t + 1) * GC], gp[:, :, O_W2 + t * GC:O_W2 + (t + 1) * GC]
                tt(one, gp[:, :, O_CC:O_D], ar[:, :, k:k + 1].to_broadcast(sc), M)
                tt(b16, ce[:, gs], ai[:, :, k:k + 1].to_broadcast(sc), M)
                tt(one, one, b16, S_)
                tt(two, cd[:, gs], nai[:, :, k:k + 1].to_broadcast(sc), M)
                tt(b16, ce[:, gs], ar[:, :, k:k + 1].to_broadcast(sc), M)
                tt(two, two, b16, S_)
            cosT, sinT = gp[:, :, O_COS:O_COS + NCH], gp[:, :, O_SIN:O_SIN + NCH]
            done(pool.memset(cosT[:, :, 0:1], 1.0))
            done(pool.memset(sinT[:, :, 0:1], 0.0))
            for j in range(self.ND):
                m = 1 << j
                sh = [P, m_, m]
                cj, sj = uc[:, :, j:j + 1].to_broadcast(sh), us[:, :, j:j + 1].to_broadcast(sh)
                lo_c, lo_s, hi_c, hi_s = cosT[:, :, 0:m], sinT[:, :, 0:m], cosT[:, :, m:2 * m], sinT[:, :, m:2 * m]
                tt(hi_c, lo_c, cj, M)
                tt(big[:, :, 0:m], lo_s, sj, M)
                tt(hi_c, hi_c, big[:, :, 0:m], S_)
                tt(hi_s, lo_s, cj, M)
                tt(big[:, :, 0:m], lo_c, sj, M)
                tt(hi_s, hi_s, big[:, :, 0:m], A_)
            done(pool.tensor_copy(gp[:, :, O_D], self.dcol[:, gs]))
            done(pool.tensor_copy(gp[:, :, O_R8], self.v["r8"][:, gs]))
            done(pool.tensor_copy(gp[:, :, O_A1], self.v["lr"][:, gs]))
            done(pool.tensor_copy(gp[:, :, O_B1], nai[:, :, 1]))
            pool.dma_start(c.ssm_gp[gs].rearrange("g p w -> p g w"), gp[:]).then_inc(self.stored, 16)
        pool.wait_ge(self.stored, 16 * (G // m_))


def project_prompt(nc, c, x_prompt, w_in, g_norm, k_out, v_out, ssm_c, a):
    TB = 1024
    NTB = T // TB
    NT = TB // P
    SEGW = WF + NF
    SEGS = [("q", CQ, WF), ("k", CK, WF), ("v", CV, WF + NF), ("ga", CGA, WF), ("u", CU, WS),
            ("gs", CGS, WS), ("qm", CQM, WM), ("gm", CGM, WM)]
    outs = []
    for si, (name, c0, w) in enumerate(SEGS):
        if name in ("k", "v", "u"):
            outs += [(si, t, None) for t in range(NT)]
        else:
            outs += [(si, m, h) for m in range(w // P) for h in range(2)]
    NO = len(outs)
    seg_end = [max(n for n, o in enumerate(outs) if o[0] == si) + 1 for si in range(len(SEGS))]
    PB = 5
    assert NO % PB == 0
    NG = KD * 2
    HT = NT // 2
    dest = {"q": (c.q_t, 0, 0.125), "qm": (c.qm_t, 0, 0.125), "ga": (c.gate_t, 0, None),
            "gs": (c.gate_t, WF, None), "gm": (c.gate_t, WF + WS, None)}
    x_v = x_prompt.rearrange("o (b t p) d -> (o b) p t d", p=P, t=NT)
    w_v = w_in.rearrange("o (k p) n -> (o p) k n", p=P)
    k_v = k_out.rearrange("l o (b t p) h d -> (l o b) t p (h d)", p=P, t=NT)
    v_v = v_out.rearrange("l o (b t p) h d -> (l o b) t p (h d)", p=P, t=NT)

    with ExitStack() as s:
        def sb(name, shape, dt=F32):
            return s.enter_context(nc.sbuf_tensor(name, shape, dt))

        def sem(name):
            return s.enter_context(nc.semaphore(name))

        x = sb("x_tok", [P, NT, D])
        xhi, xlo = sb("xhi", [P, KD, TB], F32R), sb("xlo", [P, KD, TB], F32R)
        wraw = sb("wraw", [P, KD, SEGW])
        whi, wlo = sb("whi", [P, 2, KD, SEGW], F32R), sb("wlo", [P, 2, KD, SEGW], F32R)
        fstage = sb("fstage", [P, 2, TB])
        tstage = sb("tstage", [P, 4, WF])
        ustage = sb("ustage", [P, G, 8, GC])
        gn = sb("gn", [P, KD])
        junk = sb("sq_junk", [P, D], BF16)
        ss, rstd = sb("ss", [P, NT]), sb("rstd", [P, NT])
        rstd_in = sb("rstd_in", [P, NT])
        w_loaded, g_loaded = sem("w_loaded"), sem("g_loaded")
        x_loaded = [sem("x_loaded0"), sem("x_loaded1")]
        sq_done, mean_done, rstd_done, xn_done = sem("sq_done"), sem("mean_done"), sem("rstd_done"), sem("xn_done")
        tr_done, hi_done, lo_done = sem("tr_done"), sem("hi_done"), sem("lo_done")
        whi_done, wlo_done, proj_done, evac_done = sem("whi_done"), sem("wlo_done"), sem("proj_done"), sem("evac_done")
        f_stored = [sem(f"f_stored{j}") for j in range(2)]
        t_stored = [sem(f"t_stored{j}") for j in range(4)]
        u_stored = sem("u_stored")
        ssm_c.place_scalars(s, nc)
        block = s.enter_context(nc.Block())
        NSEG = len(SEGS)
        NFM = sum(1 for si, m, h in outs if h == 1)
        fper = [16 * len([f for f in range(NFM) if f % 2 == j]) for j in range(2)]

        @block.sync
        def _(sp):
            ssm_c.load_scalars(nc, sp, a)
            with nc.allow_non_contiguous_dma(reason="1024 gains"):
                sp.dma_start(gn[:], g_norm.rearrange("o (k p) -> p (o k)", p=P)).then_inc(g_loaded, 16)
            with sp.Fori(0, NTB) as i:
                for h in range(2):
                    sp.wait_ge(lo_done, at(NG, i, KD * (h + 1) - NG))
                    sp.dma_start(x[:, HT * h:HT * (h + 1)], x_v[i, :, HT * h:HT * (h + 1)]).then_inc(x_loaded[h], 16)
                for si, (_, c0, w) in enumerate(SEGS):
                    sp.wait_ge(wlo_done, at(NSEG, i, si))
                    sp.dma_start(wraw[:, :, 0:w], w_v[:, :, c0:c0 + w]).then_inc(w_loaded, 16)

        @block.gpsimd
        def _(pool):
            ssm_c.set_signs(pool)
            with pool.Fori(0, NTB) as i:
                for h in range(2):
                    half = slice(HT * h, HT * (h + 1))
                    pool.wait_ge(mean_done, 2 * i + h + 1)
                    pool.tensor_tensor(rstd[:, half], rstd_in[:, half], c.minus_half[:, half], ALU.pow).then_inc(rstd_done, 1)

        @block.vector
        def _(dve):
            dve.sem_inc(lo_done, NG)
            dve.sem_inc(wlo_done, NSEG)
            dve.wait_ge(g_loaded, 16)
            ssm_c.scalars(dve)

            def split(i, si):
                w = SEGS[si][2]
                dve.wait_ge(w_loaded, 16 * (NSEG * i + si + 1))
                before = seg_end[si - 2] if si >= 2 else seg_end[si - 2] - NO
                dve.wait_ge(proj_done, at(NO, i, before))
                dve.tensor_copy(whi[:, si % 2, :, 0:w], wraw[:, :, 0:w]).then_inc(whi_done, 1)
                dve.wait_ge(whi_done, NSEG * i + si + 1)
                hi = whi[:, si % 2, :, 0:w]
                dve.tensor_tensor(wlo[:, si % 2, :, 0:w], wraw[:, :, 0:w], hi.bitcast(F32),
                                  ALU.subtract).then_inc(wlo_done, 1)

            with dve.Fori(0, NTB) as i:
                for h in range(2):
                    half = slice(HT * h, HT * (h + 1))
                    dve.wait_ge(x_loaded[h], 16 * (i + 1))
                    for t in range(HT * h, HT * (h + 1)):
                        if t:
                            dve.wait_ge(sq_done, NT * i + t)
                        dve.tensor_tensor_reduce(junk[:], x[:, t, :], x[:, t, :], 1.0, 0.0, ALU.mult, ALU.add,
                                                 ss[:, t:t + 1]).then_inc(sq_done, 1)
                    dve.wait_ge(sq_done, NT * i + HT * (h + 1))
                    dve.tensor_scalar(rstd_in[:, half], ss[:, half], 1.0 / D, EPS, ALU.mult, ALU.add).then_inc(mean_done, 1)
                    dve.wait_ge(rstd_done, 2 * i + h + 1)
                    for t in range(HT * h, HT * (h + 1)):
                        dve.tensor_scalar(x[:, t, :], x[:, t, :], rstd[:, t:t + 1], None,
                                          ALU.mult).then_inc(xn_done, 1)
                split(i, 0)
                for g in range(NG):
                    k, h = g % KD, g // KD
                    dve.wait_ge(hi_done, NG * i + g + 1)
                    hi = xhi[:, k, 512 * h:512 * (h + 1)]
                    dve.scalar_tensor_tensor(xlo[:, k, 512 * h:512 * (h + 1)], c.bank[g % 2][:], gn[:, k:k + 1],
                                             hi.bitcast(F32), ALU.mult, ALU.subtract).then_inc(lo_done, 1)
                for si in range(1, NSEG):
                    split(i, si)

        @block.tensor
        def _(pe):
            pe.sem_inc(proj_done, NO)
            with pe.Fori(0, NTB) as i:
                for g in range(NG):
                    k, h = g % KD, g // KD
                    if k == 0:
                        pe.wait_ge(xn_done, NT * i + HT * (h + 1))
                    pe.wait_ge(lo_done, at(NG, i, g - 1))
                    for t in range(4):
                        tr = pe.transpose(c.bank[g % 2][:, t * P:(t + 1) * P],
                                          x[:, 4 * h + t, k * P:(k + 1) * P], c.ident[:])
                    tr.then_inc(tr_done, 1)
                pe.wait_ge(lo_done, at(NG, i, NG))
                for n, (si, m, h) in enumerate(outs):
                    w = SEGS[si][2]
                    if n == 0 or outs[n - 1][0] != si:
                        pe.wait_ge(wlo_done, at(NSEG, i, si + 1))
                    pe.wait_ge(evac_done, at(NO, i, n - PB + 1))
                    bank = c.bank[2 + n % PB]
                    b = si % 2
                    for k in range(KD):
                        for xs, ws in ((xhi, whi), (xlo, whi), (xhi, wlo)):
                            if h is not None:
                                lhsT, rhs = ws[:, b, k, m * P:(m + 1) * P], xs[:, k, 512 * h:512 * (h + 1)]
                                dst = bank[:, :]
                            elif SEGS[si][0] == "u":
                                lhsT, rhs, dst = xs[:, k, m:TB:8], ws[:, b, k, 0:w], bank[:, 0:w]
                            else:
                                lhsT, rhs, dst = xs[:, k, m * P:(m + 1) * P], ws[:, b, k, 0:w], bank[:, 0:w]
                            last = pe.matmul(dst, lhsT, rhs, start=(k == 0 and ws is whi and xs is xhi),
                                             stop=(k == KD - 1 and ws is wlo))
                    last.then_inc(proj_done, 1)

        @block.scalar
        def _(act):
            act.sem_inc(evac_done, NO)
            for j in range(2):
                act.sem_inc(f_stored[j], fper[j])
            for j in range(4):
                act.sem_inc(t_stored[j], 16 * 4)
            act.sem_inc(u_stored, 16)
            ssm_c.scalar_functions(act)
            act.wait_ge(g_loaded, 16)
            with act.Fori(0, NTB) as i:
                for g in range(NG):
                    k, h = g % KD, g // KD
                    act.wait_ge(tr_done, NG * i + g + 1)
                    act.activation(xhi[:, k, 512 * h:512 * (h + 1)], c.bank[g % 2][:], ACT.Copy,
                                   scale=gn[:, k:k + 1]).then_inc(hi_done, 1)
                fm = tm = 0
                for n, (si, m, h) in enumerate(outs):
                    name, c0, w = SEGS[si]
                    act.wait_ge(proj_done, at(NO, i, n + 1))
                    bank = c.bank[2 + n % PB]
                    if h is not None:
                        dram, row, scale = dest[name]
                        slot = fm % 2
                        if h == 0:
                            act.wait_ge(f_stored[slot], at(fper[slot], i, 16 * (fm // 2)))
                        func = ACT.Silu if scale is None else ACT.Copy
                        act.activation(fstage[:, slot, 512 * h:512 * (h + 1)], bank[:], func,
                                       scale=1.0 if scale is None else scale).then_inc(evac_done, 1)
                        if h == 1:
                            act.wait_ge(evac_done, at(NO, i, n + 1))
                            r0 = row + m * P
                            act.dma_start(dram[r0:r0 + P, bass.ds(i * TB, TB)], fstage[:, slot, :]
                                          ).then_inc(f_stored[slot], 16)
                            fm += 1
                    elif name == "u":
                        if m == 0:
                            act.wait_ge(u_stored, at(16, i, 0))
                        act.activation(ustage[:, :, m, :], bank[:, 0:WS].rearrange("p (g c) -> p g c", c=GC),
                                       ACT.Copy).then_inc(evac_done, 1)
                        if m == NT - 1:
                            act.wait_ge(evac_done, at(NO, i, n + 1))
                            act.dma_start(c.u_chunks[i], ustage[:].rearrange("p g t c -> p (g t c)")
                                          ).then_inc(u_stored, 16)
                    else:
                        slot = tm % 4
                        act.wait_ge(t_stored[slot], at(64, i, 16 * (tm // 4)))
                        if name == "v":
                            act.activation(c.flogit[:, i * NT + m, :], bank[:, WF:WF + NF], ACT.Copy)
                        act.activation(tstage[:, slot, :], bank[:, 0:WF], ACT.Copy).then_inc(evac_done, 1)
                        act.wait_ge(evac_done, at(NO, i, n + 1))
                        act.dma_start((k_v if name == "k" else v_v)[i, m], tstage[:, slot, :]
                                      ).then_inc(t_stored[slot], 16)
                        tm += 1
            for j in range(2):
                act.wait_ge(f_stored[j], at(fper[j], NTB, 0))
            for j in range(4):
                act.wait_ge(t_stored[j], at(64, NTB, 0))
            act.wait_ge(u_stored, at(16, NTB, 0))


def forget_gates(nc, c, b_f, logf_out):
    NT = T // P
    with ExitStack() as s:
        def sb(name, shape, dt=F32):
            return s.enter_context(nc.sbuf_tensor(name, shape, dt))

        def sem(name):
            return s.enter_context(nc.semaphore(name))

        bf = sb("bf", [P, NF])
        z, zn, za, ez, sp_ = (sb(n, [P, NT, NF]) for n in ("fz", "fzn", "fza", "fez", "fsp"))
        lf = sb("lf", [P, NT, NF])
        pre = sb("lf_prefix", [P, NF, NT])
        prex = sb("lf_before", [P, NT, NF])
        rows = sb("crow_stage", [P, 2, P], F32R)
        loaded, dve_step, act_step, pe_step, stored = sem("bf_loaded"), sem("f_dve"), sem("f_act"), sem("f_pe"), sem("f_stored")
        block = s.enter_context(nc.Block())
        cum = c.bank[0][:, 0:NT * NF]

        @block.sync
        def _(sp):
            with nc.allow_non_contiguous_dma(reason="six forget gates a token"):
                sp.dma_start(bf[:], b_f[0].partition_broadcast(P)).then_inc(loaded, 16)
                sp.wait_ge(dve_step, 5)
                sp.dma_start(logf_out.rearrange("l o (t p) h -> p (l o t) h", p=P), lf[:]).then_inc(stored, 16)
                sp.wait_ge(dve_step, 17)
                sp.dma_start(c.negc_rows.rearrange("h (t p) -> (h t) p", p=P)[0:P], rows[:, 0, :].bitcast(F32)).then_inc(stored, 16)
                sp.dma_start(c.negc_rows.rearrange("h (t p) -> (h t) p", p=P)[P:NF * NT], rows[0:NF * NT - P, 1, :].bitcast(F32)
                             ).then_inc(stored, 16)
            sp.wait_ge(stored, 48)

        @block.vector
        def _(dve):
            n = [0]

            def done(ins):
                n[0] += 1
                ins.then_inc(dve_step, 1)
                dve.wait_ge(dve_step, n[0])

            dve.wait_ge(loaded, 16)
            done(dve.tensor_tensor(z[:], c.flogit[:], bf[:].unsqueeze(1).to_broadcast([P, NT, NF]), ALU.add))
            done(dve.tensor_scalar(zn[:], z[:], -1.0, None, ALU.mult))
            done(dve.tensor_tensor(za[:], z[:], zn[:], ALU.min))
            done(dve.tensor_scalar(zn[:], z[:], 0.0, None, ALU.min))
            dve.wait_ge(act_step, 2)
            done(dve.tensor_tensor(lf[:], zn[:], sp_[:], ALU.subtract))
            for h in range(NF):
                dve.tensor_tensor_scan(pre[:, h, :], c.ones[:, 0:NT], lf[:, :, h], 0.0, ALU.mult,
                                       ALU.add).then_inc(dve_step, 1)
            dve.memset(prex[:, 0, :], 0.0).then_inc(dve_step, 1)
            dve.wait_ge(dve_step, 12)
            dve.tensor_copy(prex[:, 1:NT, :], pre[:, :, 0:NT - 1].rearrange("p h t -> p t h")).then_inc(dve_step, 1)
            dve.wait_ge(pe_step, 1)
            dve.tensor_scalar(c.negc[:], cum.rearrange("p (t h) -> p h t", h=NF), -1.0, None, ALU.mult
                              ).then_inc(dve_step, 1)
            dve.wait_ge(pe_step, 2)
            dve.tensor_copy(rows[:, 0, :], c.bank[1][:, 0:P]).then_inc(dve_step, 1)
            dve.wait_ge(pe_step, 3)
            dve.tensor_copy(rows[0:NF * NT - P, 1, :], c.bank[2][0:NF * NT - P, 0:P]).then_inc(dve_step, 1)
            dve.wait_ge(dve_step, 16)
            dve.sem_inc(dve_step, 1)

        @block.scalar
        def _(act):
            act.wait_ge(dve_step, 3)
            act.activation(ez[:], za[:], ACT.Exp).then_inc(act_step, 1)
            act.wait_ge(act_step, 1)
            act.activation(sp_[:], ez[:], ACT.Ln, bias=1.0).then_inc(act_step, 1)

        @block.tensor
        def _(pe):
            pe.wait_ge(dve_step, 13)
            pe.matmul(cum, c.upper[:], lf[:].rearrange("p t h -> p (t h)"), start=True, stop=False)
            pe.matmul(cum, c.ones[:], prex[:].rearrange("p t h -> p (t h)"), start=False, stop=True
                      ).then_inc(pe_step, 1)
            pe.wait_ge(dve_step, 14)
            negc = c.negc[:].rearrange("p h t -> p (h t)")
            pe.transpose(c.bank[1][:, 0:P], negc[:, 0:P], c.ident[:]).then_inc(pe_step, 1)
            pe.transpose(c.bank[2][0:NF * NT - P, 0:P], negc[:, P:NF * NT], c.ident[:]).then_inc(pe_step, 1)


def fox_prompt(nc, c, k_out, v_out, ssm_c, a):
    NB = T // 512
    NT = T // P
    KG = 4
    k_h = k_out.rearrange("l o (t p) h d -> (l o h) p t d", p=P)
    v_h = v_out.rearrange("l o (g t p) h d -> (l o h) g p t d", p=P, t=KG)
    q_h = c.q_t.rearrange("(h d) t -> h d t", d=HD)
    g_h = c.gate_t.rearrange("(h d) t -> h d t", d=HD)
    m_h = c.mix_t.rearrange("(h d) t -> h d t", d=HD)
    c_h = c.negc_rows.rearrange("h (o t) -> h o t", o=1)
    SB, XB, NPRE, TB, OB = 2, 2, 3, 5, 6
    pre = [(b, r, ch, 512 if ch < b else (r + 1) * P) for b in range(NB) for r in range(4) for ch in range(b + 1)]
    pre_end = [4 * (b + 1) * (b + 2) // 2 for b in range(NB)]
    main = [(b, j, max(0, (j - 4 * b) * P)) for b in range(NB) for j in range(4 * b + 4)]
    main_end = [sum(4 * x + 4 for x in range(b + 1)) for b in range(NB)]
    NPR, NMN = len(pre), len(main)
    NG = NT // KG
    LASTB = NB - 1
    QS = 4

    with ExitStack() as s:
        def sb(name, shape, dt=F32):
            return s.enter_context(nc.sbuf_tensor(name, shape, dt))

        def sem(name):
            return nc.alloc_semaphore(name)

        q2 = sb("q2", [P, 2, 512])
        qhi = sb("qhi", [P, QS, 512], F32R)
        qlo = sb("qlo", [HD + 2, QS, 512], F32R)
        qone = sb("qone", [HD + 2, QS, 512], F32R)
        ktok = sb("ktok", [P, NT, HD])
        khl = sb("khl", [P, NT, 2, HD])
        kst = sb("kst", [P, T], F32R)
        kone = sb("kone", [HD + 2, T], F32R)
        vone = sb("vone", [P, NT, P])
        gate = sb("gate_a", [HD, T])
        ncol = sb("ncol", [P, NT])
        p = sb("p", [P, 3, 512])
        pm = sb("pm", [P, 4, NB])
        nm = sb("nm", [P, 2, 4])
        mrow = sb("mrow", [4, QS, P], F32R)
        rec = sb("rec", [HD, 512])
        on = sb("on", [HD, 512])
        og = sb("og", [HD, 2, 512])
        q_in = [sem("q_in0"), sem("q_in1")]
        g_in = [sem(f"g_in{b}") for b in range(NB)]
        k_in, ones_set = sem("k_in"), sem("ones_set")
        vc_in = [sem(f"vc_in{g}") for g in range(NG)]
        q_ready, khl_done, ktr, kst_done, kone_done = (sem(n) for n in ("q_ready", "khl_done", "ktr", "kst_done", "kone_done"))
        pre_s, pre_max, nm_done, nm_tr, mrow_done = (sem(n) for n in ("pre_s", "pre_max", "nm_done", "nm_tr", "mrow_done"))
        m_in = [sem(f"m_in{j}") for j in range(QS)]
        sc, ex, pv = sem("scores"), sem("exp_done"), sem("pv_done")
        s_turn = sem("store_turn")
        o_rec, o_norm, o_gated = sem("o_rec"), sem("o_norm"), sem("o_gated")
        o_stored = [sem("o_stored0"), sem("o_stored1")]
        ssm_c.place_tables(s, nc)
        block = s.enter_context(nc.Block())

        def heads(engine, body):
            with engine.Fori(0, NF - 1) as h:
                body(h, False)
            body(NF - 1, True)

        @block.sync
        def _(sp):
            def load_q(h, b):
                sp.dma_start(q2[0:HD, b % 2, :], q_h[h, :, 512 * b:512 * (b + 1)]).then_inc(q_in[b % 2], 16)
                sp.dma_start(q2[HD:P, b % 2, :], q_h[h, :, 512 * b:512 * (b + 1)]).then_inc(q_in[b % 2], 16)
                sp.dma_start(gate[:, 512 * b:512 * (b + 1)], g_h[h, :, 512 * b:512 * (b + 1)]).then_inc(g_in[b], 16)

            def load_vc(h, g):
                sp.dma_start(vone[:, KG * g:KG * (g + 1), 0:HD], v_h[h, g]).then_inc(vc_in[g], 16)
                sp.dma_start(kone[HD + 1:HD + 2, 512 * g:512 * (g + 1)].bitcast(F32), c_h[h, :, 512 * g:512 * (g + 1)]
                             ).then_inc(vc_in[g], 16)

            def m_row(h, b):
                sp.wait_ge(mrow_done, NB * h + b + 1)
                sp.dma_start(qlo[HD:HD + 1, b % QS, :].bitcast(F32), mrow[:, b % QS, :].bitcast(F32)).then_inc(m_in[b % QS], 16)

            def store(h, b):
                sp.wait_ge(o_gated, NB * h + b + 1)
                sp.sem_inc(s_turn, 1)
                sp.dma_start(m_h[h, :, 512 * b:512 * (b + 1)], og[:, b % 2, :]).then_inc(o_stored[b % 2], 16)

            def body(h, last):
                for b in range(NB):
                    if b == 1 and not last:
                        sp.wait_ge(khl_done, 2 * (h + 1))
                        sp.dma_start(ktok[:], k_h[h + 1]).then_inc(k_in, 16)
                    if b and (b + 3 < NB or not last):
                        sp.wait_ge(q_ready, 3 * (NB * h + b + 2))
                        load_q(h + (b + 3) // NB, (b + 3) % NB)
                    if b:
                        store(h, b - 1)
                    if b and b + 2 < NB:
                        m_row(h, b + 2)
                if not last:
                    for g in range(NG):
                        sp.wait_ge(pv, at(NMN, h, main_end[LASTB - 1] + KG * (g + 1)))
                        load_vc(h + 1, g)
                        if g in (2, 3, 5):
                            m_row(h + 1, g // 2 if g > 3 else g - 2)
                    sp.wait_ge(q_ready, 3 * (NB * (h + 1) + 2))
                    load_q(h + 1, 3)
                store(h, LASTB)

            sp.dma_start(ktok[:], k_h[0]).then_inc(k_in, 16)
            load_q(0, 0)
            load_q(0, 1)
            sp.wait_ge(ones_set, 5)
            for g in range(NG):
                load_vc(0, g)
            m_row(0, 0)
            sp.wait_ge(q_ready, 3)
            load_q(0, 2)
            m_row(0, 1)
            sp.wait_ge(q_ready, 6)
            m_row(0, 2)
            load_q(0, 3)
            heads(sp, body)
            for j in range(2):
                sp.wait_ge(o_stored[j], at(16 * NB // 2, NF, 0))

        @block.gpsimd
        def _(pool):
            pool.memset(vone[:, :, HD:P], 1.0).then_inc(ones_set, 1)
            pool.wait_ge(ones_set, 1)
            pool.memset(kone[HD:HD + 2, :].bitcast(F32), 1.0).then_inc(ones_set, 1)
            pool.wait_ge(ones_set, 2)
            pool.memset(qlo[HD:HD + 2, :, :].bitcast(F32), 0.0).then_inc(ones_set, 1)
            pool.wait_ge(ones_set, 3)
            pool.memset(qone[HD:HD + 2, :, :].bitcast(F32), 1.0).then_inc(ones_set, 1)
            pool.wait_ge(ones_set, 4)
            pool.memset(qone[HD:HD + 1, :, :].bitcast(F32), 0.0).then_inc(ones_set, 1)
            pool.wait_ge(ones_set, 5)
            ssm_c.tables(pool, c)

        @block.vector
        def _(dve):
            dve.sem_inc(pre_max, 2 * NPR)
            dve.sem_inc(o_norm, NB)
            for j in range(2):
                dve.sem_inc(o_stored[j], 16 * NB // 2)

            def split_k(h):
                dve.wait_ge(k_in, 16 * (h + 1))
                dve.tensor_copy(khl[:, :, 0, :].bitcast(F32R), ktok[:]).then_inc(khl_done, 1)
                dve.wait_ge(khl_done, 2 * h + 1)
                dve.tensor_tensor(khl[:, :, 1, :].bitcast(F32R), ktok[:], khl[:, :, 0, :], ALU.subtract).then_inc(khl_done, 1)

            def split_q(h, b):
                n, d = 3 * (NB * h + b), b % QS
                dve.wait_ge(q_in[b % 2], 32 * (NB // 2 * h + b // 2 + 1))
                dve.tensor_copy(qhi[:, d, :], q2[:, b % 2, :]).then_inc(q_ready, 1)
                dve.wait_ge(q_ready, n + 1)
                dve.tensor_copy(qone[0:HD, d, :], qhi[0:HD, d, :].bitcast(F32)).then_inc(q_ready, 1)
                dve.tensor_tensor(qlo[0:HD, d, :], q2[0:HD, b % 2, :], qhi[0:HD, d, :].bitcast(F32), ALU.subtract).then_inc(q_ready, 1)

            def k_one(h, g):
                dve.wait_ge(kst_done, NG * h + g + 1)
                dve.tensor_copy(ncol[:, KG * g:KG * (g + 1)], c.negc[:, h, KG * g:KG * (g + 1)]).then_inc(kone_done, 1)
                dve.tensor_copy(kone[0:HD, 512 * g:512 * (g + 1)], kst[0:HD, 512 * g:512 * (g + 1)].bitcast(F32)
                                ).then_inc(kone_done, 1)

            def maxima(h, n0, n1):
                for n in range(n0, n1):
                    b, r, ch, w = pre[n]
                    dve.wait_ge(pre_s, NPR * h + n + 1)
                    dve.tensor_reduce(pm[:, r, ch:ch + 1], c.bank[XB + n % NPRE][:, 0:w], AX.X, ALU.max
                                      ).then_inc(pre_max, 1)
                    if n + 1 == pre_end[b]:
                        dve.wait_ge(pre_max, at(NPR, h + 1, n + 1))
                        dve.tensor_reduce(nm[:, b % 2, :], pm[:, :, 0:b + 1], AX.X, ALU.max, negate=True
                                          ).then_inc(nm_done, 1)
                        dve.wait_ge(nm_tr, NB * h + b + 1)
                        dve.tensor_copy(mrow[:, b % QS, :], c.bank[TB][0:4, 0:P]).then_inc(mrow_done, 1)

            def finish(h, b):
                dve.wait_ge(pv, at(NMN, h, main_end[b]))
                ob = c.bank[OB + b % 2]
                dve.reciprocal(rec[:], ob[HD:P, :]).then_inc(o_rec, 1)
                dve.wait_ge(o_rec, NB * h + b + 1)
                dve.tensor_tensor(on[:], ob[0:HD, :], rec[:], ALU.mult).then_inc(o_norm, 1)
                dve.wait_ge(o_norm, at(NB, h, b + 1))
                dve.wait_ge(g_in[b], 16 * (h + 1))
                dve.wait_ge(o_stored[b % 2], at(16 * NB // 2, h, 16 * (b // 2)))
                dve.tensor_tensor(og[:, b % 2, :], on[:], gate[:, 512 * b:512 * (b + 1)], ALU.mult
                                  ).then_inc(o_gated, 1)

            def body(h, last):
                for b in range(NB):
                    if b and b + 2 < NB:
                        first = pre_end[b + 1] + NPRE
                        maxima(h, pre_end[b + 1], first)
                        finish(h, b - 1)
                        maxima(h, first, pre_end[b + 2])
                    elif b:
                        finish(h, b - 1)
                    if b == LASTB - 1 and not last:
                        split_k(h + 1)
                    if b == LASTB and not last:
                        k_one(h + 1, 0)
                        split_q(h + 1, 2)
                        maxima(h + 1, 0, pre_end[0])
                        k_one(h + 1, 1)
                        maxima(h + 1, pre_end[0], pre_end[1])
                        for g in range(2, 4):
                            k_one(h + 1, g)
                        maxima(h + 1, pre_end[1], pre_end[2])
                        for g in range(4, NG):
                            k_one(h + 1, g)
                    elif b + 3 < NB or not last:
                        split_q(h + (b + 3) // NB, (b + 3) % NB)
                finish(h, LASTB)

            split_k(0)
            split_q(0, 0)
            split_q(0, 1)
            dve.wait_ge(ones_set, 5)
            k_one(0, 0)
            maxima(0, 0, pre_end[0])
            k_one(0, 1)
            maxima(0, pre_end[0], pre_end[1])
            split_q(0, 2)
            k_one(0, 2)
            maxima(0, pre_end[1], pre_end[2])
            for g in range(3, NG):
                k_one(0, g)
            ssm_c.copy_c(dve, c)
            heads(dve, body)

        @block.scalar
        def _(act):
            ssm_c.load_tables(nc, act, a)
            act.sem_inc(ex, NMN)

            def k_turned(h, g):
                act.wait_ge(ktr, NG * h + g + 1)
                act.activation(kst[:, 512 * g:512 * (g + 1)], c.bank[TB][:], ACT.Copy).then_inc(kst_done, 1)

            def body(h, last):
                for n, (b, j, q0) in enumerate(main):
                    if j == 0:
                        act.wait_ge(kone_done, 2 * (NG * h + b + 1))
                    act.wait_ge(sc, NMN * h + n + 1)
                    act.wait_ge(pv, at(NMN, h, n - 2))
                    act.activation(p[:, n % 3, q0:512], c.bank[n % SB][:, q0:512], ACT.Exp,
                                   bias=ncol[:, j:j + 1]).then_inc(ex, 1)
                    if b == LASTB and not last and j and j % KG == 0:
                        k_turned(h + 1, j // KG - 1)
                if not last:
                    k_turned(h + 1, NG - 1)

            for g in range(NG):
                k_turned(0, g)
            heads(act, body)

        @block.tensor
        def _(pe):
            pe.sem_inc(pv, NMN)

            def turn_k(h, g):
                pe.wait_ge(khl_done, 2 * (h + 1))
                if not (isinstance(h, int) and h == 0 and g == 0):
                    pe.wait_ge(kst_done, NG * h + g)
                for t in range(KG):
                    tr = pe.transpose(c.bank[TB][:, t * P:(t + 1) * P],
                                      khl[:, KG * g + t, :, :].rearrange("p a d -> p (a d)"), c.ident[:])
                tr.then_inc(ktr, 1)

            def maxima_to_rows(h, b, turned):
                pe.wait_ge(nm_done, NB * h + b + 1)
                pe.wait_ge(kst_done, turned)
                pe.transpose(c.bank[TB][0:4, 0:P], nm[:, b % 2, :], c.ident[:]).then_inc(nm_tr, 1)

            def first_pass(h, n0, n1):
                for n in range(n0, n1):
                    b, r, ch, w = pre[n]
                    if r == 0 and ch == 0:
                        pe.wait_ge(q_ready, 3 * (NB * h + b + 1))
                        pe.wait_ge(kone_done, 2 * (NG * h + b + 1))
                        pe.wait_ge(vc_in[b], 32 * (h + 1))
                    pe.wait_ge(pre_max, at(NPR, h + 1, n - NPRE + 1))
                    q = slice(r * P, (r + 1) * P)
                    bank = c.bank[XB + n % NPRE]
                    mm = pe.matmul(bank[:, 0:w], qone[:, b % QS, q], kone[:, 512 * ch:512 * ch + w],
                                   start=True, stop=True)
                    if ch == b:
                        mm = pe.matmul(bank[:, w - P:w], c.identb[:], c.mask_qk[:], start=False, stop=True,
                                       skip_group_check=True)
                    mm.then_inc(pre_s, 1)

            def weighted(h, n):
                b, j, q0 = main[n]
                pe.wait_ge(ex, at(NMN, h, n + 1))
                if j == 0:
                    pe.wait_ge(o_norm, at(NB, h, b - 1))
                pe.matmul(c.bank[OB + b % 2][:, q0:512], vone[:, j, :], p[:, n % 3, q0:512], start=(j == 0),
                          stop=(j == 4 * b + 3), skip_group_check=True).then_inc(pv, 1)

            ROWS_AT = (13, 18, 26)

            def body(h, last):
                for n, (b, j, q0) in enumerate(main):
                    if j == 0:
                        pe.wait_ge(m_in[b % QS], 16 * (NB // QS * h + b // QS + 1))
                        ahead = 0 < b and b + 2 < NB
                        n_pre = pre_end[b + 1] if ahead else NPR
                        rows_due = ahead
                    bank = c.bank[n % SB]
                    pe.wait_ge(ex, at(NMN, h, n - SB + 1))
                    pe.matmul(bank[:, q0:512], kst[:, j * P:(j + 1) * P], qhi[:, b % QS, q0:512], start=True, stop=False)
                    mm = pe.matmul(bank[:, q0:512], kone[:, j * P:(j + 1) * P], qlo[:, b % QS, q0:512], start=False, stop=True)
                    if j >= 4 * b:
                        mm = pe.matmul(bank[:, q0:q0 + P], c.identb[:], c.mask_kq[:], start=False, stop=True,
                                       skip_group_check=True)
                    mm.then_inc(sc, 1)
                    if ahead:
                        if n_pre == pre_end[b + 2] and rows_due:
                            maxima_to_rows(h, b + 2, NG * (h + 1))
                            rows_due = False
                        rate = (3 if b < 3 else 2, 2 if b == 2 else 1, 0, 0)[j] if j < 4 else (3 if b == 1 else 2)
                        upto = min(n_pre + rate, pre_end[b + 2])
                        first_pass(h, n_pre, upto)
                        n_pre = upto
                    elif b == LASTB and not last:
                        if j in ROWS_AT:
                            maxima_to_rows(h + 1, ROWS_AT.index(j), NG * (h + 1) + j // KG)
                        if 8 <= j < 12:
                            first_pass(h + 1, j - 8, j - 7)
                        elif 13 <= j < 17:
                            first_pass(h + 1, pre_end[0] + 2 * (j - 13), pre_end[0] + 2 * (j - 12))
                        elif 19 <= j < 25:
                            first_pass(h + 1, pre_end[1] + 2 * (j - 19), pre_end[1] + 2 * (j - 18))
                    if n:
                        weighted(h, n - 1)
                    if j == 4 * b + 3 and rows_due:
                        maxima_to_rows(h, b + 2, NG * (h + 1))
                    if b == LASTB and not last and j and j % KG == 0:
                        rows = sum(x < j for x in ROWS_AT)
                        if rows > sum(x < j - KG for x in ROWS_AT):
                            pe.wait_ge(mrow_done, NB * (h + 1) + rows)
                        turn_k(h + 1, j // KG - 1)
                weighted(h, NMN - 1)
                if not last:
                    turn_k(h + 1, NG - 1)

            turn_k(0, 0)
            pe.wait_ge(ones_set, 5)
            first_pass(0, 0, pre_end[0])
            maxima_to_rows(0, 0, 1)
            pe.wait_ge(mrow_done, 1)
            turn_k(0, 1)
            first_pass(0, pre_end[0], pre_end[1])
            maxima_to_rows(0, 1, 2)
            pe.wait_ge(mrow_done, 2)
            turn_k(0, 2)
            first_pass(0, pre_end[1], pre_end[2])
            maxima_to_rows(0, 2, 3)
            pe.wait_ge(mrow_done, 3)
            for g in range(3, NG):
                turn_k(0, g)
            ssm_c.turn_c(pe, c)
            pe.wait_ge(ssm_c.c_out, 2)
            heads(pe, body)


def memory_prompt(nc, c, mem, g_mem, w_kv, mk_out, mv_out, also):
    NB = T // 512
    MT = NMEM // P
    with ExitStack() as s:
        def sb(name, shape, dt=F32):
            return s.enter_context(nc.sbuf_tensor(name, shape, dt))

        def sem(name):
            return s.enter_context(nc.semaphore(name))

        x = sb("mem_x", [P, MT, D])
        w = sb("mem_w", [P, KD, 2 * WM])
        gm = sb("mem_g", [P, KD])
        xt = sb("mem_xt", [P, KD, NMEM])
        junk = sb("mem_junk", [P, D], BF16)
        ss, rin, rstd = sb("mem_ss", [P, MT]), sb("mem_rin", [P, MT]), sb("mem_rstd", [P, MT])
        kv = sb("mem_kv", [P, MT, 2 * WM])
        kt = sb("mem_kt", [P, 2, NMEM])
        q = sb("mem_q", [P, 2, 2, 512])
        gate = sb("mem_gate", [HD, 2, NM, 512])
        nmax, tot, rtot = sb("mem_nmax", [P, 2, NM]), sb("mem_tot", [P, 2, NM]), sb("mem_rtot", [P, 2, NM])
        p = sb("mem_p", [P, 2, NM, NMEM])
        pn = sb("mem_pn", [P, 2, NM, NMEM])
        pt = sb("mem_pt", [P, 2, NM, MT, 512])
        og = sb("mem_og", [HD, 2, NM, 512])
        loaded, step, powed, pe1 = sem("mem_loaded"), sem("mem_step"), sem("mem_powed"), sem("mem_pe")
        q_in = [sem("mem_q_in0"), sem("mem_q_in1")]
        s_done, max_done, exp_done, norm_done, tr_done, pt_done = (
            sem(n) for n in ("mem_s", "mem_max", "mem_exp", "mem_norm", "mem_tr", "mem_ptd"))
        r_done, o_done, og_done = sem("mem_r"), sem("mem_o"), sem("mem_ogd")
        o_stored = [sem("mem_st0"), sem("mem_st1")]
        kv_stored, turn = sem("mem_kv_stored"), sem("mem_turn")
        block = s.enter_context(nc.Block())
        NT = 4
        q_v = c.qm_t.rearrange("(a p) (b t) -> b p a t", p=P, t=512)
        g_v = c.gate_t[WF + WS:D].rearrange("(h d) (b t) -> b d h t", d=HD, t=512)
        m_v = c.mix_t[WF + WS:D].rearrange("(h d) (b t) -> b d h t", d=HD, t=512)

        @block.sync
        def _(sp):
            with nc.allow_non_contiguous_dma(reason="1024 gains"):
                sp.dma_start(gm[:], g_mem.rearrange("o (k p) -> p (o k)", p=P)).then_inc(loaded, 16)
            sp.dma_start(x[:], mem.rearrange("o (t p) d -> p (o t) d", p=P)).then_inc(loaded, 16)
            sp.dma_start(w[:], w_kv.rearrange("o (k p) n -> p (o k) n", p=P)).then_inc(loaded, 16)

            def load(i, j):
                sp.dma_start(q[:, j], q_v[2 * i + j]).then_inc(q_in[j], 16)
                sp.dma_start(gate[:, j], g_v[2 * i + j]).then_inc(q_in[j], 16)

            def store(i, j):
                sp.wait_ge(og_done, at(2 * NM, i, NM * (j + 1)))
                sp.sem_inc(turn, 1)
                sp.dma_start(m_v[2 * i + j], og[:, j]).then_inc(o_stored[j], 16)

            load(0, 0)
            load(0, 1)
            with sp.Fori(0, NB // 2 - 1) as i:
                for j in range(2):
                    store(i, j)
                    load(i + 1, j)
            for j in range(2):
                store(NB // 2 - 1, j)

        @block.gpsimd
        def _(pool):
            pool.wait_ge(step, MT + 1)
            pool.tensor_tensor(rstd[:], rin[:], c.minus_half[:, 0:MT], ALU.pow).then_inc(powed, 1)

        @block.vector
        def _(dve):
            for sem_ in (og_done,):
                dve.sem_inc(sem_, 2 * NM)
            dve.sem_inc(pt_done, 4 * NT)
            dve.sem_inc(norm_done, 2 * NT * NM)
            dve.wait_ge(loaded, 48)
            for t in range(MT):
                dve.tensor_tensor_reduce(junk[:], x[:, t, :], x[:, t, :], 1.0, 0.0, ALU.mult, ALU.add,
                                         ss[:, t:t + 1]).then_inc(step, 1)
                dve.wait_ge(step, t + 1)
            dve.tensor_scalar(rin[:], ss[:], 1.0 / D, EPS, ALU.mult, ALU.add).then_inc(step, 1)
            dve.wait_ge(powed, 1)
            for t in range(MT):
                dve.tensor_scalar(x[:, t, :], x[:, t, :], rstd[:, t:t + 1], None, ALU.mult).then_inc(step, 1)
            for k in range(KD):
                dve.wait_ge(pe1, k + 1)
                dve.tensor_scalar(xt[:, k, :], c.bank[k % 4][:, 0:NMEM], gm[:, k:k + 1], None, ALU.mult
                                  ).then_inc(step, 1)
            for t in range(MT):
                dve.wait_ge(pe1, KD + t + 1)
                dve.tensor_copy(kv[:, t, :], c.bank[4 + t][:]).then_inc(step, 1)
            dve.wait_ge(pe1, KD + MT + 1)
            dve.tensor_copy(kt[:].rearrange("p a n -> p (a n)"), c.bank[0][:]).then_inc(step, 1)

            def prepare(i, j, t):
                n = 4 * j + t
                for a in range(2):
                    dve.wait_ge(s_done, 16 * i + 2 * n + a + 1)
                    dve.tensor_reduce(nmax[:, t % 2, a:NM:2],
                                      c.bank[2 * (t % 2) + a][:].rearrange("p (h k) -> p h k", h=2), AX.X, ALU.max,
                                      negate=True).then_inc(max_done, 1)

            def normalize(i, j, t):
                n = 4 * j + t
                dve.wait_ge(exp_done, at(2 * NT * NM, i, NM * (n + 1)))
                dve.reciprocal(rtot[:, t % 2, :], tot[:, t % 2, :]).then_inc(r_done, 1)
                dve.wait_ge(r_done, 8 * i + n + 1)
                dve.wait_ge(tr_done, at(32, i, 4 * (n - 1)))
                for h in range(NM):
                    dve.tensor_scalar(pn[:, t % 2, h, :], p[:, t % 2, h, :], rtot[:, t % 2, h:h + 1], None,
                                      ALU.mult).then_inc(norm_done, 1)

            def take(i, j, t):
                n = 4 * j + t
                for b in range(2):
                    dve.wait_ge(tr_done, at(32, i, 4 * n + 2 * b + 2))
                    dve.tensor_copy(pt[:, j, 2 * b:2 * b + 2, :, t * P:(t + 1) * P],
                                    c.bank[4 + b][:].rearrange("p (h k q) -> p h k q", h=2, k=MT)).then_inc(pt_done, 1)

            def body(i, last):
                for j in range(2):
                    for t in range(NT):
                        normalize(i, j, t)
                        if t + 1 < NT:
                            prepare(i, j, t + 1)
                        take(i, j, t)
                    if not (last and j == 1):
                        prepare(i + j, 1 - j, 0)
                    dve.wait_ge(q_in[j], 32 * (i + 1))
                    dve.wait_ge(o_stored[j], at(16, i, 0))
                    for h in range(NM):
                        dve.wait_ge(o_done, 2 * NM * i + NM * j + h + 1)
                        dve.tensor_tensor(og[:, j, h, :], c.bank[6 + h % 2][0:HD, :], gate[:, j, h, :], ALU.mult
                                          ).then_inc(og_done, 1)

            prepare(0, 0, 0)
            with dve.Fori(0, NB // 2 - 1) as i:
                body(i, False)
            body(NB // 2 - 1, True)

        @block.scalar
        def _(act):
            act.sem_inc(exp_done, 2 * NT * NM)
            for j in range(2):
                act.sem_inc(o_stored[j], 16)
            act.wait_ge(step, 1 + 2 * MT + KD + MT)
            act.dma_start(mk_out.rearrange("l o (t p) h d -> p (l o t) (h d)", p=P), kv[:, :, 0:WM]).then_inc(kv_stored, 16)
            act.dma_start(mv_out.rearrange("l o (t p) h d -> p (l o t) (h d)", p=P), kv[:, :, WM:]).then_inc(kv_stored, 16)
            with act.Fori(0, NB // 2) as i:
                for j in range(2):
                    for t in range(NT):
                        n = 4 * j + t
                        act.wait_ge(norm_done, at(2 * NT * NM, i, NM * (n - 1)))
                        for h in range(NM):
                            act.wait_ge(max_done, 16 * i + 2 * n + h % 2 + 1)
                            act.activation(p[:, t % 2, h, :], c.bank[2 * (t % 2) + h % 2][:, (h // 2) * NMEM:(h // 2 + 1) * NMEM],
                                           ACT.Exp, bias=nmax[:, t % 2, h:h + 1], accum_out=tot[:, t % 2, h:h + 1]
                                           ).then_inc(exp_done, 1)
            for j in range(2):
                act.wait_ge(o_stored[j], at(16, NB // 2, 0))
            act.wait_ge(kv_stored, 32)

        @block.tensor
        def _(pe):
            pe.sem_inc(tr_done, 32)
            pe.wait_ge(step, 2 * MT + 1)
            for k in range(KD):
                if k >= 4:
                    pe.wait_ge(step, 2 * MT + 1 + k - 3)
                for t in range(MT):
                    tr = pe.transpose(c.bank[k % 4][:, t * P:(t + 1) * P], x[:, t, k * P:(k + 1) * P], c.ident[:])
                tr.then_inc(pe1, 1)
            pe.wait_ge(step, 2 * MT + 1 + KD)
            for t in range(MT):
                for k in range(KD):
                    mm = pe.matmul(c.bank[4 + t][:], xt[:, k, t * P:(t + 1) * P], w[:, k, :], start=(k == 0), stop=(k == KD - 1))
                mm.then_inc(pe1, 1)
            pe.wait_ge(step, 2 * MT + 1 + KD + MT)
            for a in range(2):
                for t in range(MT):
                    tr = pe.transpose(c.bank[0][:, a * NMEM + t * P:a * NMEM + (t + 1) * P], kv[:, t, a * P:(a + 1) * P], c.ident[:])
            tr.then_inc(pe1, 1)
            pe.wait_ge(step, 2 * MT + 2 + KD + MT)

            def scores(i, j, t):
                n = 4 * j + t
                if t == 0:
                    pe.wait_ge(q_in[j], 32 * (i + 1))
                pe.wait_ge(exp_done, at(2 * NT * NM, i, NM * (n - 1)))
                for h in range(NM):
                    r = HD * (h % 2)
                    mm = pe.matmul(c.bank[2 * (t % 2) + h % 2][:, (h // 2) * NMEM:(h // 2 + 1) * NMEM],
                                   q[r:r + HD, j, h // 2, t * P:(t + 1) * P], kt[r:r + HD, h // 2, :], start=True, stop=True)
                    if h >= 2:
                        mm.then_inc(s_done, 1)

            def body(i, last):
                for j in range(2):
                    for t in range(NT):
                        if t + 1 < NT:
                            scores(i, j, t + 1)
                        n = 4 * j + t
                        for h in range(NM):
                            pe.wait_ge(norm_done, at(2 * NT * NM, i, NM * n + h + 1))
                            if h % 2 == 0:
                                pe.wait_ge(pt_done, at(4 * NT, i, 2 * (n - 1) + h // 2 + 1))
                            for k in range(MT):
                                tr = pe.transpose(c.bank[4 + h // 2][:, ((h % 2) * MT + k) * P:((h % 2) * MT + k + 1) * P],
                                                  pn[:, t % 2, h, k * P:(k + 1) * P], c.ident[:])
                            tr.then_inc(tr_done, 1)
                    if not (last and j == 1):
                        scores(i + j, 1 - j, 0)
                    pe.wait_ge(pt_done, at(4 * NT, i, 2 * (4 * j + NT)))
                    for h in range(NM):
                        pe.wait_ge(og_done, at(2 * NM, i, NM * j + h - 1))
                        for k in range(MT):
                            mm = pe.matmul(c.bank[6 + h % 2][0:HD, :], kv[:, k, WM + h * HD:WM + (h + 1) * HD], pt[:, j, h, k, :],
                                           start=(k == 0), stop=(k == MT - 1))
                        mm.then_inc(o_done, 1)

            scores(0, 0, 0)
            with pe.Fori(0, NB // 2 - 1) as i:
                body(i, False)
            body(NB // 2 - 1, True)

        also(block)


def sample_project(nc, c, a, o, block):
    W, WB = 512, 3
    CH = [(c0, min(W, DIN - c0)) for c0 in range(0, DIN, W)]
    with ExitStack() as s:
        def sb(name, shape, dt=F32):
            return s.enter_context(nc.sbuf_tensor(name, shape, dt))

        def sem(name):
            return s.enter_context(nc.semaphore(name))

        x = sb("sx", [8, D])
        junk = sb("sx_junk", [8, D], BF16)
        ss, rin, rstd = sb("sx_ss", [8, 1]), sb("sx_rin", [8, 1]), sb("sx_rstd", [8, 1])
        gn = sb("sx_g", [P, KD])
        xt = sb("sx_t", [P, KD, 8])
        w = sb("sx_w", [P, WB, KD, W])
        z = sb("sx_z", [8, DIN])
        bf = sb("sx_bf", [8, NF])
        f = [sb(f"sx_f{i}", [8, NF]) for i in range(5)]
        loaded, step, powed, turned, prod, acted, stored = (
            sem(n) for n in ("sx_loaded", "sx_step", "sx_powed", "sx_turned", "sx_prod", "sx_acted", "sx_stored"))
        w_in = [sem(f"sx_w_in{j}") for j in range(WB)]
        w_v = a["w_in"].rearrange("o (k p) n -> (o p) k n", p=P)
        BASE = 5

        @block.sync
        def _(sp):
            with nc.allow_non_contiguous_dma(reason="1024 gains"):
                sp.dma_start(gn[:], a["g_norm"].rearrange("o (k p) -> p (o k)", p=P)).then_inc(loaded, 16)
            sp.dma_start(x[:], a["x_sample"].rearrange("b o d -> (b o) d")).then_inc(loaded, 16)
            sp.dma_start(bf[:], a["b_f"][0].partition_broadcast(8)).then_inc(loaded, 16)
            sp.wait_ge(step, BASE + len(CH))
            sp.dma_start(c.zs, z[:]).then_inc(stored, 16)
            sp.dma_start(o["k_sample"].rearrange("l b o h d -> (l b o) (h d)"), z[:, CK:CK + WF]).then_inc(stored, 16)
            sp.dma_start(o["v_sample"].rearrange("l b o h d -> (l b o) (h d)"), z[:, CV:CV + WF]).then_inc(stored, 16)
            sp.wait_ge(step, BASE + len(CH) + 5)
            sp.dma_start(o["logf_sample"].rearrange("l b o h -> (l b o) h"), c.lfs[:]).then_inc(stored, 16)
            sp.wait_ge(stored, 64)

        @block.gpsimd
        def _(pool):
            for n, (c0, cw) in enumerate(CH):
                if n == WB:
                    pool.wait_ge(step, 2)
                    pool.tensor_tensor(rstd[:], rin[:], c.minus_half[0:8, 0:1], ALU.pow).then_inc(powed, 1)
                if n >= WB:
                    pool.wait_ge(prod, n - WB + 1)
                pool.dma_start(w[:, n % WB, :, 0:cw], w_v[:, :, c0:c0 + cw]).then_inc(w_in[n % WB], 16)

        @block.vector
        def _(dve):
            n = [0]

            def done(ins):
                n[0] += 1
                ins.then_inc(step, 1)
                dve.wait_ge(step, n[0])

            dve.wait_ge(loaded, 48)
            done(dve.tensor_tensor_reduce(junk[:], x[:], x[:], 1.0, 0.0, ALU.mult, ALU.add, ss[:]))
            done(dve.tensor_scalar(rin[:], ss[:], 1.0 / D, EPS, ALU.mult, ALU.add))
            dve.wait_ge(powed, 1)
            done(dve.tensor_scalar(x[:], x[:], rstd[:], None, ALU.mult))
            dve.wait_ge(turned, 1)
            done(dve.tensor_tensor(xt[:], c.bank[0][:, 0:KD * 8].rearrange("p (k b) -> p k b", b=8),
                                   gn[:].unsqueeze(2).to_broadcast([P, KD, 8]), ALU.mult))
            done(dve.tensor_copy(f[0][:], bf[:]))
            for m, (c0, cw) in enumerate(CH):
                dve.wait_ge(prod, m + 1)
                done(dve.tensor_copy(z[:, c0:c0 + cw], c.bank[1 + m % 2][0:8, 0:cw]))
            done(dve.tensor_tensor(f[1][:], z[:, CF:CF + NF], f[0][:], ALU.add))
            done(dve.tensor_scalar(f[2][:], f[1][:], -1.0, None, ALU.mult))
            done(dve.tensor_tensor(f[3][:], f[1][:], f[2][:], ALU.min))
            done(dve.tensor_scalar(f[2][:], f[1][:], 0.0, None, ALU.min))
            dve.wait_ge(acted, 2)
            done(dve.tensor_tensor(c.lfs[:], f[2][:], f[4][:], ALU.subtract))

        @block.scalar
        def _(act):
            act.wait_ge(step, BASE + len(CH) + 3)
            act.activation(f[0][:], f[3][:], ACT.Exp).then_inc(acted, 1)
            act.wait_ge(acted, 1)
            act.activation(f[4][:], f[0][:], ACT.Ln, bias=1.0).then_inc(acted, 1)

        @block.tensor
        def _(pe):
            pe.wait_ge(step, 3)
            for k in range(KD):
                tr = pe.transpose(c.bank[0][:, k * 8:(k + 1) * 8], x[:, k * P:(k + 1) * P], c.ident[0:8, 0:8])
            tr.then_inc(turned, 1)
            pe.wait_ge(step, 4)
            for m, (c0, cw) in enumerate(CH):
                pe.wait_ge(w_in[m % WB], 16 * (m // WB + 1))
                if m >= 2:
                    pe.wait_ge(step, BASE + m - 1)
                for k in range(KD):
                    mm = pe.matmul(c.bank[1 + m % 2][0:8, 0:cw], xt[:, k, :], w[:, m % WB, k, 0:cw], start=(k == 0), stop=(k == KD - 1))
                mm.then_inc(prod, 1)


class Past:

    CP = 2
    SUMS = 6

    def __init__(self, nc, s, a):
        def sb(name, shape, dt=F32):
            return s.enter_context(nc.sbuf_tensor(name, shape, dt))

        self.nbs, self.npg = a["page_table"].shape
        self.chunks = self.npg // self.CP
        self.pages = sb("pages", [1, self.nbs * self.npg], I32)
        self.v, self.lf = sb("past_v", [P, self.nbs, self.npg, WF]), sb("past_lf", [P, self.nbs, self.npg, NF])
        self.qk = sb("past_qk", [P, self.nbs, self.npg, NF])
        self.k, self.q = sb("past_k", [P, 2, self.CP, WF]), sb("past_q", [P, WF])
        self.p_in, self.v_in, self.lf_in, self.q_in, self.summed, self.turn = (
            nc.alloc_semaphore("past_" + n) for n in ("p_in", "v_in", "lf_in", "q_in", "summed", "turn"))
        self.k_in = [nc.alloc_semaphore(f"past_k_in{j}") for j in range(2)]
        self.all_in = 16 * self.nbs * self.npg

    def load_sample(self, nc, sp, a, b):
        cv, cl = a["cache_v"].rearrange("o n p h d -> (o n) p (h d)"), a["cache_logf"].rearrange("o n p h -> (o n) p h")
        with nc.allow_non_contiguous_dma(reason="six log f a key"):
            for n in range(self.npg):
                page = sp.value_load(self.pages[0:1, bass.ds(b * self.npg + n, 1)], min_val=0, max_val=a["cache_v"].shape[1] - 1)
                sp.dma_start(self.v[:, b, n, :], cv[page]).then_inc(self.v_in, 16)
                sp.dma_start(self.lf[:, b, n, :], cl[page]).then_inc(self.lf_in, 16)

    def work(self, nc, pool, a, c):
        ck = a["cache_k"].rearrange("o n p h d -> (o n) p (h d)")
        c_q = c.zs[:, CQ:CQ + WF]
        NCK, CP = self.chunks, self.CP
        PER = 1 + self.SUMS

        def load(b, ch):
            for n in range(CP * ch, CP * (ch + 1)):
                page = pool.value_load(self.pages[0:1, bass.ds(b * self.npg + n, 1)], min_val=0, max_val=a["cache_v"].shape[1] - 1)
                pool.dma_start(self.k[:, ch % 2, n % CP, :], ck[page]).then_inc(self.k_in[ch % 2], 16)

        def body(b, last):
            for ch in range(NCK):
                n0 = PER * (NCK * b + ch)
                k = self.k[:, ch % 2]
                if ch == 0:
                    pool.wait_ge(self.q_in, 16 * (b + 1))
                pool.wait_ge(self.k_in[ch % 2], 16 * CP * (NCK // 2 * b + ch // 2 + 1))
                pool.tensor_tensor(k, k, self.q[:].unsqueeze(1).to_broadcast([P, CP, WF]), ALU.mult).then_inc(self.summed, 1)
                w = HD
                kv = k.rearrange("p n (h d) -> p n h d", d=HD)
                for m in range(self.SUMS):
                    w //= 2
                    pool.wait_ge(self.summed, n0 + m + 1)
                    if m == 0 and ch == NCK - 1 and not last:
                        pool.sem_inc(self.turn, 1)
                        pool.dma_start(self.q[:], c_q[b + 1].partition_broadcast(P)).then_inc(self.q_in, 16)
                    out = kv[:, :, :, 0:w]
                    if m == self.SUMS - 1:
                        pool.sem_inc(self.turn, 1)
                        out = self.qk[:, b, CP * ch:CP * (ch + 1), :].unsqueeze(3)
                    pool.tensor_tensor(out, kv[:, :, :, 0:w], kv[:, :, :, w:2 * w], ALU.add).then_inc(self.summed, 1)
                if ch + 2 < NCK or not last:
                    pool.wait_ge(self.summed, n0 + PER)
                    pool.sem_inc(self.turn, 1)
                    load(b + (ch + 2) // NCK, (ch + 2) % NCK)

        pool.dma_start(self.pages[:], a["page_table"].rearrange("(o b) n -> o (b n)", o=1)).then_inc(self.p_in, 16)
        pool.dma_start(self.q[:], c_q[0].partition_broadcast(P)).then_inc(self.q_in, 16)
        pool.wait_ge(self.p_in, 16)
        load(0, 0)
        load(0, 1)
        with pool.Fori(0, self.nbs - 1) as b:
            body(b, False)
        body(self.nbs - 1, True)
        pool.wait_ge(self.summed, PER * NCK * self.nbs)


def ssm(nc, c, a, ssm_prompt, ssm_sample, past):
    NB = 4
    with ExitStack() as s:
        def sb(name, shape, dt=F32):
            return s.enter_context(nc.sbuf_tensor(name, shape, dt))

        def sem(name):
            return s.enter_context(nc.semaphore(name))

        y = sb("ssm_y", [P, NB, STEP, WS])
        turns = sb("ssm_turns", [P, 2, O_R])
        gp = sb("ssm_gp", [P, 2, GPW - O_R])
        u = sb("ssm_u", [P, 2, NB, SC])
        us = sb("ssm_us", [8, 2, SC])
        ut = sb("ssm_ut", [P, 2, NCH])
        sm = sb("ssm_sm", [P, 2, 2 * SC + 8])
        toep = sb("ssm_toep", [P, 2, SC])
        wj = sb("ssm_wj", [P, 2, SC])
        vc, vs = sb("ssm_vc", [P, 2, NCH]), sb("ssm_vs", [P, 2, NCH])
        vr, gs = vc, vs
        cg, sg = sb("ssm_cg", [P, 2, NCH + 1]), sb("ssm_sg", [P, 2, NCH + 1])
        hl = sb("ssm_hl", [P, 2, G])
        table = sb("ssm_table", [P, 1])
        h0in = vc[0:96, 0, 0:4 * NS].rearrange("q (t p r) -> q t p r", t=2, r=2)
        h0p = vs[0:96].rearrange("q x (y r p) -> q x y r p", y=4, r=2)[:, :, 0:2]
        h0, h0s, hn, hm, vsm = (sb(n, [P, 8, G]) for n in ("ssm_h0", "ssm_h0s", "ssm_hn", "ssm_hm", "ssm_vsm"))
        ab = sb("ssm_ab", [P, G, 2])
        yst = sb("ssm_yst", [GC, G, 8])
        hlt = u[0:G, 0, 0:2, :]
        hlo = u[0:G, 1, 0, :].rearrange("g (p r) -> g p r", r=2)
        hno = u[0:96, 1, 2:4, :].rearrange("q t (p r) -> q t p r", r=2)
        g_in = [sem("ssm_in0"), sem("ssm_in1")]
        u_in = [sem("ssm_u_in0"), sem("ssm_u_in1")]
        turns_in = [sem("ssm_turns_in0"), sem("ssm_turns_in1")]
        h_in, prep, prep_pe, zeroed = sem("ssm_h_in"), sem("ssm_prep"), sem("ssm_prep_pe"), sem("ssm_zeroed")
        ut_tr, sm_tr, ut_done, sm_done, toep_done = (sem(n) for n in ("ssm_ut_tr", "ssm_sm_tr", "ssm_ut_d", "ssm_sm_d", "ssm_toep_d"))
        v_done, turned, scanned, cg_done, small = (sem(n) for n in ("ssm_v", "ssm_turned", "ssm_scan", "ssm_cg_d", "ssm_small"))
        y_done, y_out = sem("ssm_y_d"), sem("ssm_y_out")
        tail, tail_pe, ends, stored = sem("ssm_tail"), sem("ssm_tail_pe"), sem("ssm_ends"), sem("ssm_stored")
        block = s.enter_context(nc.Block())
        u_v = c.u_chunks.rearrange("b p (g w) -> g p b w", g=G)
        z_u = c.zs[:, CU:CU + WS].rearrange("b (g c) -> g b c", c=GC)

        @block.sync
        def _(sp):
            sp.dma_start(h0in, a["state_ssm"].rearrange("o b g p r -> (o b g) (p r)").rearrange("(t q) w -> q t w", q=96)
                         .rearrange("q t (p r) -> q t p r", r=2)).then_inc(h_in, 16)
            with nc.allow_non_contiguous_dma(reason="two columns of each group"):
                sp.dma_start(ab[:], c.ssm_gp[:, :, O_A1:O_A1 + 2].rearrange("g p w -> p g w")).then_inc(h_in, 16)
            sp.wait_ge(zeroed, 1)
            def groups(i, with_past):
                for j in range(2):
                    sp.wait_ge(sm_tr, at(2, i, j - 1))
                    sp.dma_start(u[:, j], u_v[2 * i + j]).then_inc(u_in[j], 16)
                    sp.dma_start(us[:, j, SC - GC:SC], z_u[2 * i + j]).then_inc(u_in[j], 16)
                for j in range(2):
                    sp.wait_ge(cg_done, at(4, i, 2 * j - 2))
                    sp.dma_start(turns[:, j], c.ssm_gp[2 * i + j, :, 0:O_R]).then_inc(turns_in[j], 16)
                for j in range(2):
                    sp.wait_ge(y_done, at(2, i, j - 1))
                    sp.dma_start(gp[:, j], c.ssm_gp[2 * i + j, :, O_R:GPW]).then_inc(g_in[j], 16)
                if with_past:
                    past.load_sample(nc, sp, a, i)

            sp.wait_ge(past.p_in, 16)
            with sp.Fori(0, past.nbs) as i:
                groups(i, True)
            with sp.Fori(past.nbs, G // 2) as i:
                groups(i, False)
            sp.wait_ge(y_out, at(2, G // 2, 0))
            sp.dma_start(c.y_chunks.rearrange("b p t f -> p b (t f)"), y[:].rearrange("p b t f -> p b (t f)")).then_inc(stored, 16)
            sp.dma_start(c.ys_t.rearrange("(g c) b -> c g b", c=GC), yst[:]).then_inc(stored, 16)
            sp.wait_ge(ends, 5)
            sp.dma_start(ssm_prompt.rearrange("o b g p r -> (o b g) p r"), hlo).then_inc(stored, 16)
            sp.dma_start(ssm_sample.rearrange("o b g p r -> (o b g) (p r)").rearrange("(t q) w -> q t w", q=96), hno
                         .rearrange("q t p r -> q t (p r)")).then_inc(stored, 16)
            sp.wait_ge(stored, 64)

        @block.gpsimd
        def _(pool):
            pool.memset(us[:], 0.0).then_inc(zeroed, 1)
            past.work(nc, pool, a, c)

        @block.vector
        def _(dve):
            dve.sem_inc(cg_done, 4)
            dve.sem_inc(small, 2)
            dve.sem_inc(turned, 4)
            dve.sem_inc(toep_done, 2)
            M, A_, S_ = ALU.mult, ALU.add, ALU.subtract
            dve.memset(cg[:, :, 0], 0.0).then_inc(prep, 1)
            dve.memset(sg[:, :, 0], 0.0).then_inc(prep, 1)
            dve.wait_ge(h_in, 32)
            for r in range(2):
                dve.tensor_copy(h0p[:, :, 0, r, :], h0in[:, :, :, r]).then_inc(prep, 1)
                dve.tensor_copy(h0p[:, :, 1, r, :], h0in[:, :, :, 1 - r]).then_inc(prep, 1)
            dve.wait_ge(prep_pe, 1)
            dve.tensor_copy(h0[:].rearrange("p b g -> p (b g)"), c.bank[0][:, 0:8 * G]).then_inc(prep, 1)
            dve.tensor_copy(h0s[:].rearrange("p b g -> p (b g)"), c.bank[1][:, 0:8 * G]).then_inc(prep, 1)
            dve.wait_ge(prep, 8)
            with dve.Fori(0, G // 2) as i:
                for j in range(2):
                    g = 2 * i + j
                    dve.wait_ge(sm_done, at(2, i, j + 1))
                    dve.wait_ge(y_done, at(2, i, j - 1))
                    dve.scalar_tensor_tensor(toep[:, j], c.ident[:], gp[:, j, O_D - O_R:O_D - O_R + 1], sm[:, j, SC:2 * SC], M, A_)
                    dve.tensor_copy(wj[:, j, 0:HD], sm[:, j, HD:SC])
                    dve.tensor_scalar(wj[:, j, HD:SC], sm[:, j, 0:HD], -1.0, None, M).then_inc(toep_done, 1)
                for j in range(2):
                    g = 2 * i + j
                    cosT, sinT = turns[:, j, O_COS:O_COS + NCH], turns[:, j, O_SIN:O_SIN + NCH]
                    dve.wait_ge(turns_in[j], 16 * (i + 1))
                    dve.wait_ge(v_done, 2 * i + j + 1)
                    dve.tensor_tensor(vc[:, j], c.bank[4][:], cosT, M).then_inc(turned, 1)
                    dve.tensor_tensor(vs[:, j], c.bank[5][:], sinT, M).then_inc(turned, 1)
                    dve.wait_ge(turned, at(4, i, 2 * j + 2))
                    dve.tensor_tensor(vr[:, j], vc[:, j], vs[:, j], A_).then_inc(scanned, 1)
                    dve.wait_ge(scanned, 4 * i + 2 * j + 1)
                    dve.tensor_tensor_scan(gs[:, j], gp[:, j, O_R8 - O_R:O_R8 - O_R + 1].to_broadcast([P, NCH]), vr[:, j], 0.0, M, A_
                                           ).then_inc(scanned, 1)
                    dve.wait_ge(scanned, 4 * i + 2 * j + 2)
                    dve.wait_ge(y_done, at(2, i, j - 1))
                    dve.tensor_tensor(cg[:, j, 1:NCH + 1], cosT, gs[:, j], M).then_inc(cg_done, 1)
                    dve.tensor_tensor(sg[:, j, 1:NCH + 1], sinT, gs[:, j], M).then_inc(cg_done, 1)
                    dve.wait_ge(cg_done, at(4, i, 2 * j + 2))
                    dve.tensor_copy(hl[:, 0, bass.ds(g, 1)], cg[:, j, NCH:NCH + 1])
                    dve.tensor_copy(hl[:, 1, bass.ds(g, 1)], sg[:, j, NCH:NCH + 1]).then_inc(small, 1)
            bc = [P, 8, G]
            dve.wait_ge(y_out, at(2, G // 2, 0))
            dve.tensor_tensor(hn[:], h0[:], ab[:, :, 0].unsqueeze(1).to_broadcast(bc), M).then_inc(tail, 1)
            dve.tensor_tensor(hm[:], h0s[:], ab[:, :, 1].unsqueeze(1).to_broadcast(bc), M).then_inc(tail, 1)
            dve.wait_ge(tail, 2)
            dve.tensor_tensor(hn[:], hn[:], hm[:], A_).then_inc(tail, 1)
            dve.wait_ge(tail, 3)
            dve.tensor_tensor(hn[:], hn[:], vsm[:], A_).then_inc(tail, 1)
            dve.wait_ge(tail_pe, 1)
            dve.tensor_copy(hlt.rearrange("g a w -> g (a w)"), c.bank[0][0:G, 0:2 * P]).then_inc(ends, 1)
            dve.wait_ge(ends, 1)
            dve.tensor_tensor(hlo[:, :, 0], hlt[:, 0, 0:HD], hlt[:, 1, HD:P], S_).then_inc(ends, 1)
            dve.tensor_tensor(hlo[:, :, 1], hlt[:, 0, HD:P], hlt[:, 1, 0:HD], A_).then_inc(ends, 1)
            for r in range(2):
                dve.tensor_copy(hno[:, :, :, r], c.bank[1][0:96, 0:2 * P].rearrange("q (t r p) -> q t p r", t=2, r=2)[:, :, :, r]
                                ).then_inc(ends, 1)

        @block.scalar
        def _(act):
            act.sem_inc(sm_done, 2)
            act.sem_inc(ut_done, 2)
            act.sem_inc(y_out, 2)
            with act.Fori(0, G // 2) as i:
                act.wait_ge(y_out, at(2, i, 0))
                act.activation(table[:], c.minus_half[:, 0:1], ACT.Gelu)
                for j in range(2):
                    act.wait_ge(ut_tr, 2 * i + j + 1)
                    act.wait_ge(y_done, at(2, i, j - 1))
                    act.activation(ut[:, j], c.bank[j][:], ACT.Copy).then_inc(ut_done, 1)
                    act.wait_ge(sm_tr, at(2, i, j + 1))
                    act.activation(sm[:, j], c.bank[2 + j][:, 0:2 * SC + 8], ACT.Copy).then_inc(sm_done, 1)
                for j in range(2):
                    g = 2 * i + j
                    act.wait_ge(y_done, at(2, i, j + 1))
                    act.activation(vsm[:, :, g], c.bank[7][:, 0:8], ACT.Copy)
                    act.activation(yst[:, g, :], c.bank[7][0:GC, 16:24], ACT.Gelu)
                    act.activation(y[:, :, :, bass.ds(g * GC, GC)], c.bank[6][:].rearrange("p (b t c) -> p b t c", b=NB, c=GC),
                                   ACT.Gelu).then_inc(y_out, 1)

        @block.tensor
        def _(pe):
            pe.sem_inc(y_done, 2)
            pe.sem_inc(sm_tr, 2)
            pe.wait_ge(prep, 6)
            for k in range(2):
                for t in range(2):
                    tr = pe.transpose(c.bank[k][:, t * 96:(t + 1) * 96], h0p[:, t, k, :, :].rearrange("q r p -> q (r p)"), c.ident[0:96, 0:96])
            tr.then_inc(prep_pe, 1)
            pe.wait_ge(prep, 8)
            with pe.Fori(0, G // 2) as i:
                for j in range(2):
                    pe.wait_ge(u_in[j], 32 * (i + 1))
                    pe.wait_ge(g_in[j], 16 * (i + 1))
                    pe.wait_ge(ut_done, at(2, i, j - 1))
                    for b in range(NB):
                        tr = pe.transpose(c.bank[j][:, b * P:(b + 1) * P], u[:, j, b, :], c.ident[:])
                    tr.then_inc(ut_tr, 1)
                    pe.wait_ge(sm_done, at(2, i, j - 1))
                    small_b = c.bank[2 + j]
                    pe.transpose(small_b[:, 0:SC], gp[:, j, 0:SC], c.ident[:])
                    for t in range(STEP):
                        w0 = (STEP - 1 - t) * GC
                        pe.matmul(small_b[:, SC + t * GC:SC + (t + 1) * GC], gp[:, j, w0:w0 + SC], gp[:, j, O_CC - O_R:O_CC - O_R + GC],
                                  start=True, stop=True)
                    pe.transpose(small_b[:, 2 * SC:2 * SC + 8], us[:, j, :], c.ident[0:8, 0:8]).then_inc(sm_tr, 1)
                for j in range(2):
                    g = 2 * i + j
                    pe.wait_ge(ut_done, at(2, i, j + 1))
                    pe.wait_ge(toep_done, at(2, i, j + 1))
                    pe.wait_ge(turned, at(4, i, 2 * j))
                    pe.matmul(c.bank[4][:], sm[:, j, 0:SC], ut[:, j], start=True, stop=True)
                    pe.matmul(c.bank[5][:], wj[:, j], ut[:, j], start=True, stop=True).then_inc(v_done, 1)
                for j in range(2):
                    g = 2 * i + j
                    w1, w2 = gp[:, j, O_W1 - O_R:O_W1 - O_R + SC], gp[:, j, O_W2 - O_R:O_W2 - O_R + SC]
                    pe.wait_ge(cg_done, at(4, i, 2 * j + 2))
                    pe.wait_ge(y_out, at(2, i, j))
                    pe.matmul(c.bank[7][:, 0:8], sm[:, j, 0:SC], sm[:, j, 2 * SC:], start=True, stop=True)
                    for b in range(NB):
                        dst = c.bank[6][:, b * P:(b + 1) * P]
                        pe.matmul(dst, ut[:, j, b * P:(b + 1) * P], toep[:, j], start=True, stop=False)
                        pe.matmul(dst, cg[:, j, b * P:(b + 1) * P], w1, start=False, stop=False)
                        pe.matmul(dst, sg[:, j, b * P:(b + 1) * P], w2, start=False, stop=True)
                    dst = c.bank[7][0:GC, 16:24]
                    pe.matmul(dst, toep[:, j, SC - GC:SC], sm[:, j, 2 * SC:], start=True, stop=False)
                    pe.matmul(dst, w1[:, 0:GC], h0[:, :, g], start=False, stop=True).then_inc(y_done, 1)
            pe.wait_ge(small, at(2, G // 2, 0))
            pe.wait_ge(tail, 4)
            for r in range(2):
                pe.transpose(c.bank[0][0:G, r * P:(r + 1) * P], hl[:, r, :], c.ident[:])
            for t in range(2):
                tr = pe.transpose(c.bank[1][0:96, t * P:(t + 1) * P], hn[:].rearrange("p b g -> p (b g)")[:, t * 96:(t + 1) * 96], c.ident[:])
            tr.then_inc(tail_pe, 1)


def sample_attend(nc, c, a, past):
    NBS, NPG = a["page_table"].shape
    NPOOL = a["cache_k"].shape[1]
    NMT = NMEM // P
    BH, BM = NBS * NF, NBS * NM
    with ExitStack() as s:
        def sb(name, shape, dt=F32):
            return s.enter_context(nc.sbuf_tensor(name, shape, dt))

        def sem(name):
            return s.enter_context(nc.semaphore(name))

        pages, lf, vb = past.pages, past.lf, past.v
        z = sb("at_z", [NBS, DIN])
        prod = sb("at_prod", [P, NPG, WF])
        lfx = sb("at_lfx", [P, NBS, NPG, NF])
        sc = past.qk
        mk, mv = sb("at_mk", [P, NBS, NMT, WM]), sb("at_mv", [P, NBS, NMT, WM])
        mq = sb("at_mq", [P, NBS, WM])
        ms = sb("at_ms", [P, NBS, NMT, NM])
        mx = sb("at_mx", [P, BH + BM])
        mxa = sb("at_mxa", [P, BH + BM])
        qk = sb("at_qk", [NBS, WF])
        new = sb("at_new", [NBS, 2, NF])
        newd = sb("at_newd", [NBS, 2, NBS, NF])
        newb = sb("at_newb", [P, 2, NBS, NF])
        pn = sb("at_pn", [P, NBS, NF])
        part = sb("at_part", [P, BH + BM])
        rt = sb("at_rt", [P, BH + BM])
        zt = sb("at_zt", [P, 11, NBS])
        zg = sb("at_zg", [P, 8, NBS])
        oh = sb("at_oh", [NF, NBS, WF])
        of = sb("at_of", [NBS, WF])
        ohs, ofs = sem("at_ohs"), sem("at_ofs")
        t0 = sb("at_t0", [P, 3, NBS])
        loaded, m_in = sem("at_loaded"), sem("at_m_in")
        step, pe_, act_, pool_ = sem("at_step"), sem("at_pe"), sem("at_act"), sem("at_pool")
        ov, o_out = sem("at_ov"), sem("at_oo")
        block = s.enter_context(nc.Block())
        LOADS = 16 * 2

        NEWD_AT, LFX_AT, MAX_AT, EXP_AT, SUM_AT, NORM_AT = 6, 15, 23, 27, 30, 35

        @block.sync
        def _(sp):
            sp.dma_start(z[:], c.zs).then_inc(loaded, 16)
            sp.dma_start(mq[:], c.zs[:, CQM:CQM + WM].partition_broadcast(P)).then_inc(loaded, 16)

            sp.wait_ge(ohs, NBS)
            for h in range(NF):
                sp.dma_start(of[:, h * HD:(h + 1) * HD], oh[h:h + 1, :, h * HD:(h + 1) * HD]).then_inc(ofs, 16)

        @block.scalar
        def _(act):
            act.dma_start(mk[:], a["cache_mem_k"].rearrange("o b (t p) h d -> p (o b) t (h d)", p=P)).then_inc(m_in, 16)
            act.dma_start(mv[:], a["cache_mem_v"].rearrange("o b (t p) h d -> p (o b) t (h d)", p=P)).then_inc(m_in, 16)
            act.wait_ge(pe_, 1)
            act.activation(zg[:], c.bank[0][:, 3 * NBS:11 * NBS].rearrange("p (k b) -> p k b", b=NBS), ACT.Silu).then_inc(act_, 1)
            act.wait_ge(step, EXP_AT)
            act.activation(sc[:], sc[:], ACT.Exp).then_inc(act_, 1)
            act.activation(ms[:], ms[:], ACT.Exp, scale=HD ** -0.5).then_inc(act_, 1)
            act.activation(pn[:], pn[:], ACT.Exp).then_inc(act_, 1)

        @block.gpsimd
        def _(pool):
            pool.wait_ge(step, MAX_AT)
            pool.partition_all_reduce(mxa[:], mx[:], P, bass.bass_isa.ReduceOp.max).then_inc(pool_, 1)


        @block.vector
        def _(dve):
            n = [0]
            M, A_, S_ = ALU.mult, ALU.add, ALU.subtract

            def done(ins):
                n[0] += 1
                ins.then_inc(step, 1)
                dve.wait_ge(step, n[0])

            dve.wait_ge(loaded, LOADS)
            done(dve.tensor_copy(new[:, 1, :], c.lfs[:]))
            done(dve.tensor_tensor(qk[:], z[:, CQ:CQ + WF], z[:, CK:CK + WF], M))
            done(dve.tensor_reduce(new[:, 0, :], qk[:].rearrange("b (h d) -> b h d", d=HD), AX.X, A_))
            done(dve.tensor_scalar(new[:, 0, :], new[:, 0, :], HD ** -0.5, None, M))
            for k in range(2):
                done(dve.tensor_tensor(newd[:, k], c.ident[0:NBS, 0:NBS].unsqueeze(2).to_broadcast([NBS, NBS, NF]),
                                       new[:, k, :].unsqueeze(1).to_broadcast([NBS, NBS, NF]), M))
            assert n[0] == NEWD_AT
            dve.wait_ge(past.lf_in, past.all_in)
            done(dve.memset(lfx[:, :, NPG - 1, :], 0.0))
            for g in range(NPG - 2, -1, -1):
                done(dve.tensor_tensor(lfx[:, :, g, :], lfx[:, :, g + 1, :], lf[:, :, g + 1, :], A_))
            dve.wait_ge(pe_, 2)
            done(dve.tensor_copy(newb[:].rearrange("p k b h -> p (k b h)"), c.bank[1][:, 0:2 * BH]))
            assert n[0] == LFX_AT
            dve.wait_ge(pe_, 3)
            bf = c.bank[2][:, 0:NBS * NPG * NF]
            scf = sc[:].rearrange("p b n h -> p (b n h)")
            done(dve.scalar_tensor_tensor(scf, scf, HD ** -0.5, bf, M, A_))
            done(dve.tensor_tensor(sc[:], sc[:], newb[:, 1].unsqueeze(2).to_broadcast([P, NBS, NPG, NF]), A_))
            done(dve.tensor_reduce(mx[:, 0:BH].rearrange("p (b h) -> p b h", h=NF), sc[:].rearrange("p b n h -> p b h n"), AX.X, ALU.max))
            dve.wait_ge(m_in, 32)
            for t in range(NMT):
                done(dve.tensor_tensor(prod[:, :, 0:WM], mk[:, :, t, :], mq[:], M))
                done(dve.tensor_reduce(ms[:, :, t, :], prod[:, :, 0:WM].rearrange("p b (h d) -> p b h d", d=HD), AX.X, A_))
            done(dve.tensor_reduce(mx[:, BH:].rearrange("p (b h) -> p b h", h=NM), ms[:].rearrange("p b t h -> p b h t"), AX.X, ALU.max))
            assert n[0] == MAX_AT, n[0]
            dve.wait_ge(pool_, 1)
            m3 = mxa[:, 0:BH].rearrange("p (b h) -> p b h", h=NF)
            mm3 = mxa[:, BH:].rearrange("p (b h) -> p b h", h=NM)
            done(dve.tensor_tensor(m3, m3, newb[:, 0], ALU.max))
            done(dve.tensor_tensor(sc[:], sc[:], m3.unsqueeze(2).to_broadcast([P, NBS, NPG, NF]), S_))
            done(dve.tensor_tensor(ms[:], ms[:], mm3.unsqueeze(2).to_broadcast([P, NBS, NMT, NM]), S_))
            done(dve.tensor_tensor(pn[:], newb[:, 0], m3, S_))
            assert n[0] == EXP_AT, n[0]
            dve.wait_ge(act_, 4)
            done(dve.tensor_reduce(part[:, 0:BH].rearrange("p (b h) -> p b h", h=NF), sc[:].rearrange("p b n h -> p b h n"), AX.X, A_))
            done(dve.tensor_reduce(part[:, BH:].rearrange("p (b h) -> p b h", h=NM), ms[:].rearrange("p b t h -> p b h t"), AX.X, A_))
            done(dve.tensor_copy(zt[:, 0:3], c.bank[0][:, 0:3 * NBS].rearrange("p (k b) -> p k b", b=NBS)))
            assert n[0] == SUM_AT
            dve.wait_ge(pe_, 4)
            r3, q3 = rt[:, 0:BH].rearrange("p (b h) -> p b h", h=NF), rt[:, BH:].rearrange("p (b h) -> p b h", h=NM)
            done(dve.tensor_tensor(rt[:, 0:BH], c.bank[3][:, 0:BH], pn[:].rearrange("p b h -> p (b h)"), A_))
            done(dve.tensor_copy(rt[:, BH:], c.bank[3][:, BH:BH + BM]))
            done(dve.reciprocal(rt[:], rt[:]))
            done(dve.tensor_tensor(sc[:], sc[:], r3.unsqueeze(2).to_broadcast([P, NBS, NPG, NF]), M))
            done(dve.tensor_tensor(ms[:], ms[:], q3.unsqueeze(2).to_broadcast([P, NBS, NMT, NM]), M))
            assert n[0] == NORM_AT
            done(dve.tensor_tensor(pn[:], pn[:], r3, M))
            for r in range(2):
                rows = slice(HD * r, HD * (r + 1))
                done(dve.tensor_tensor(t0[rows], zt[rows, 0:3], pn[rows].rearrange("p b (k r) -> p r k b", r=2)[:, r], M))
            for b in range(NBS):
                dve.wait_ge(ov, b + 1)
                dve.tensor_copy(oh[:, b, :], c.bank[4 + b % 2][0:NF, 0:WF]).then_inc(ohs, 1)
            dve.wait_ge(o_out, 1)
            done(dve.tensor_tensor(t0[:], t0[:], c.bank[7][:, 0:3 * NBS].rearrange("p (k b) -> p k b", b=NBS), A_))
            done(dve.tensor_tensor(c.mix_s[:, 0:3], t0[:], zg[:, 0:3], M))
            dve.wait_ge(pe_, 5)
            om = c.bank[6][:, 0:NBS * NM].rearrange("p (b k r) -> p k b r", r=2, k=2)
            for r in range(2):
                rows = slice(HD * r, HD * (r + 1))
                done(dve.tensor_tensor(c.mix_s[rows, 6:8], om[rows, :, :, r], zg[rows, 6:8], M))
            done(dve.tensor_copy(c.mix_s[:, 3:6], zg[:, 3:6]))

        @block.tensor
        def _(pe):
            pe.wait_ge(loaded, LOADS)
            cols = [CV + k * P for k in range(3)] + [CGA + k * P for k in range(3)] + [CGS + k * P for k in range(3)] + \
                   [CGM + k * P for k in range(2)]
            for k, c0 in enumerate(cols):
                tr = pe.transpose(c.bank[0][:, k * NBS:(k + 1) * NBS], z[:, c0:c0 + P], c.ident[0:NBS, 0:NBS])
            tr.then_inc(pe_, 1)
            pe.wait_ge(step, NEWD_AT)
            pe.matmul(c.bank[1][:, 0:2 * BH], c.ones[0:NBS, :], newd[:].rearrange("q k b h -> q (k b h)"), start=True, stop=True
                      ).then_inc(pe_, 1)
            pe.wait_ge(step, LFX_AT)
            bf = c.bank[2][:, 0:NBS * NPG * NF]
            pe.matmul(bf, c.lower_strict[:], lf[:].rearrange("p b n h -> p (b n h)"), start=True, stop=False)
            pe.matmul(bf, c.ones[:], lfx[:].rearrange("p b n h -> p (b n h)"), start=False, stop=True).then_inc(pe_, 1)
            pe.wait_ge(step, SUM_AT)
            pe.matmul(c.bank[3][:, 0:BH + BM], c.ones[:], part[:], start=True, stop=True).then_inc(pe_, 1)
            pe.wait_ge(step, NORM_AT)
            for b in range(NBS):
                for k in range(2):
                    dst = c.bank[6][:, b * NM + 2 * k:b * NM + 2 * k + 2]
                    for t in range(NMT):
                        mm = pe.matmul(dst, mv[:, b, t, k * P:(k + 1) * P], ms[:, b, t, 2 * k:2 * k + 2], start=(t == 0), stop=(t == NMT - 1))
            mm.then_inc(pe_, 1)
            pe.wait_ge(past.v_in, past.all_in)
            for b in range(NBS):
                if b >= 2:
                    pe.wait_ge(ohs, b - 1)
                for g in range(NPG):
                    mm = pe.matmul(c.bank[4 + b % 2][0:NF, 0:WF], sc[:, b, g, :], vb[:, b, g, :], start=(g == 0), stop=(g == NPG - 1))
                mm.then_inc(ov, 1)
            pe.wait_ge(ofs, 16 * NF)
            for k in range(3):
                tr = pe.transpose(c.bank[7][:, k * NBS:(k + 1) * NBS], of[:, k * P:(k + 1) * P], c.ident[0:NBS, 0:NBS])
            tr.then_inc(o_out, 1)


def mix_out(nc, c, a, y_prompt, y_sample):
    NB, TB = T // 512, 512
    NT = TB // P
    NKS = WS // P
    with ExitStack() as s:
        def sb(name, shape, dt=F32):
            return s.enter_context(nc.sbuf_tensor(name, shape, dt))

        def sem(name):
            return s.enter_context(nc.semaphore(name))

        whi, wlo = sb("wo_hi", [P, KD, D], F32R), sb("wo_lo", [P, KD, D], F32R)
        wraw = sb("wo_raw", [P, 2, D])
        wg = sb("w_glu", [P, NKS, WS])
        bg = sb("b_glu", [P, NKS])
        gf = sb("g_fin", [P, D])
        am = sb("mx_am", [P, 5, TB])
        gate = sb("mx_gate", [P, NKS, TB])
        yc = sb("mx_y", [HD, STEP, WS])
        st = sb("mx_st", [P, NKS, TB])
        sig = sb("mx_sig", [P, NKS, TB])
        mhi, mlo = sb("mx_hi", [P, 2, KD, TB], F32R), sb("mx_lo", [P, 2, KD, TB], F32R)
        xr = sb("mx_x", [P, 2, D])
        xo = sb("mx_xo", [P, 2, D])
        stats = sb("mx_stats", [P, 3, 2])
        ss, rin, rstd = (stats[:, k] for k in range(3))
        junk = sb("mx_junk", [P, D], BF16)
        yss = sb("mx_ys", [P, NKS, 8])
        sgs = sb("mx_sgs", [P, NKS, 8])
        shi, slo = sb("mx_shi", [P, KD, 8], F32R), sb("mx_slo", [P, KD, 8], F32R)
        xs = wraw[0:8, 0]
        w_in = [sem("wo_in0"), sem("wo_in1")]
        p_in, xs_in, w_hi, w_split = sem("mx_p_in"), sem("mx_xs_in"), sem("wo_hi_d"), sem("wo_split")
        step, spe, sact, spool = sem("mx_step"), sem("mx_spe"), sem("mx_sact"), sem("mx_spool")
        in_ = sem("mx_in")
        tr_done, st_done, glu_done, sig_done = sem("mx_tr"), sem("mx_st_d"), sem("mx_glu"), sem("mx_sig_d")
        s_done, hi_done, lo_done = sem("mx_s_d"), sem("mx_hi_d"), sem("mx_lo_d")
        x_in = [sem("mx_x0"), sem("mx_x1")]
        y_st = [sem("mx_y0"), sem("mx_y1")]
        op_done, xo_done, sq_done, mean_done, rs_done, y_done = (
            sem(n) for n in ("mx_op", "mx_xo_d", "mx_sq", "mx_mean", "mx_rs", "mx_y_d"))
        block = s.enter_context(nc.Block())
        wo = a["w_out"].rearrange("o (k p) n -> (o k) p n", p=P)
        m_v = c.mix_t.rearrange("(k p) (b t) -> b p k t", p=P, t=TB)
        g_v = c.gate_t.rearrange("(k p) (b t) -> b p k t", p=P, t=TB)
        y_v = c.y_chunks.rearrange("b (a p) t f -> (b a) p t f", p=HD)
        x_v = a["x_prompt"].rearrange("o (b t p) d -> (o b) t p d", p=P, t=NT)
        o_v = y_prompt.rearrange("o (b t p) d -> (o b) t p d", p=P, t=NT)
        M, A_, S_ = ALU.mult, ALU.add, ALU.subtract

        def schedule(engine, ready, project, gate_samples, project_samples):
            ready(0, 0)
            with engine.Fori(0, NB // 2 - 1) as i:
                ready(2 * i + 1, 1)
                project(2 * i, 0)
                ready(2 * i + 2, 0)
                project(2 * i + 1, 1)
            ready(NB - 1, 1)
            gate_samples()
            project(NB - 2, 0)
            project_samples()
            project(NB - 1, 1)

        GATED_AT, SPLIT_AT, ADDED_AT, MEAN_AT, LAST_AT = 6, 8, 10, 12, 13

        @block.sync
        def _(sp):
            with nc.allow_non_contiguous_dma(reason="384 biases"):
                sp.dma_start(bg[:], a["b_glu"].rearrange("o (k p) -> p (o k)", p=P)).then_inc(p_in, 16)
            sp.dma_start(wg[:], a["w_glu"].rearrange("o (k p) n -> p (o k) n", p=P)).then_inc(p_in, 16)
            sp.dma_start(gf[:], a["g_final"].partition_broadcast(P)).then_inc(p_in, 16)
            sp.dma_start(yss[:], c.ys_t.rearrange("(k p) b -> p k b", p=P)).then_inc(p_in, 16)

            def ready(n, j):
                sp.wait_ge(lo_done, at(KD, n, 0))
                sp.dma_start(am[:, 0:3], m_v[n, :, 0:3, :]).then_inc(in_, 16)
                sp.dma_start(am[:, 3:5], m_v[n, :, 6:8, :]).then_inc(in_, 16)
                sp.dma_start(gate[:], g_v[n, :, 3:6, :]).then_inc(in_, 16)
                sp.dma_start(yc[:], y_v[n]).then_inc(in_, 16)

            def project(n, j):
                for t in range(NT):
                    sp.wait_ge(xo_done, at(NT, n, t - 1))
                    sp.dma_start(xr[:, t % 2], x_v[n, t]).then_inc(x_in[t % 2], 16)

            schedule(sp, ready, project, lambda: None, lambda: None)

        @block.gpsimd
        def _(pool):
            for k in range(KD):
                if k >= 2:
                    pool.wait_ge(w_split, k - 1)
                pool.dma_start(wraw[:, k % 2], wo[k]).then_inc(w_in[k % 2], 16)
            pool.wait_ge(w_split, KD)
            pool.dma_start(xs, a["x_sample"].rearrange("b o d -> (b o) d")).then_inc(xs_in, 16)

            def means(n):
                for t in range(NT):
                    pool.wait_ge(mean_done, NT * n + t + 1)
                    pool.tensor_tensor(rstd[:, t % 2:t % 2 + 1], rin[:, t % 2:t % 2 + 1], c.minus_half[:, 0:1], ALU.pow
                                       ).then_inc(rs_done, 1)

            with pool.Fori(0, NB - 1) as n:
                means(n)
            pool.wait_ge(step, MEAN_AT)
            pool.tensor_tensor(rstd[0:8, 0:1], rin[0:8, 0:1], c.minus_half[0:8, 0:1], ALU.pow).then_inc(spool, 1)
            means(NB - 1)

        @block.vector
        def _(dve):
            n_ = [0]

            def done(ins):
                n_[0] += 1
                ins.then_inc(step, 1)
                dve.wait_ge(step, n_[0])

            dve.sem_inc(lo_done, KD)
            dve.sem_inc(xo_done, NT)
            for k in range(KD):
                dve.wait_ge(w_in[k % 2], 16 * (k // 2 + 1))
                dve.tensor_copy(whi[:, k, :], wraw[:, k % 2]).then_inc(w_hi, 1)
                dve.wait_ge(w_hi, k + 1)
                dve.tensor_tensor(wlo[:, k, :], wraw[:, k % 2], whi[:, k, :].bitcast(F32), S_).then_inc(w_split, 1)

            def ready(n, j):
                for k in range(NKS):
                    dve.wait_ge(sig_done, NKS * n + k + 1)
                    dve.tensor_tensor(sig[:, k], sig[:, k], st[:, k], M).then_inc(s_done, 1)
                    dve.wait_ge(s_done, 2 * NKS * n + 2 * k + 1)
                    dve.tensor_tensor(sig[:, k], sig[:, k], gate[:, k], M).then_inc(s_done, 1)
                for m in range(KD):
                    src = am[:, m] if m < 3 else (sig[:, m - 3] if m < 6 else am[:, m - 3])
                    dve.wait_ge(hi_done, at(KD, n, m + 1))
                    dve.tensor_tensor(mlo[:, j, m], src, mhi[:, j, m].bitcast(F32), S_).then_inc(lo_done, 1)

            def project(n, j):
                def finish(t):
                    q = t % 2
                    dve.wait_ge(sq_done, at(NT, n, t + 1))
                    dve.tensor_scalar(rin[:, q:q + 1], ss[:, q:q + 1], 1.0 / D, EPS, M, A_).then_inc(mean_done, 1)
                    dve.wait_ge(rs_done, NT * n + t + 1)
                    dve.scalar_tensor_tensor(xo[:, q], xo[:, q], rstd[:, q:q + 1], gf[:], M, M).then_inc(y_done, 1)

                for t in range(NT):
                    q = t % 2
                    dve.wait_ge(x_in[q], 16 * (NT // 2) * n + 16 * (t // 2 + 1))
                    dve.wait_ge(y_st[q], at(16 * NT // 2, n, 16 * (t // 2)))
                    for h in range(2):
                        dve.wait_ge(op_done, 2 * NT * n + 2 * t + h + 1)
                        ins = dve.tensor_tensor(xo[:, q, 512 * h:512 * (h + 1)], xr[:, q, 512 * h:512 * (h + 1)],
                                                c.bank[4 + 2 * q + h][:], A_)
                    ins.then_inc(xo_done, 1)
                    if t:
                        finish(t - 1)
                finish(NT - 1)

            def gate_samples():
                dve.wait_ge(p_in, 64)
                dve.wait_ge(sact, NKS)
                for k in range(NKS):
                    done(dve.tensor_tensor(sgs[:, k], sgs[:, k], yss[:, k], M))
                    done(dve.tensor_tensor(c.mix_s[:, 3 + k], c.mix_s[:, 3 + k], sgs[:, k], M))
                assert n_[0] == GATED_AT
                done(dve.tensor_copy(shi[:], c.mix_s[:]))
                done(dve.tensor_tensor(slo[:], c.mix_s[:], shi[:].bitcast(F32), S_))
                assert n_[0] == SPLIT_AT

            def project_samples():
                dve.wait_ge(xs_in, 16)
                for h in range(2):
                    dve.wait_ge(spe, NKS + 1 + h)
                    done(dve.tensor_tensor(xs[:, 512 * h:512 * (h + 1)], xs[:, 512 * h:512 * (h + 1)], c.bank[4 + h][0:8, :], A_))
                assert n_[0] == ADDED_AT
                done(dve.tensor_tensor_reduce(junk[0:8], xs, xs, 1.0, 0.0, M, A_, ss[0:8, 0:1]))
                done(dve.tensor_scalar(rin[0:8, 0:1], ss[0:8, 0:1], 1.0 / D, EPS, M, A_))
                assert n_[0] == MEAN_AT
                dve.wait_ge(spool, 1)
                done(dve.scalar_tensor_tensor(xs, xs, rstd[0:8, 0:1], gf[0:8, :], M, M))
                assert n_[0] == LAST_AT

            schedule(dve, ready, project, gate_samples, project_samples)

        @block.scalar
        def _(act):
            for j in range(2):
                act.sem_inc(y_st[j], 16 * NT // 2)
            act.sem_inc(hi_done, KD)
            act.sem_inc(sq_done, NT)
            act.wait_ge(p_in, 64)

            def ready(n, j):
                act.wait_ge(in_, 64 * n + 64)
                for k in range(NKS):
                    act.wait_ge(tr_done, NKS * n + k + 1)
                    act.activation(st[:, k].rearrange("p (c t) -> p t c", t=STEP), c.bank[k % 2][:].rearrange("p (t c) -> p t c", t=STEP),
                                   ACT.Copy).then_inc(st_done, 1)
                for k in range(NKS):
                    act.wait_ge(glu_done, NKS * n + k + 1)
                    act.activation(sig[:, k], c.bank[2 + k % 2][:], ACT.Sigmoid, bias=bg[:, k:k + 1]).then_inc(sig_done, 1)
                for m in range(KD):
                    src = am[:, m] if m < 3 else (sig[:, m - 3] if m < 6 else am[:, m - 3])
                    if 3 <= m < 6:
                        act.wait_ge(s_done, 2 * NKS * n + 2 * (m - 3) + 2)
                    act.activation(mhi[:, j, m], src, ACT.Copy).then_inc(hi_done, 1)

            def project(n, j):
                def store(t):
                    act.wait_ge(y_done, NT * n + t + 1)
                    act.dma_start(o_v[n, t], xo[:, t % 2]).then_inc(y_st[t % 2], 16)

                for t in range(NT):
                    q = t % 2
                    act.wait_ge(xo_done, at(NT, n, t + 1))
                    act.wait_ge(sq_done, at(NT, n, t))
                    act.activation(junk[:], xo[:, q], ACT.Square, accum_out=ss[:, q:q + 1]).then_inc(sq_done, 1)
                    if t:
                        store(t - 1)
                store(NT - 1)

            def gate_samples():
                for e in range(NKS):
                    act.wait_ge(spe, e + 1)
                    act.activation(sgs[:, e], c.bank[e][:, 0:8], ACT.Sigmoid, bias=bg[:, e:e + 1]).then_inc(sact, 1)

            def project_samples():
                act.wait_ge(step, LAST_AT)
                act.dma_start(y_sample.rearrange("b o d -> (b o) d"), xs).then_inc(sact, 16)

            schedule(act, ready, project, gate_samples, project_samples)
            for j in range(2):
                act.wait_ge(y_st[j], at(16 * NT // 2, NB, 0))
            act.wait_ge(sact, NKS + 16)

        @block.tensor
        def _(pe):
            pe.wait_ge(p_in, 64)

            def ready(n, j):
                pe.wait_ge(in_, 64 * n + 64)
                for k in range(NKS):
                    if k == 0:
                        pe.wait_ge(lo_done, at(KD, n, 0))
                    elif k == 2:
                        pe.wait_ge(st_done, NKS * n + 1)
                    for t in range(STEP):
                        tr = pe.matmul(c.bank[k % 2][:, t * HD:(t + 1) * HD], yc[:, t, k * P:(k + 1) * P], c.ident[0:HD, 0:HD],
                                       start=True, stop=True)
                    tr.then_inc(tr_done, 1)
                pe.wait_ge(st_done, NKS * n + NKS)
                for e in range(NKS):
                    if e == 2:
                        pe.wait_ge(sig_done, NKS * n + 1)
                    for k in range(NKS):
                        mm = pe.matmul(c.bank[2 + e % 2][:], wg[:, k, e * P:(e + 1) * P], st[:, k], start=(k == 0), stop=(k == NKS - 1))
                    mm.then_inc(glu_done, 1)

            def project(n, j):
                pe.wait_ge(w_split, KD)
                pe.wait_ge(lo_done, at(KD, n, KD))
                for t in range(NT):
                    pe.wait_ge(xo_done, at(NT, n, t - 1))
                    for h in range(2):
                        for k in range(KD):
                            for ms_, ws_ in ((mhi, whi), (mlo, whi), (mhi, wlo)):
                                mm = pe.matmul(c.bank[4 + 2 * (t % 2) + h][:], ms_[:, j, k, t * P:(t + 1) * P],
                                               ws_[:, k, 512 * h:512 * (h + 1)], start=(k == 0 and ws_ is whi and ms_ is mhi),
                                               stop=(k == KD - 1 and ws_ is wlo))
                        mm.then_inc(op_done, 1)

            def gate_samples():
                pe.wait_ge(sig_done, NKS * NB)
                for e in range(NKS):
                    for k in range(NKS):
                        mm = pe.matmul(c.bank[e][:, 0:8], wg[:, k, e * P:(e + 1) * P], yss[:, k, :], start=(k == 0), stop=(k == NKS - 1))
                    mm.then_inc(spe, 1)

            def project_samples():
                pe.wait_ge(xo_done, at(NT, NB - 1, 0))
                pe.wait_ge(step, SPLIT_AT)
                for h in range(2):
                    for k in range(KD):
                        for ms_, ws_ in ((shi, whi), (slo, whi), (shi, wlo)):
                            mm = pe.matmul(c.bank[4 + h][0:8, :], ms_[:, k, :], ws_[:, k, 512 * h:512 * (h + 1)],
                                           start=(k == 0 and ws_ is whi and ms_ is shi), stop=(k == KD - 1 and ws_ is wlo))
                    mm.then_inc(spe, 1)
                pe.wait_ge(step, ADDED_AT)

            schedule(pe, ready, project, gate_samples, project_samples)


def build(nc, a, o):
    c = Core()

    def scratch(name, shape):
        return nc.dram_tensor(name, shape, F32).ap()

    c.q_t = scratch("q_t", (WF, T))
    c.qm_t = scratch("qm_t", (WM, T))
    c.gate_t = scratch("gate_t", (D, T))
    c.mix_t = scratch("mix_t", (D, T))
    c.u_chunks = scratch("u_chunks", (4, P, G * 8 * GC))
    c.y_chunks = scratch("y_chunks", (4, P, 8, WS))
    c.negc_rows = scratch("negc_rows", (NF, T))
    c.ssm_gp = scratch("ssm_consts", (G, P, GPW))
    c.zs = scratch("z_sample", (8, DIN))
    c.ys_t = scratch("ys_t", (WS, 8))
    with ExitStack() as s:
        def sb(name, shape, dt=F32):
            return s.enter_context(nc.sbuf_tensor(name, shape, dt))

        c.ident, c.identb = sb("ident", [P, P]), sb("identb", [P, P], BF16)
        c.upper, c.lower_strict = sb("upper", [P, P]), sb("lower_strict", [P, P])
        c.mask_kq, c.mask_qk = sb("mask_kq", [P, P], BF16), sb("mask_qk", [P, P], BF16)
        c.ones = sb("ones", [P, P])
        c.minus_half = sb("minus_half", [P, 8])
        c.flogit = sb("flogit", [P, T // P, NF])
        c.negc = sb("negc", [P, NF, T // P])
        c.lfs = sb("lf_sample", [8, NF])
        c.mix_s = sb("mix_s", [P, KD, 8])
        c.bank = [s.enter_context(nc.psum_tensor(f"bank{i}", [P, 512], F32)) for i in range(8)]
        setup_constants(nc, c)
        with nc.cleanup_on_exit(), ExitStack() as s2:
            ssm_c = SsmConstants(nc, s2)
            project_prompt(nc, c, a["x_prompt"], a["w_in"], a["g_norm"], o["k_prompt"], o["v_prompt"], ssm_c, a)
            forget_gates(nc, c, a["b_f"], o["logf_prompt"])
            fox_prompt(nc, c, o["k_prompt"], o["v_prompt"], ssm_c, a)
        memory_prompt(nc, c, a["mem_prompt"], a["g_mem"], a["w_mem_kv"], o["memk_prompt"], o["memv_prompt"],
                      lambda block: sample_project(nc, c, a, o, block))
        with nc.cleanup_on_exit(), ExitStack() as s2:
            past = Past(nc, s2, a)
            ssm(nc, c, a, o["ssm_prompt"], o["ssm_sample"], past)
            sample_attend(nc, c, a, past)
        mix_out(nc, c, a, o["y_prompt"], o["y_sample"])


INS = ["x_prompt", "x_sample", "mem_prompt", "cache_k", "cache_v", "cache_logf", "state_ssm", "cache_mem_k",
       "cache_mem_v", "page_table", "g_norm", "w_in", "b_f", "lam_re", "lam_im", "log_dt", "b_re", "b_im",
       "c_re", "c_im", "d_skip", "w_glu", "b_glu", "g_mem", "w_mem_kv", "w_out", "g_final"]
OUTS = [("y_prompt", (1, T, D)), ("y_sample", (8, 1, D)),
        ("k_prompt", (1, 1, T, NF, HD)), ("v_prompt", (1, 1, T, NF, HD)), ("logf_prompt", (1, 1, T, NF)),
        ("ssm_prompt", (1, 1, G, NS, 2)), ("memk_prompt", (1, 1, NMEM, NM, HD)),
        ("memv_prompt", (1, 1, NMEM, NM, HD)), ("k_sample", (1, 8, 1, NF, HD)),
        ("v_sample", (1, 8, 1, NF, HD)), ("logf_sample", (1, 8, 1, NF)), ("ssm_sample", (1, 8, G, NS, 2))]


def kernel(**inputs):
    import numpy as np
    import concourse.bacc as bacc
    from concourse.bass_utils import run_bass_kernel_spmd

    nc = bacc.Bacc("TRN2", target_bir_lowering=False, num_devices=1)
    arrays, a, o = {}, {}, {}
    for name in INS:
        x = np.ascontiguousarray(inputs[name])
        arrays[f"in_{name}"] = x
        a[name] = nc.dram_tensor(f"in_{name}", x.shape, mybir.dt.from_np(x.dtype), kind="ExternalInput").ap()
    for name, shape in OUTS:
        o[name] = nc.dram_tensor(f"out_{name}", shape, F32, kind="ExternalOutput").ap()
    build(nc, a, o)
    r = run_bass_kernel_spmd(nc, [arrays], core_ids=[0])
    return tuple(r.results[0][f"out_{name}"] for name, _ in OUTS)
```
